# Optimizing a Trainium2 kernel written in Bass

```python
import math
import jax, jax.numpy as jnp
from jax import lax
import numpy as np

D_MODEL = 1024
BATCH = 1
SEQ = 1024
DEPTH = 1

MEM_LEN = 256
HEAD_DIM = 64
MIX_WIDTH = D_MODEL
DA_WIDTH = MIX_WIDTH // 2
SB_WIDTH = MIX_WIDTH - DA_WIDTH
DA_HEADS = DA_WIDTH // (2 * HEAD_DIM)
DA_V = 2 * HEAD_DIM
SB_HEADS = SB_WIDTH // HEAD_DIM
DA_Q_COLS = DA_HEADS * 2 * HEAD_DIM
DA_K_COLS = DA_HEADS * 2 * HEAD_DIM
DA_V_COLS = DA_HEADS * DA_V
SB_COLS = SB_HEADS * HEAD_DIM
IN_COLS = DA_Q_COLS + DA_K_COLS + DA_V_COLS + 3 * SB_COLS
ROT_DIM = HEAD_DIM // 4
ROPE_THETA = 500000.0
X_HEADS = 4
X_HEAD_DIM = D_MODEL // X_HEADS
D_FF = 4 * D_MODEL
Q_BLOCK = 128
EPS = 1e-6


def rms_norm(x, g):
    xf = x.astype(jnp.float32)
    y = xf * lax.rsqrt(jnp.mean(xf * xf, axis=-1, keepdims=True) + EPS)
    return (y * g.astype(jnp.float32)).astype(x.dtype)

def rope_tables(positions, dtype):
    inv_freq = ROPE_THETA ** (-jnp.arange(0, ROT_DIM, 2, dtype=jnp.float32) / ROT_DIM)
    ang = positions.astype(jnp.float32)[..., None] * inv_freq
    return jnp.cos(ang).astype(dtype), jnp.sin(ang).astype(dtype)

def apply_partial_rope(x, cos, sin):
    extra = x.ndim - 3
    c = cos.reshape(cos.shape[:2] + (1,) * extra + cos.shape[-1:])
    s = sin.reshape(sin.shape[:2] + (1,) * extra + sin.shape[-1:])
    half = ROT_DIM // 2
    x1, x2, xp = x[..., :half], x[..., half:ROT_DIM], x[..., ROT_DIM:]
    return jnp.concatenate([x1 * c - x2 * s, x2 * c + x1 * s, xp], axis=-1)

def diff_attention(q, k, v, lam, g_subln, lam_init):
    B, S, H = q.shape[0], q.shape[1], q.shape[2]
    nb = S // Q_BLOCK
    scale = 1.0 / math.sqrt(HEAD_DIM)
    kh = k.transpose(0, 2, 3, 1, 4)
    vh = v.transpose(0, 2, 1, 3).astype(jnp.float32)
    qb = q.transpose(0, 2, 3, 1, 4).reshape(B, H, 2, nb, Q_BLOCK, HEAD_DIM)
    qb = jnp.moveaxis(qb, 3, 0)
    qidx = jnp.arange(S, dtype=jnp.int32).reshape(nb, Q_BLOCK)
    kidx = jnp.arange(S, dtype=jnp.int32)

    def block(args):
        qblk, qi = args
        s = jnp.einsum('bhcqd,bhckd->bhcqk', qblk, kh).astype(jnp.float32) * scale
        mask = kidx[None, :] <= qi[:, None]
        p = jax.nn.softmax(jnp.where(mask, s, -jnp.inf), axis=-1)
        w = p[:, :, 0] - lam * p[:, :, 1]
        return jnp.einsum('bhqk,bhkv->bhqv', w, vh)

    o = lax.map(block, (qb, qidx))
    o = o.transpose(1, 0, 3, 2, 4).reshape(B, S, H, DA_V)
    o = rms_norm(o, g_subln) * (1.0 - lam_init)
    return o.reshape(B, S, H * DA_V)

def stick_breaking_attention(q, k, v):
    B, S, H = q.shape[0], q.shape[1], q.shape[2]
    nb = S // Q_BLOCK
    scale = 1.0 / math.sqrt(HEAD_DIM)
    kh = k.transpose(0, 2, 1, 3)
    vh = v.transpose(0, 2, 1, 3).astype(jnp.float32)
    qb = q.transpose(0, 2, 1, 3).reshape(B, H, nb, Q_BLOCK, HEAD_DIM)
    qb = jnp.moveaxis(qb, 2, 0)
    qidx = jnp.arange(S, dtype=jnp.int32).reshape(nb, Q_BLOCK)
    kidx = jnp.arange(S, dtype=jnp.int32)

    def block(args):
        qblk, qi = args
        z = jnp.einsum('bhqd,bhkd->bhqk', qblk, kh).astype(jnp.float32) * scale
        strict = kidx[None, :] < qi[:, None]
        log_beta = jax.nn.log_sigmoid(z)
        log_1mb = jnp.where(strict, jax.nn.log_sigmoid(-z), 0.0)
        between = lax.cumsum(log_1mb, axis=3, reverse=True) - log_1mb
        a = jnp.exp(jnp.where(strict, log_beta + between, -jnp.inf))
        return jnp.einsum('bhqk,bhkd->bhqd', a, vh)

    o = lax.map(block, (qb, qidx))
    return o.transpose(1, 0, 3, 2, 4).reshape(B, S, H * HEAD_DIM)

def cross_attention(h, memn, w_xq, w_xkv, w_xo):
    B, S, _ = h.shape
    q = (h @ w_xq).reshape(B, S, X_HEADS, X_HEAD_DIM)
    kv = memn @ w_xkv
    k = kv[..., :D_MODEL].reshape(B, MEM_LEN, X_HEADS, X_HEAD_DIM)
    v = kv[..., D_MODEL:].reshape(B, MEM_LEN, X_HEADS, X_HEAD_DIM).astype(jnp.float32)
    s = jnp.einsum('bqhd,bkhd->bhqk', q, k).astype(jnp.float32) / math.sqrt(X_HEAD_DIM)
    p = jax.nn.softmax(s, axis=-1)
    o = jnp.einsum('bhqk,bkhd->bqhd', p, v).reshape(B, S, D_MODEL).astype(h.dtype)
    return o @ w_xo

def first_inputs(seed: int = 0) -> dict:
    key = jax.random.key(seed)
    ks = jax.random.split(key, 24)
    f32 = jnp.float32

    def w(k, shape, fan_in):
        return jax.random.normal(k, shape, f32) * (fan_in ** -0.5)

    def gain(k, shape):
        return 1.0 + 0.02 * jax.random.normal(k, shape, f32)

    L = DEPTH
    return {
        "x": jax.random.normal(ks[0], (BATCH, SEQ, D_MODEL), f32),
        "mem": jax.random.normal(ks[1], (BATCH, MEM_LEN, D_MODEL), f32),
        "positions": jnp.broadcast_to(jnp.arange(SEQ, dtype=jnp.int32), (BATCH, SEQ)),
        "g_mix": gain(ks[2], (L, D_MODEL)),
        "w_in": w(ks[3], (L, D_MODEL, IN_COLS), D_MODEL),
        "lambda_q1": 0.1 * jax.random.normal(ks[4], (L, HEAD_DIM), f32),
        "lambda_k1": 0.1 * jax.random.normal(ks[5], (L, HEAD_DIM), f32),
        "lambda_q2": 0.1 * jax.random.normal(ks[6], (L, HEAD_DIM), f32),
        "lambda_k2": 0.1 * jax.random.normal(ks[7], (L, HEAD_DIM), f32),
        "g_subln": gain(ks[8], (L, DA_V)),
        "w_out": w(ks[9], (L, MIX_WIDTH, D_MODEL), MIX_WIDTH),
        "g_cross": gain(ks[10], (L, D_MODEL)),
        "g_mem": gain(ks[11], (L, D_MODEL)),
        "w_xq": w(ks[12], (L, D_MODEL, D_MODEL), D_MODEL),
        "w_xkv": w(ks[13], (L, D_MODEL, 2 * D_MODEL), D_MODEL),
        "w_xo": w(ks[14], (L, D_MODEL, D_MODEL), D_MODEL),
        "g_mlp": gain(ks[15], (L, D_MODEL)),
        "w_up": w(ks[16], (L, D_MODEL, D_FF), D_MODEL),
        "w_down": w(ks[17], (L, D_FF, D_MODEL), D_FF),
        "g_final": gain(ks[18], (D_MODEL,)),
    }

def first_block(x, mem, positions, g_mix, w_in, lambda_q1, lambda_k1, lambda_q2, lambda_k2,
              g_subln, w_out, g_cross, g_mem, w_xq, w_xkv, w_xo, g_mlp, w_up, w_down,
              g_final):
    B, S, _ = x.shape
    cos, sin = rope_tables(positions, x.dtype)
    h = x
    for l in range(DEPTH):
        lam_init = 0.8 - 0.6 * math.exp(-0.3 * l)
        u = rms_norm(h, g_mix[l]) @ w_in[l]
        o0 = 0
        qa = u[..., o0:o0 + DA_Q_COLS].reshape(B, S, DA_HEADS, 2, HEAD_DIM); o0 += DA_Q_COLS
        ka = u[..., o0:o0 + DA_K_COLS].reshape(B, S, DA_HEADS, 2, HEAD_DIM); o0 += DA_K_COLS
        va = u[..., o0:o0 + DA_V_COLS].reshape(B, S, DA_HEADS, DA_V); o0 += DA_V_COLS
        qs = u[..., o0:o0 + SB_COLS].reshape(B, S, SB_HEADS, HEAD_DIM); o0 += SB_COLS
        ksb = u[..., o0:o0 + SB_COLS].reshape(B, S, SB_HEADS, HEAD_DIM); o0 += SB_COLS
        vs = u[..., o0:o0 + SB_COLS].reshape(B, S, SB_HEADS, HEAD_DIM)
        qa = apply_partial_rope(qa, cos, sin)
        ka = apply_partial_rope(ka, cos, sin)
        lam = (jnp.exp(jnp.sum(lambda_q1[l].astype(jnp.float32) * lambda_k1[l].astype(jnp.float32)))
               - jnp.exp(jnp.sum(lambda_q2[l].astype(jnp.float32) * lambda_k2[l].astype(jnp.float32)))
               + lam_init)
        ya = diff_attention(qa, ka, va, lam, g_subln[l], lam_init)
        yb = stick_breaking_attention(qs, ksb, vs)
        y = jnp.concatenate([ya.astype(h.dtype), yb.astype(h.dtype)], axis=-1)
        h = h + y @ w_out[l]
        h = h + cross_attention(rms_norm(h, g_cross[l]), rms_norm(mem, g_mem[l]),
                                w_xq[l], w_xkv[l], w_xo[l])
        a = jnp.square(jax.nn.relu(rms_norm(h, g_mlp[l]) @ w_up[l]))
        h = h + a @ w_down[l]
    return rms_norm(h, g_final)


MIX_WIDTH_2 = D_MODEL
ATTN_WIDTH = MIX_WIDTH_2 // 2
ATTN_Q_HEADS = ATTN_WIDTH // HEAD_DIM
ATTN_KV_HEADS = 2
KV_WIDTH = ATTN_KV_HEADS * HEAD_DIM
WINDOW = 128
ATTN_BLOCK = 128
RWKV_WIDTH = MIX_WIDTH_2 // 4
RWKV_HEADS = RWKV_WIDTH // HEAD_DIM
DECAY_LORA = 64
ICLR_LORA = 64
RWKV_LN_EPS = 64e-5
GLA_VAL_WIDTH = MIX_WIDTH_2 // 4
GLA_HEADS = 4
GLA_VAL_DIM = GLA_VAL_WIDTH // GLA_HEADS
GLA_KEY_WIDTH = GLA_VAL_WIDTH // 2
GLA_KEY_DIM = GLA_KEY_WIDTH // GLA_HEADS
GLA_GATE_LORA = 16
GLA_GATE_NORMALIZER = 16.0
GLA_CHUNK = 64
IN_SPLITS = (ATTN_WIDTH, KV_WIDTH, KV_WIDTH, ATTN_WIDTH,
             3 * RWKV_WIDTH, RWKV_WIDTH,
             GLA_KEY_WIDTH, GLA_KEY_WIDTH, GLA_VAL_WIDTH, GLA_VAL_WIDTH)
IN_WIDTH = 2 * ATTN_WIDTH + 2 * KV_WIDTH + 4 * RWKV_WIDTH + 2 * GLA_KEY_WIDTH + 2 * GLA_VAL_WIDTH
NORM_EPS = 1e-6


def _rmsnorm(x, g):
    xf = x.astype(jnp.float32)
    y = xf * lax.rsqrt(jnp.mean(xf * xf, axis=-1, keepdims=True) + NORM_EPS)
    return (y * g.astype(jnp.float32)).astype(x.dtype)

def _shift(z):
    return jnp.pad(z, ((0, 0), (1, 0), (0, 0)))[:, :-1]

def _sliding_window_attention(q, k, v, sinks):
    B, T, Hq, D = q.shape
    Hkv = k.shape[2]
    G = Hq // Hkv
    nb = T // ATTN_BLOCK
    qb = q.reshape(B, nb, ATTN_BLOCK, Hkv, G, D)

    def band(z):
        zb = z.reshape(B, nb, ATTN_BLOCK, Hkv, D)
        prev = jnp.concatenate([jnp.zeros_like(zb[:, :1]), zb[:, :-1]], axis=1)
        return jnp.concatenate([prev, zb], axis=2)

    kb, vb = band(k), band(v)
    s = jnp.einsum('bnqhgd,bnkhd->bnhgqk', qb, kb,
                   preferred_element_type=jnp.float32) * (D ** -0.5)
    qi = jnp.arange(ATTN_BLOCK)[:, None]
    kj = jnp.arange(2 * ATTN_BLOCK)[None, :]
    dist = qi - kj + ATTN_BLOCK
    key_pos = jnp.arange(nb)[:, None, None] * ATTN_BLOCK + kj[None] - ATTN_BLOCK
    valid = (dist >= 0) & (dist < WINDOW) & (key_pos >= 0)
    slopes = 2.0 ** (-8.0 * jnp.arange(1, Hq + 1, dtype=jnp.float32) / Hq)
    s = s - slopes.reshape(Hkv, G)[:, :, None, None] * dist.astype(jnp.float32)
    s = jnp.where(valid[None, :, None, None], s, -jnp.inf)
    sink = jnp.broadcast_to(sinks.astype(jnp.float32).reshape(Hkv, G)[:, :, None, None],
                            s.shape[:-1] + (1,))
    p = jax.nn.softmax(jnp.concatenate([s, sink], axis=-1), axis=-1)[..., :-1]
    o = jnp.einsum('bnhgqk,bnkhd->bnqhgd', p.astype(v.dtype), vb)
    return o.reshape(B, T, Hq * D)

def _rwkv7_mixer(h, r, k, v, mu_w, mu_a, w0, w1, w2, a0, a1, a2, k_k, k_a, r_k, ln_w, ln_b):
    B, T, _ = h.shape
    f32 = jnp.float32
    h_prev = _shift(h)
    xw = h + (h_prev - h) * mu_w
    xa = h + (h_prev - h) * mu_a
    w = -jax.nn.softplus(-(w0 + jnp.tanh(xw @ w1) @ w2).astype(f32)) - 0.5
    decay = jnp.exp(-jnp.exp(w))
    a = jax.nn.sigmoid((a0 + (xa @ a1) @ a2).astype(f32))
    r, k, v = r.astype(f32), k.astype(f32), v.astype(f32)
    heads = lambda z: z.reshape(B, T, RWKV_HEADS, HEAD_DIM)
    kk = heads(k * k_k.astype(f32))
    kk = kk / jnp.maximum(jnp.linalg.norm(kk, axis=-1, keepdims=True), 1e-12)
    k = k * (1.0 + (a - 1.0) * k_a.astype(f32))

    def step(S, inp):
        r_t, w_t, k_t, v_t, kk_t, a_t = inp
        sa = jnp.einsum('bhvk,bhk->bhv', S, -kk_t)
        S = (S * w_t[:, :, None, :] + sa[..., None] * (kk_t * a_t)[:, :, None, :]
             + v_t[..., None] * k_t[:, :, None, :])
        return S, jnp.einsum('bhvk,bhk->bhv', S, r_t)

    tm = lambda z: jnp.moveaxis(z, 1, 0)
    S0 = jnp.zeros((B, RWKV_HEADS, HEAD_DIM, HEAD_DIM), f32)
    _, y = lax.scan(step, S0, (tm(heads(r)), tm(heads(decay)), tm(heads(k)), tm(heads(v)),
                               tm(kk), tm(heads(a))))
    y = jnp.moveaxis(y, 0, 1)
    mean = jnp.mean(y, axis=-1, keepdims=True)
    var = jnp.mean(jnp.square(y - mean), axis=-1, keepdims=True)
    y = ((y - mean) * lax.rsqrt(var + RWKV_LN_EPS)).reshape(B, T, RWKV_WIDTH)
    y = y * ln_w.astype(f32) + ln_b.astype(f32)
    bonus = jnp.sum(heads(r) * heads(k) * r_k.astype(f32), axis=-1, keepdims=True) * heads(v)
    return (y + bonus.reshape(B, T, RWKV_WIDTH)).astype(h.dtype)

def _gla_mixer(h, q, k, v, gk1, gk2, gk_b, norm_w):
    B, T, _ = h.shape
    f32 = jnp.float32
    n = T // GLA_CHUNK
    gk = jax.nn.log_sigmoid(((h @ gk1) @ gk2 + gk_b).astype(f32)) / GLA_GATE_NORMALIZER

    def chunks(z, d):
        return z.reshape(B, n, GLA_CHUNK, GLA_HEADS, d).transpose(1, 0, 3, 2, 4).astype(f32)

    qc = chunks(q, GLA_KEY_DIM) * (GLA_KEY_DIM ** -0.5)
    kc = chunks(k, GLA_KEY_DIM)
    vc = chunks(v, GLA_VAL_DIM)
    gc = chunks(gk, GLA_KEY_DIM)
    causal = jnp.tril(jnp.ones((GLA_CHUNK, GLA_CHUNK), bool))

    def step(S, inp):
        q_c, k_c, v_c, g_c = inp
        b = jnp.cumsum(g_c, axis=2)
        diff = b[:, :, :, None, :] - b[:, :, None, :, :]
        diff = jnp.where(causal[:, :, None], diff, -jnp.inf)
        A = jnp.einsum('bhid,bhjd,bhijd->bhij', q_c, k_c, jnp.exp(diff))
        o = A @ v_c + jnp.einsum('bhid,bhdv->bhiv', q_c * jnp.exp(b), S)
        b_last = b[:, :, -1:, :]
        S = (jnp.exp(b_last[:, :, 0, :])[..., None] * S
             + jnp.einsum('bhjd,bhjv->bhdv', k_c * jnp.exp(b_last - b), v_c))
        return S, o

    S0 = jnp.zeros((B, GLA_HEADS, GLA_KEY_DIM, GLA_VAL_DIM), f32)
    _, o = lax.scan(step, S0, (qc, kc, vc, gc))
    o = o.transpose(1, 0, 3, 2, 4).reshape(B, T, GLA_HEADS, GLA_VAL_DIM)
    o = o * lax.rsqrt(jnp.mean(o * o, axis=-1, keepdims=True) + 1e-5) * norm_w.astype(f32)
    return o.reshape(B, T, GLA_VAL_WIDTH).astype(h.dtype)

def _hybrid_layer(x, c_act, ada_w, ada_b, g_pre, g_post, w_in, w_out, sinks,
                  mu_rkv, mu_w, mu_a, w0, w1, w2, a0, a1, a2, k_k, k_a, r_k, ln_w, ln_b,
                  gk1, gk2, gk_b, gla_norm_w):
    B, T, _ = x.shape
    shift, scale, gate = jnp.split(c_act @ ada_w + ada_b, 3, axis=-1)
    h = _rmsnorm(x, g_pre) * (1.0 + scale[:, None]) + shift[:, None]
    proj = h @ w_in
    aq, ak, av, ag, rkv, rg, gq, gkk, gv, gg = jnp.split(proj, list(np.cumsum(IN_SPLITS)[:-1]), axis=-1)
    attn = _sliding_window_attention(aq.reshape(B, T, ATTN_Q_HEADS, HEAD_DIM),
                                     ak.reshape(B, T, ATTN_KV_HEADS, HEAD_DIM),
                                     av.reshape(B, T, ATTN_KV_HEADS, HEAD_DIM), sinks)
    attn = attn * jax.nn.silu(ag)
    rkv = rkv + (_shift(rkv) - rkv) * mu_rkv
    rr, rk, rv = jnp.split(rkv, 3, axis=-1)
    rwkv = _rwkv7_mixer(h, rr, rk, rv, mu_w, mu_a, w0, w1, w2, a0, a1, a2, k_k, k_a, r_k, ln_w, ln_b)
    rwkv = rwkv * jax.nn.silu(rg)
    gla = _gla_mixer(h, gq, gkk, gv, gk1, gk2, gk_b, gla_norm_w) * jax.nn.silu(gg)
    y = jnp.concatenate([attn, rwkv, gla], axis=-1) @ w_out
    return x + gate[:, None] * _rmsnorm(y, g_post)

def second_inputs(seed: int = 0) -> dict:
    key = jax.random.key(seed)
    ks = jax.random.split(key, 32)
    nrm = lambda k, shape, s: s * jax.random.normal(k, shape, jnp.float32)
    uni = lambda k, shape, lo, hi: jax.random.uniform(k, shape, jnp.float32, lo, hi)
    D, L = D_MODEL, DEPTH
    return {
        "x": nrm(ks[0], (BATCH, SEQ, D), 1.0),
        "c": nrm(ks[1], (BATCH, D), 1.0),
        "ada_w": nrm(ks[2], (L, D, 3 * D), 0.5 * D ** -0.5),
        "ada_b": nrm(ks[3], (L, 3 * D), 0.02),
        "norm_pre": 1.0 + nrm(ks[4], (L, D), 0.05),
        "norm_post": 1.0 + nrm(ks[5], (L, D), 0.05),
        "w_in": nrm(ks[6], (L, D, IN_WIDTH), D ** -0.5),
        "w_out": nrm(ks[7], (L, MIX_WIDTH_2, D), MIX_WIDTH_2 ** -0.5),
        "attn_sinks": nrm(ks[8], (L, ATTN_Q_HEADS), 0.5),
        "rwkv_mu_rkv": uni(ks[9], (L, 3 * RWKV_WIDTH), 0.0, 1.0),
        "rwkv_mu_w": uni(ks[10], (L, D), 0.0, 1.0),
        "rwkv_mu_a": uni(ks[11], (L, D), 0.0, 1.0),
        "rwkv_w0": uni(ks[12], (L, RWKV_WIDTH), -4.0, 1.0),
        "rwkv_w1": nrm(ks[13], (L, D, DECAY_LORA), D ** -0.5),
        "rwkv_w2": nrm(ks[14], (L, DECAY_LORA, RWKV_WIDTH), 0.5 * DECAY_LORA ** -0.5),
        "rwkv_a0": nrm(ks[15], (L, RWKV_WIDTH), 0.1),
        "rwkv_a1": nrm(ks[16], (L, D, ICLR_LORA), D ** -0.5),
        "rwkv_a2": nrm(ks[17], (L, ICLR_LORA, RWKV_WIDTH), 0.5 * ICLR_LORA ** -0.5),
        "rwkv_k_k": 0.85 + nrm(ks[18], (L, RWKV_WIDTH), 0.05),
        "rwkv_k_a": 1.0 + nrm(ks[19], (L, RWKV_WIDTH), 0.05),
        "rwkv_r_k": nrm(ks[20], (L, RWKV_HEADS, HEAD_DIM), 0.1),
        "rwkv_ln_w": 1.0 + nrm(ks[21], (L, RWKV_WIDTH), 0.05),
        "rwkv_ln_b": nrm(ks[22], (L, RWKV_WIDTH), 0.02),
        "gla_gk1": nrm(ks[23], (L, D, GLA_GATE_LORA), D ** -0.5),
        "gla_gk2": nrm(ks[24], (L, GLA_GATE_LORA, GLA_KEY_WIDTH), GLA_GATE_LORA ** -0.5),
        "gla_gk_b": nrm(ks[25], (L, GLA_KEY_WIDTH), 0.1),
        "gla_norm_w": 1.0 + nrm(ks[26], (L, GLA_VAL_DIM), 0.05),
    }

def second_block(x, c, ada_w, ada_b, norm_pre, norm_post, w_in, w_out, attn_sinks,
              rwkv_mu_rkv, rwkv_mu_w, rwkv_mu_a, rwkv_w0, rwkv_w1, rwkv_w2,
              rwkv_a0, rwkv_a1, rwkv_a2, rwkv_k_k, rwkv_k_a, rwkv_r_k, rwkv_ln_w, rwkv_ln_b,
              gla_gk1, gla_gk2, gla_gk_b, gla_norm_w):
    c_act = jax.nn.silu(c)
    for l in range(DEPTH):
        x = _hybrid_layer(x, c_act, ada_w[l], ada_b[l], norm_pre[l], norm_post[l], w_in[l], w_out[l],
                          attn_sinks[l], rwkv_mu_rkv[l], rwkv_mu_w[l], rwkv_mu_a[l],
                          rwkv_w0[l], rwkv_w1[l], rwkv_w2[l], rwkv_a0[l], rwkv_a1[l], rwkv_a2[l],
                          rwkv_k_k[l], rwkv_k_a[l], rwkv_r_k[l], rwkv_ln_w[l], rwkv_ln_b[l],
                          gla_gk1[l], gla_gk2[l], gla_gk_b[l], gla_norm_w[l])
    return x


def setup_inputs(seed=0):
    out = dict(first_inputs(seed))
    for name, value in second_inputs(seed + 1).items():
        if name != "x":
            out[name + "_2"] = value
    return out


def reference(
    x, mem, positions, g_mix, w_in, lambda_q1, lambda_k1, lambda_q2, lambda_k2, g_subln, w_out,
    g_cross, g_mem, w_xq, w_xkv, w_xo, g_mlp, w_up, w_down, g_final, c_2, ada_w_2, ada_b_2,
    norm_pre_2, norm_post_2, w_in_2, w_out_2, attn_sinks_2, rwkv_mu_rkv_2, rwkv_mu_w_2,
    rwkv_mu_a_2, rwkv_w0_2, rwkv_w1_2, rwkv_w2_2, rwkv_a0_2, rwkv_a1_2, rwkv_a2_2, rwkv_k_k_2,
    rwkv_k_a_2, rwkv_r_k_2, rwkv_ln_w_2, rwkv_ln_b_2, gla_gk1_2, gla_gk2_2, gla_gk_b_2,
    gla_norm_w_2,
):
    x = first_block(
        x, mem, positions, g_mix, w_in, lambda_q1, lambda_k1, lambda_q2, lambda_k2, g_subln,
        w_out, g_cross, g_mem, w_xq, w_xkv, w_xo, g_mlp, w_up, w_down, g_final,
    )
    return second_block(
        x, c_2, ada_w_2, ada_b_2, norm_pre_2, norm_post_2, w_in_2, w_out_2, attn_sinks_2,
        rwkv_mu_rkv_2, rwkv_mu_w_2, rwkv_mu_a_2, rwkv_w0_2, rwkv_w1_2, rwkv_w2_2, rwkv_a0_2,
        rwkv_a1_2, rwkv_a2_2, rwkv_k_k_2, rwkv_k_a_2, rwkv_r_k_2, rwkv_ln_w_2, rwkv_ln_b_2,
        gla_gk1_2, gla_gk2_2, gla_gk_b_2, gla_norm_w_2,
    )


_drawn_inputs = setup_inputs


def setup_inputs(seed=0):
    import zlib

    import numpy as np

    out = dict(_drawn_inputs(seed))
    spreads = {}
    factors = {'lambda_k1': 3.172,
     'lambda_q2': 3.367,
     'g_subln': 4.938,
     'g_cross': 8.0,
     'g_mem': 8.0,
     'g_mlp': 3.213,
     'norm_post_2': 4.094,
     'attn_sinks_2': 8.0,
     'rwkv_mu_w_2': 8.0,
     'rwkv_mu_a_2': 3.406,
     'rwkv_w2_2': 2.9,
     'rwkv_a0_2': 7.812,
     'rwkv_k_k_2': 11.116,
     'rwkv_k_a_2': 4.223,
     'rwkv_ln_w_2': 5.723,
     'rwkv_ln_b_2': 36.663,
     'gla_gk_b_2': 4.56,
     'gla_norm_w_2': 7.051}
    for name, (base, spread) in spreads.items():
        noise = np.random.default_rng([zlib.crc32(name.encode()), seed]).standard_normal(out[name].shape)
        drawn = base * np.exp(spread * noise) if base else spread * noise
        out[name] = __import__('jax').numpy.asarray(drawn.astype(out[name].dtype))
    for name, factor in factors.items():
        out[name] = (out[name] * factor).astype(out[name].dtype)
    return out
```

```python
import concourse.bass as bass
from concourse import mybir
from concourse.alu_op_type import AluOpType as ALU
from contextlib import ExitStack
import numpy as np

P = 128
D = 1024
T = 1024
KC = D // P
NT = T // P
HALF = 512
MEM = 256
EPS = 1e-6
NEG = -1e30
LAM_INIT = 0.2
UNITS = 8
CREDIT = 4
PAD = 8

VEC = {}
for _name, _n in [("g_mix", 8), ("g_cross", 8), ("g_mem", 8), ("g_mlp", 8), ("g_final", 8),
                  ("norm_pre", 8), ("norm_post", 8), ("g_subln", 1), ("c", 8), ("ada_b", 24),
                  ("mu_w", 8), ("mu_a", 8), ("mu_rkv", 6), ("w0", 2), ("a0", 2), ("k_k", 2), ("k_a", 2),
                  ("r_k", 2), ("ln_w", 2), ("ln_b", 2), ("gk_b", 1), ("gla_norm", 1),
                  ("lam", 4), ("sinks", 8)]:
    VEC[_name] = (sum(n for _, n in VEC.values()), _n)
NVEC = sum(n for _, n in VEC.values())

CONST = {}
for _name, _n in [("ident", 128), ("ones", 128), ("blk64", 128), ("neg_tri", 128), ("neg_ones", 128),
                  ("rot", 128), ("da_mask", 128), ("sb_mask", 128), ("sb_strict", 128),
                  ("level", 7 * 128), ("strict64", 128), ("incl64", 128), ("first_low", 128), ("gla_state", 256), ("ident64", 64),
                  ("inv_freq", 1), ("eps", 1), ("half_pi", 1), ("zero", 1), ("eps5", 1), ("eps_ln", 1)]:
    CONST[_name] = (sum(n for _, n in CONST.values()), _n)
NCONST = sum(n for _, n in CONST.values())


def constants():
    i = np.arange(P)
    c = np.zeros((P, NCONST), np.float32)

    def put(name, a):
        o, n = CONST[name]
        c[:, o:o + n] = a

    put("ident", np.eye(P))
    put("ones", 1.0)
    put("blk64", (i[:, None] // 64) == (i[None, :] // 64))
    put("neg_tri", -1.0 * (i[:, None] >= i[None, :]))
    put("neg_ones", -1.0)
    rot = np.zeros((P, P))
    for b in (0, 64):
        for m in range(8):
            rot[b + m + 8, b + m] = -1.0
            rot[b + m, b + m + 8] = 1.0
    put("rot", rot)
    put("da_mask", NEG * (i[None, :] > i[:, None]))
    put("sb_mask", NEG * (i[:, None] >= i[None, :]))
    put("sb_strict", i[:, None] < i[None, :])
    f = np.zeros(P, np.float32)
    for b in (0, 64):
        for m in range(16):
            f[b + m] = np.float32(500000.0) ** np.float32(-(2.0 * (m % 8)) / 16.0)
    j, t = i[:, None], i[None, :]
    put("level", np.concatenate([(j >> (l + 1) == t >> (l + 1)) & (j >> l & 1 == 0) & (t >> l & 1 == 1)
                                 for l in range(7)], axis=1))
    put("strict64", (j // 64 == t // 64) & (j < t))
    put("incl64", (j // 64 == t // 64) & (j <= t))
    put("first_low", (j >> 1 == t >> 1) & (j & 1 == 1) & (t & 1 == 0))
    put("ident64", i[:, None] % 64 == np.arange(64)[None, :])
    put("gla_state", (i[:, None] // 32) == (np.arange(256)[None, :] // 64))
    put("inv_freq", f[:, None])
    put("eps", EPS)
    put("half_pi", np.pi / 2)
    put("eps5", 1e-5)
    put("eps_ln", 64e-5)
    return c


def window_bias():
    q, k = np.arange(P)[:, None], np.arange(2 * P)[None, :]
    dist = q - k + P
    b = np.zeros((P, 8, 2 * P), np.float32)
    for g in range(2):
        for par in range(2):
            for c in range(2):
                head = 4 * g + 2 * c + par
                slope = np.float32(2.0) ** np.float32(-8.0 * (head + 1) / 8)
                b[:, 4 * g + 2 * par + c] = np.where((dist >= 0) & (dist < P), -slope * dist.astype(np.float32), NEG)
    return b.reshape(P, 8 * 2 * P)


def program(nc, xT_d, memT_d, pos_d, vec_d, const_d, bias_d, lora_d, w_d, out_d):
    F = mybir.dt.float32
    I32 = mybir.dt.int32
    ACT = mybir.ActivationFunctionType
    AX = mybir.AxisListType.X
    ctx = ExitStack()
    with ctx:
        def sb(name, shape, dt=F):
            return ctx.enter_context(nc.sbuf_tensor(name, shape, dt))

        sems = {}

        def S(name):
            if name not in sems:
                sems[name] = ctx.enter_context(nc.semaphore(name))
            return sems[name]

        PS = ctx.enter_context(nc.psum_tensor("PS", [P, 8 * HALF], F))

        def bank(b, n=1):
            return PS[:, b * HALF:(b + n) * HALF]

        const = sb("const", [P, NCONST])
        vec = sb("vec", [P, NVEC])

        def cst(name):
            o, n = CONST[name]
            return const[:, o:o + n]

        def vcol(name, j=0):
            return vec[:, VEC[name][0] + j:VEC[name][0] + j + 1]

        hT = sb("hT", [P, KC, T])
        uT = sb("uT", [P, KC, PAD + T])
        yT = sb("yT", [P, KC, T])
        NS = 4
        wring = sb("wring", [P, NS, D])
        small = sb("small", [P, 64])
        ada = sb("ada", [P, 24])
        arena = sb("arena", [P, 18432])

        def U(k, lo=0, hi=T):
            return uT[:, k, PAD + lo:PAD + hi]

        class Arena:

            def __init__(self):
                self.at = 0

            def take(self, n):
                self.at += n
                assert self.at <= 18432, self.at
                return arena[:, self.at - n:self.at]

        def slot(s, k, lo=0, hi=P):
            return wring[:, s, k * P + lo:k * P + hi]


        UNIT_PANELS = 6 * UNITS
        w_in = [S(f"weight_in_slot{s}") for s in range(NS)]

        def w_ready(s, nth):
            return 16 * (nth + 1) + (16 * 2 * UNITS if s < 3 else 0)

        def loop(e, n):
            return e.Fori(0, n)

        NB = 6 * HALF
        NORMS = {n: m for m, n in enumerate(["mix", "mem", "x", "mlp", "fin", "pre", "post"])}

        def norm_out(n, k):
            return S("norm_out"), KC * NORMS[n] + k

        def norm_act(act, n, src, width, sq, rs, ready):
            m = NORMS[n]
            for k in range(KC):
                for name, v in ready(k):
                    act.wait_ge(S(name), v)
                if k >= sq.shape[1]:
                    act.wait_ge(S("norm_sq_summed"), KC * m + k + 1 - sq.shape[1])
                act.activation(sq[:, k % sq.shape[1], :width], src(k), ACT.Square).then_inc(S("norm_sq_ready"), 1)
            act.wait_ge(S("norm_sq_summed"), KC * m + KC)
            act.activation(rs[:, :width], PS[:, NB:NB + width], ACT.Sqrt, bias=cst("eps"),
                           scale=1.0 / D).then_inc(S("norm_root"), 1)

        def norm_pe(pe, n, width, sq):
            m = NORMS[n]
            for k in range(KC):
                pe.wait_ge(S("norm_sq_ready"), KC * m + k + 1)
                for h in range(0, width, HALF):
                    w = min(HALF, width)
                    mm = pe.matmul(PS[:, NB + h:NB + h + w], cst("ones"), sq[:, k % sq.shape[1], h:h + w],
                                  start=(k == 0), stop=(k == KC - 1))
                mm.then_inc(S("norm_sq_summed"), 1)

        def norm_dve(dve, n, src, dst, gain, width, rs):
            m = NORMS[n]
            dve.wait_ge(S("norm_root"), m + 1)
            dve.reciprocal(rs[:, :width], rs[:, :width]).then_inc(S("norm_rstd"), 1)
            dve.wait_ge(S("norm_rstd"), m + 1)
            for k in range(KC):
                dve.scalar_tensor_tensor(dst(k), src(k), gain(k), rs[:, :width], ALU.mult, ALU.mult)\
                   .then_inc(S("norm_out"), 1)

        def panel_product(pe, n, s, banks, evac_from, rhs, token_major, width):
            for h in range(max(1, width // HALF)):
                w = min(width, HALF)
                pe.wait_ge(S(n + "_evac"), evac_from + h)
                if token_major:
                    for t in range(w // P):
                        lo = h * HALF + t * P
                        for k in range(KC):
                            m = pe.matmul(banks[h][:, t * P:(t + 1) * P], rhs(k, lo, lo + P), slot(s, k),
                                          start=(k == 0), stop=(k == KC - 1))
                            if h == 0 and t == 0 and k == 0:
                                m.then_inc(S("weight_free"), 1)
                else:
                    for k in range(KC):
                        m = pe.matmul(banks[h][:, :w], slot(s, k), rhs(k, h * HALF, h * HALF + w),
                                      start=(k == 0), stop=(k == KC - 1))
                        if h == 0 and k == 0:
                            m.then_inc(S("weight_free"), 1)
                m.then_inc(S(n + "_mm"), 1)

        def gemm_banks(j, halves):
            return [bank((halves * j + h) % 4) for h in range(halves)]

        def gemm_pe(pe, n, g0, count, rhs, token_major=False, width=T, peeled=False, done=0):
            halves = max(1, width // HALF)

            def body(i):
                for j in range(NS):
                    pe.wait_ge(w_in[j], 16 * i + w_ready(j, (g0 - UNIT_PANELS) // NS))
                    panel_product(pe, n, j, gemm_banks(j, halves), halves * (NS * i + j + done) + 1,
                                  rhs, token_major, width)

            if peeled:
                body(0)
            else:
                with loop(pe, count // NS) as i:
                    body(i)

        def gemm_evac(e, n, count, width, one, done=0):
            halves = max(1, width // HALF)
            with loop(e, count // NS) as i:
                for j in range(NS):
                    for h in range(halves):
                        e.wait_ge(S(n + "_mm"), halves * (NS * i + j + done) + h + 1)
                        one(i, j, h, gemm_banks(j, halves)[h][:, :min(width, HALF)])

        def add_to_h(dve, n):
            def one(i, j, h, b):
                dst = hT[:, bass.ds(NS * i + j, 1), h * HALF:(h + 1) * HALF].rearrange("p o t -> p (o t)")
                dve.tensor_tensor(dst, dst, b, ALU.add).then_inc(S(n + "_evac"), 1)
            return one

        ar = Arena()
        raw = ar.take(6 * HALF).rearrange("p (c t) -> p c t", c=6)
        qh, kh = ar.take(T), ar.take(T)
        Vh = ar.take(T).rearrange("p (t f) -> p t f", t=NT)
        cosT, sinT = ar.take(T), ar.take(T)
        at_da = ar.at
        Pr = ar.take(4 * T).rearrange("p (b c t) -> p b c t", b=2, c=2)
        wgt = ar.take(2 * T).rearrange("p (b t) -> p b t", b=2)
        wgtT = ar.take(T)
        oT, osq, tmp = ar.take(T), ar.take(T), ar.take(T)
        n_sq = arena[:, at_da:at_da + 2 * T].rearrange("p (b t) -> p b t", b=2)
        n_rs = arena[:, at_da + 2 * T:at_da + 3 * T]
        ang, turns, posf = (arena[:, at_da + (3 + m) * T:at_da + (4 + m) * T] for m in range(3))
        pos_i = sb("pos_i", [P, T], I32)
        nm = sb("nm", [P, 16])
        el = sb("el", [P, 16])
        er = sb("er", [P, 16])
        lamt = sb("lamt", [P, 8])
        gsub = sb("gsub", [P, 1])
        cact = sb("cact", [P, 8])

        PROJ = 7

        def proj_pe(pe, u, c):
            if c == 0:
                pe.wait_ge(S("proj_evac"), PROJ * u + 1)
            elif c >= 2:
                pe.wait_ge(S("proj_evac"), PROJ * u + c)
            b = bank(c % 2)
            if c < 6:
                s, h = c // 2, c % 2
                if h == 0:
                    pe.wait_ge(w_in[s], 32 * u + 16)
                if s < 2:
                    for k in range(KC):
                        m = pe.matmul(b, slot(s, k), U(k, h * HALF, (h + 1) * HALF), start=(k == 0), stop=(k == KC - 1))
                        if h == 0 and k == 0:
                            m.then_inc(S("weight_free"), 1)
                else:
                    for t in range(4):
                        lo = h * HALF + t * P
                        for k in range(KC):
                            m = pe.matmul(b[:, t * P:(t + 1) * P], U(k, lo, lo + P), slot(s, k), start=(k == 0), stop=(k == KC - 1))
                            if h == 0 and t == 0 and k == 0:
                                m.then_inc(S("weight_free"), 1)
            else:
                for s in range(3):
                    pe.wait_ge(w_in[s], 32 * u + 32)
                    for k in range(KC):
                        m = pe.matmul(b[:, s:s + 1], slot(s, k), cact[:, k:k + 1], start=(k == 0), stop=(k == KC - 1))
                        if k == 0:
                            m.then_inc(S("weight_free"), 1)
            m.then_inc(S("proj_mm"), 1)

        def proj_act(act, u, c):
            act.wait_ge(S("proj_mm"), PROJ * u + c + 1)
            if c < 6:
                act.activation(raw[:, c, :], bank(c % 2), ACT.Copy, scale=0.125 if c < 2 else 1.0).then_inc(S("proj_evac"), 1)
            else:
                act.activation(ada[:, bass.ds(3 * u, 3)] if not isinstance(u, int) else ada[:, 3 * u:3 * u + 3],
                               bank(0)[:, 0:3], ACT.Copy).then_inc(S("proj_evac"), 1)

        def rounds(t):
            return t if t <= 4 else 4 + 2 * (t - 4)

        def da_pe(pe, i):
            pe.wait_ge(S("proj_evac"), PROJ * i + 5)
            for x in range(2):
                for h in range(2):
                    m = pe.matmul(bank(2 + 2 * x + h), cst("rot"), raw[:, 2 * x + h, :], start=True, stop=True)
                m.then_inc(S("rot_ready"), 1)
            pe.wait_ge(S("qk_ready"), 2 * i + 2)

            def scores(s):
                kw = (s + 1) * P
                for c in range(2):
                    if s >= 1:
                        pe.wait_ge(S("exp_done"), 16 * i + 2 * (s - 1) + c + 1)
                    r = slice(64 * c, 64 * c + 64)
                    b = bank(2 + 2 * c, 2)
                    for lo in range(0, kw, HALF):
                        hi = min(kw, lo + HALF)
                        m = pe.matmul(b[:, lo:hi], qh[r, s * P:(s + 1) * P], kh[r, lo:hi], start=True, stop=(hi < kw))
                    m = pe.matmul(b[:, kw - P:kw], cst("ident"), cst("da_mask"), start=False, stop=True)
                    m.then_inc(S("sc_ready"), 1)

            def turn(t, rd):
                if rd == 0:
                    pe.wait_ge(S("w_ready"), 8 * i + t + 1)
                if rounds(t) + rd > 0:
                    pe.wait_ge(S("tr_copied"), 12 * i + rounds(t) + rd)
                for kb in range(4 * rd, min(4 * rd + 4, t + 1)):
                    m = pe.transpose(bank(6)[:, (kb % 4) * P:(kb % 4 + 1) * P], wgt[:, t % 2, kb * P:(kb + 1) * P], cst("ident"))
                m.then_inc(S("tr_ready"), 1)

            def values(t):
                pe.wait_ge(S("tr_copied"), 12 * i + rounds(t + 1))
                if t == 0:
                    pe.wait_ge(S("v_ready"), i + 1)
                if t == 4:
                    pe.wait_ge(S("o_evac"), 2 * i + 1)
                for kb in range(t + 1):
                    m = pe.matmul(bank(7)[:, (t % 4) * P:(t % 4 + 1) * P], Vh[:, kb, :], wgtT[:, kb * P:(kb + 1) * P],
                                  start=(kb == 0), stop=(kb == t))
                m.then_inc(S("av_ready"), 1)

            for s in range(NT + 1):
                if s >= 2:
                    values(s - 2)
                if s < NT:
                    scores(s)
                if s >= 1:
                    turn(s - 1, 0)
                if s < PROJ:
                    proj_pe(pe, i + 1, s)
                if s >= 5:
                    turn(s - 1, 1)
            values(NT - 1)
            pe.wait_ge(S("osq_ready"), i + 1)
            for h in range(2):
                m = pe.matmul(bank(6 + h), cst("ones"), osq[:, h * HALF:(h + 1) * HALF], start=True, stop=True)
            m.then_inc(S("osum_ready"), 1)

        def da_act(act, i):
            act.wait_ge(S("proj_evac"), PROJ * i + 7)
            act.activation(Vh[:, :, :].rearrange("p t f -> p (t f)"), raw[:, 4:6, :].rearrange("p c t -> p (c t)"),
                           ACT.Copy).then_inc(S("v_ready"), 1)

            def exps(s):
                kw = (s + 1) * P
                for c in range(2):
                    if s >= 2:
                        act.wait_ge(S("w_ready"), 8 * i + s - 1)
                    act.wait_ge(S("nmax_ready"), 16 * i + 2 * s + c + 1)
                    act.activation(Pr[:, s % 2, c, :kw], bank(2 + 2 * c, 2)[:, :kw], ACT.Exp, bias=nm[:, 2 * s + c:2 * s + c + 1],
                                   accum_out=el[:, 2 * s + c:2 * s + c + 1]).then_inc(S("exp_done"), 1)

            def copy_turned(t, rd):
                n = min(4, t + 1 - 4 * rd) * P
                act.wait_ge(S("tr_ready"), 12 * i + rounds(t) + rd + 1)
                act.activation(wgtT[:, 4 * P * rd:4 * P * rd + n], bank(6)[:, :n], ACT.Copy).then_inc(S("tr_copied"), 1)

            def take_o(h):
                act.wait_ge(S("av_ready"), 8 * i + 4 * h + 4)
                act.activation(oT[:, h * HALF:(h + 1) * HALF], bank(7), ACT.Copy).then_inc(S("o_evac"), 1)

            for s in range(NT + 1):
                if s == 5:
                    take_o(0)
                if s < NT:
                    exps(s)
                if s >= 1:
                    copy_turned(s - 1, 0)
                if s < PROJ:
                    if s == 0:
                        act.wait_ge(S("qk_ready"), 2 * i + 2)
                    if s == 4:
                        act.wait_ge(S("v_ready"), i + 1)
                    proj_act(act, i + 1, s)
                if s >= 5:
                    copy_turned(s - 1, 1)
            take_o(1)
            act.wait_ge(S("o_evac"), 2 * i + 2)
            act.activation(osq, oT, ACT.Square).then_inc(S("osq_ready"), 1)
            act.wait_ge(S("osum_ready"), i + 1)
            act.activation(osq, bank(6, 2), ACT.Sqrt, bias=cst("eps"), scale=1.0 / P).then_inc(S("oroot_ready"), 1)

        def da_dve(dve, i):
            for x, dst in enumerate((qh, kh)):
                src = raw[:, 2 * x:2 * x + 2, :].rearrange("p c t -> p (c t)")
                dve.wait_ge(S("rot_ready"), 2 * i + x + 1)
                dve.tensor_tensor(dst, src, cosT, ALU.mult).then_inc(S("rope_part"), 1)
                dve.tensor_tensor(tmp, bank(2 + 2 * x, 2), sinT, ALU.mult).then_inc(S("rope_part"), 1)
                dve.wait_ge(S("rope_part"), 4 * i + 2 * x + 2)
                dve.tensor_tensor(dst, dst, tmp, ALU.add).then_inc(S("qk_ready"), 1)
                dve.wait_ge(S("qk_ready"), 2 * i + x + 1)

            def maxima(s):
                for c in range(2):
                    dve.wait_ge(S("sc_ready"), 16 * i + 2 * s + c + 1)
                    dve.reduce_max(nm[:, 2 * s + c:2 * s + c + 1], bank(2 + 2 * c, 2)[:, :(s + 1) * P], AX,
                                   negate=True).then_inc(S("nmax_ready"), 1)

            def weights(t):
                kw = (t + 1) * P
                dve.wait_ge(S("exp_done"), 16 * i + 2 * t + 2)
                dve.reciprocal(er[:, 2 * t:2 * t + 2], el[:, 2 * t:2 * t + 2]).then_inc(S("recip_ready"), 1)
                dve.wait_ge(S("recip_ready"), 8 * i + t + 1)
                dve.tensor_scalar(Pr[:, t % 2, 1, :kw], Pr[:, t % 2, 1, :kw], er[:, 2 * t + 1:2 * t + 2], lamt[:, 5:6],
                                  ALU.mult, ALU.mult).then_inc(S("w_part"), 1)
                dve.wait_ge(S("w_part"), 8 * i + t + 1)
                if t >= 2:
                    dve.wait_ge(S("tr_ready"), 12 * i + rounds(t - 1))
                dve.scalar_tensor_tensor(wgt[:, t % 2, :kw], Pr[:, t % 2, 0, :kw], er[:, 2 * t:2 * t + 1],
                                         Pr[:, t % 2, 1, :kw], ALU.mult, ALU.add).then_inc(S("w_ready"), 1)

            for s in range(NT + 1):
                if s < NT:
                    maxima(s)
                if s >= 1:
                    weights(s - 1)
            dve.wait_ge(S("oroot_ready"), i + 1)
            dve.reciprocal(osq, osq).then_inc(S("orstd_ready"), 1)
            dve.wait_ge(S("orstd_ready"), i + 1)
            dve.scalar_tensor_tensor(yT[:, bass.ds(i, 1), :].rearrange("p o t -> p (o t)"), oT, gsub[:, 0:1], osq,
                                     ALU.mult, ALU.mult).then_inc(S("da_y_ready"), 1)

        ar = Arena()
        ar.at = at_da - 2 * T
        Rs = ar.take(2 * T).rearrange("p (h t) -> p h t", h=2)
        ab = ar.take(2 * T).rearrange("p (b t) -> p b t", b=2)
        sp = ar.take(2 * T).rearrange("p (b t) -> p b t", b=2)
        Aw = ar.take(2 * T).rearrange("p (b t) -> p b t", b=2)

        def sb_block(n):
            kb = NT - 1 - n // 2
            return kb, n % 2, T - kb * P

        def pieces(lo, hi):
            return [(a, min(a + HALF, hi)) for a in range(lo, hi, HALF)]

        def sb_pe(pe, j, last):
            pe.wait_ge(S("sb_qkv"), 3 * j + 3)
            for s in range(18):
                if s < 16:
                    kb, hd, w = sb_block(s)
                    if s >= 2:
                        pe.wait_ge(S("sb_a"), 16 * j + s - 1)
                    r = slice(64 * hd, 64 * hd + 64)
                    for lo, hi in pieces(0, w):
                        m = pe.matmul(bank(2 + 2 * (s % 2), 2)[:, lo:hi], kh[r, kb * P:(kb + 1) * P],
                                      qh[r, kb * P + lo:kb * P + hi], start=True, stop=True)
                    m.then_inc(S("sb_z"), 1)
                if not last and s % 2 == 0 and 2 <= s <= 14:
                    proj_pe(pe, j + 5, s // 2 - 1)
                if 1 <= s <= 16:
                    n = s - 1
                    kb, hd, w = sb_block(n)
                    b = bank(2 + 2 * (n % 2), 2)
                    pe.wait_ge(S("sb_sp"), 16 * j + n + 1)
                    for lo, hi in pieces(0, w):
                        pe.matmul(b[:, lo:hi], cst("neg_tri"), sp[:, n % 2, lo:hi], start=False, stop=True,
                                  skip_group_check=True)
                    if n >= 2:
                        pe.wait_ge(S("sb_sum"), 14 * j + n - 1)
                        for lo, hi in pieces(0, w):
                            lo = max(lo, P)
                            pe.matmul(b[:, lo:hi], cst("neg_ones"), Rs[:, hd, kb * P + lo:kb * P + hi],
                                      start=False, stop=True, skip_group_check=True)
                    pe.matmul(b[:, :P], cst("ident"), cst("sb_mask"), start=False, stop=True,
                              skip_group_check=True).then_inc(S("sb_e"), 1)
                if s >= 2:
                    n = s - 2
                    kb, hd, w = sb_block(n)
                    pe.wait_ge(S("sb_a"), 16 * j + n + 1)
                    for lo, hi in ((kb * P, HALF), (max(kb * P, HALF), T)):
                        if lo < hi:
                            m = pe.matmul(PS[64 * hd:64 * hd + 64, 6 * HALF + lo:6 * HALF + hi], Vh[:, kb, 64 * hd:64 * hd + 64],
                                          Aw[:, n % 2, lo - kb * P:hi - kb * P], start=(n < 2 or (lo < HALF and kb == 3)),
                                          stop=(kb == 0), skip_group_check=True)
                    m.then_inc(S("sb_av"), 1)

        def sb_act(act, j, last):
            act.preload_act_table_set("natural_log_exp_and_others")
            act.wait_ge(S("proj_evac"), PROJ * (j + 4) + 7)
            for dst, c in ((qh, 0), (kh, 2), (Vh[:, :, :].rearrange("p t f -> p (t f)"), 4)):
                act.activation(dst, raw[:, c:c + 2, :].rearrange("p c t -> p (c t)"), ACT.Copy).then_inc(S("sb_qkv"), 1)
            for s in range(17):
                if s < 16:
                    w = sb_block(s)[2]
                    act.wait_ge(S("sb_z"), 16 * j + s + 1)
                    if s >= 2:
                        act.wait_ge(S("sb_sp_raw"), 16 * j + s - 1)
                    act.activation(ab[:, s % 2, :w], bank(2 + 2 * (s % 2), 2)[:, :w], ACT.Abs).then_inc(S("sb_abs"), 1)
                    act.wait_ge(S("sb_abs"), 16 * j + s + 1)
                    act.activation(ab[:, s % 2, :w], ab[:, s % 2, :w], ACT.Exp, scale=-1.0).then_inc(S("sb_exp"), 1)
                    act.wait_ge(S("sb_exp"), 16 * j + s + 1)
                    act.activation(ab[:, s % 2, :w], ab[:, s % 2, :w], ACT.Ln, bias=1.0).then_inc(S("sb_ln"), 1)
                if s >= 1:
                    n = s - 1
                    w = sb_block(n)[2]
                    if n >= 2:
                        act.wait_ge(S("sb_av"), 16 * j + n - 1)
                    act.wait_ge(S("sb_e"), 16 * j + n + 1)
                    act.activation(Aw[:, n % 2, :w], bank(2 + 2 * (n % 2), 2)[:, :w], ACT.Exp).then_inc(S("sb_a"), 1)
                if not last and s % 2 == 0 and 2 <= s <= 14:
                    if s == 2:
                        act.wait_ge(S("sb_qkv"), 3 * j + 3)
                    proj_act(act, j + 5, s // 2 - 1)
            act.wait_ge(S("sb_av"), 16 * j + 16)
            act.activation(yT[:, bass.ds(j + 4, 1), :].rearrange("p o t -> p (o t)") if not isinstance(j, int) else yT[:, j + 4, :],
                           bank(6, 2), ACT.Copy).then_inc(S("sb_y_ready"), 1)

        def sb_dve(dve, j):
            for s in range(16):
                w = sb_block(s)[2]
                dve.wait_ge(S("sb_ln"), 16 * j + s + 1)
                if s >= 2:
                    dve.wait_ge(S("sb_sum"), 14 * j + s - 1)
                dve.scalar_tensor_tensor(sp[:, s % 2, :w], bank(2 + 2 * (s % 2), 2)[:, :w], 0.0, ab[:, s % 2, :w],
                                         ALU.max, ALU.add).then_inc(S("sb_sp_raw"), 1)
                dve.wait_ge(S("sb_sp_raw"), 16 * j + s + 1)
                dve.tensor_tensor(sp[:, s % 2, :P], sp[:, s % 2, :P], cst("sb_strict"), ALU.mult).then_inc(S("sb_sp"), 1)

        def sb_pool(pool, j):
            pool.wait_ge(S("sb_qkv"), 3 * j + 1)
            pool.sem_inc(S("sb_zeroing"), 1)
            pool.memset(Rs[:, :, :], 0.0).then_inc(S("sb_zero"), 1)
            pool.wait_ge(S("sb_zero"), j + 1)
            for n in range(14):
                kb, hd, w = sb_block(n)
                pool.wait_ge(S("sb_e"), 16 * j + n + 1)
                pool.tensor_tensor(Rs[:, hd, kb * P:], Rs[:, hd, kb * P:], sp[:, n % 2, :w], ALU.add).then_inc(S("sb_sum"), 1)
            pool.wait_ge(S("sb_sum"), 14 * j + 14)

        ar = Arena()
        mraw = ar.take(KC * MEM).rearrange("p (k t) -> p k t", k=KC)
        mT = ar.take(KC * MEM).rearrange("p (k t) -> p k t", k=KC)
        m_rs, x_rs = ar.take(MEM), ar.take(T)
        KcT = ar.take(KC * MEM).rearrange("p (k t) -> p k t", k=KC)
        Vc = ar.take(2 * D).rearrange("p (t f) -> p t f", t=2)
        at_x = ar.at
        qcT = ar.take(KC * T).rearrange("p (k t) -> p k t", k=KC)
        x_sq = qcT
        m_sq = KcT
        ar2 = Arena()
        kx = ar2.take(2 * MEM).rearrange("p (c t) -> p c t", c=2)
        vx = ar2.take(2 * MEM).rearrange("p (t f) -> p t f", t=2)
        Px = ar2.take(4 * MEM).rearrange("p (b q t) -> p b q t", b=2, q=2)
        pT = ar2.take(2 * T).rearrange("p (t q) -> p t q", t=2)
        assert ar2.at <= 2 * KC * MEM
        qx = uT[:, 0:2, PAD:PAD + T]

        def dyn(t, k, n, lo=0, hi=None):
            return t[:, bass.ds(k, n), lo:hi]

        def x_pe(pe, i):
            pe.wait_ge(S("x_copied"), 3 * i + 3)
            for s in range(6):
                if s < 4:
                    if s >= 2:
                        pe.wait_ge(S("x_exp"), 8 * i + 2 * s - 2)
                    for q in range(2):
                        lo = (2 * s + q) * P
                        for c in range(2):
                            m = pe.matmul(bank(s % 2)[:, q * MEM:(q + 1) * MEM], qx[:, c, lo:lo + P], kx[:, c, :],
                                          start=(c == 0), stop=(c == 1))
                    m.then_inc(S("x_scores"), 1)
                if 1 <= s <= 4:
                    t = s - 1
                    if t >= 2:
                        pe.wait_ge(S("x_tcopied"), 4 * i + t - 1)
                    pe.wait_ge(S("x_probs"), 8 * i + 2 * t + 2)
                    for kt in range(2):
                        for q in range(2):
                            m = pe.transpose(bank(2 + t % 2)[:, (2 * kt + q) * P:(2 * kt + q + 1) * P],
                                             Px[:, t % 2, q, kt * P:(kt + 1) * P], cst("ident"))
                    m.then_inc(S("x_turned"), 1)
                if s in (3, 5):
                    h = s // 4
                    pe.wait_ge(S("x_tcopied"), 4 * i + 2 * h + 2)
                    if h == 1:
                        pe.wait_ge(S("x_o_evac"), 4 * i + 2)
                    for dc in range(2):
                        for kt in range(2):
                            m = pe.matmul(bank(4 + dc), vx[:, kt, dc * P:(dc + 1) * P], pT[:, kt, h * HALF:(h + 1) * HALF],
                                          start=(kt == 0), stop=(kt == 1))
                        m.then_inc(S("x_o_mm"), 1)

        def x_act(act, i):
            act.activation(qx, dyn(qcT, 2 * i, 2), ACT.Copy).then_inc(S("x_copied"), 1)
            act.activation(kx, dyn(KcT, 2 * i, 2), ACT.Copy).then_inc(S("x_copied"), 1)
            act.activation(vx, Vc[:, :, bass.ds(i * MEM, MEM)], ACT.Copy).then_inc(S("x_copied"), 1)

            def turned(t):
                act.wait_ge(S("x_turned"), 4 * i + t + 1)
                act.activation(pT[:, :, t * MEM:(t + 1) * MEM], bank(2 + t % 2).rearrange("p (k q) -> p k q", k=2),
                               ACT.Copy).then_inc(S("x_tcopied"), 1)

            for s in range(5):
                if s < 4:
                    if s >= 2:
                        act.wait_ge(S("x_turned"), 4 * i + s - 1)
                    act.wait_ge(S("x_nmax"), 4 * i + s + 1)
                    for q in range(2):
                        act.activation(Px[:, s % 2, q, :], bank(s % 2)[:, q * MEM:(q + 1) * MEM], ACT.Exp,
                                       bias=nm[:, 2 * s + q:2 * s + q + 1], accum_out=el[:, 2 * s + q:2 * s + q + 1])\
                           .then_inc(S("x_exp"), 1)
                if s >= 1:
                    turned(s - 1)
            act.wait_ge(S("x_o_mm"), 4 * i + 4)

        def x_dve(dve, i):
            for s in range(6):
                if s < 4:
                    dve.wait_ge(S("x_scores"), 4 * i + s + 1)
                    dve.reduce_max(nm[:, 2 * s:2 * s + 2], bank(s % 2).rearrange("p (q t) -> p q t", q=2), AX,
                                   negate=True).then_inc(S("x_nmax"), 1)
                if 1 <= s <= 4:
                    t = s - 1
                    dve.wait_ge(S("x_exp"), 8 * i + 2 * t + 2)
                    dve.reciprocal(er[:, 2 * t:2 * t + 2], el[:, 2 * t:2 * t + 2]).then_inc(S("x_recip"), 1)
                    dve.wait_ge(S("x_recip"), 4 * i + t + 1)
                    for q in range(2):
                        dve.tensor_scalar(Px[:, t % 2, q, :], Px[:, t % 2, q, :], er[:, 2 * t + q:2 * t + q + 1], None,
                                          ALU.mult).then_inc(S("x_probs"), 1)
                if s in (3, 5):
                    h = s // 4
                    for dc in range(2):
                        dve.wait_ge(S("x_o_mm"), 4 * i + 2 * h + dc + 1)
                        dve.tensor_copy(yT[:, bass.ds(2 * i + dc, 1), h * HALF:(h + 1) * HALF].rearrange("p o t -> p (o t)"),
                                        bank(4 + dc)).then_inc(S("x_o_evac"), 1)

        ar = Arena()
        f_sq = ar.take(KC * T).rearrange("p (k t) -> p k t", k=KC)
        f_rs = ar.take(T)
        rl = ar.take(4 * HALF).rearrange("p (b t) -> p b t", b=4)

        def mlp_pe(pe, g):
            for q in range(32):
                p, h, s = q // 2, q % 2, q // 2 % NS
                if h == 0:
                    pe.wait_ge(w_in[s], 64 * g + 16 * (p // NS) + w_ready(s, (88 - UNIT_PANELS) // NS))
                if q < 4 or q >= 20:
                    pe.wait_ge(S("dn_evac"), 16 * g + (q if q < 4 else q - 16) + 1)
                else:
                    pe.wait_ge(S("relu_done"), 16 * g + q - 3)
                for k in range(KC):
                    if q == 16:
                        pe.wait_ge(S("hid_ready"), 16 * g + 2 * k + 2)
                    rhs = U(k, h * HALF, (h + 1) * HALF) if q < 16 else yT[:, k, h * HALF:(h + 1) * HALF]
                    m = pe.matmul(bank(q % 4), slot(s, k), rhs, start=(k == 0), stop=(k == KC - 1))
                    if h == 0 and k == 0:
                        m.then_inc(S("weight_free"), 1)
                m.then_inc(S("mlp_mm"), 1)

        def mlp_act(act, g):
            for q in range(16):
                act.wait_ge(S("mlp_mm"), 32 * g + q + 1)
                if q >= 4:
                    act.wait_ge(S("hid_ready"), 16 * g + q - 3)
                act.activation(rl[:, q % 4, :], bank(q % 4), ACT.Relu).then_inc(S("relu_done"), 1)

        def mlp_dve(dve, g):
            for q in range(16):
                dve.wait_ge(S("relu_done"), 16 * g + q + 1)
                dve.tensor_tensor(yT[:, q // 2, q % 2 * HALF:(q % 2 + 1) * HALF], rl[:, q % 4, :], rl[:, q % 4, :],
                                  ALU.mult).then_inc(S("hid_ready"), 1)
            for q in range(16):
                dve.wait_ge(S("mlp_mm"), 32 * g + 16 + q + 1)
                dst = hT[:, q // 2, q % 2 * HALF:(q % 2 + 1) * HALF]
                dve.tensor_tensor(dst, dst, bank(q % 4), ALU.add).then_inc(S("dn_evac"), 1)

        gpre = sb("gpre", [P, KC])

        G2 = 56 + UNIT_PANELS + 48
        P2_BANK = [q % 4 for q in range(12)] + [7] * 8 + [6 + q % 2 for q in range(28)]

        def p2_pe(pe, q):
            p, h, s = q // 2, q % 2, q // 2 % NS
            if h == 0:
                pe.wait_ge(w_in[s], 16 * (p // NS) + w_ready(s, (G2 - UNIT_PANELS) // NS))
            before = [x for x in range(q) if P2_BANK[x] == P2_BANK[q]]
            if before:
                pe.wait_ge(S("p2_evac"), before[-1] + 1)
            b = bank(P2_BANK[q])
            if p in (5, 8, 9):
                for t in range(4):
                    lo = h * HALF + t * P
                    for k in range(KC):
                        m = pe.matmul(b[:, t * P:(t + 1) * P], U(k, lo, lo + P), slot(s, k), start=(k == 0), stop=(k == KC - 1))
                        if h == 0 and t == 0 and k == 0:
                            m.then_inc(S("weight_free"), 1)
            else:
                for k in range(KC):
                    m = pe.matmul(b, slot(s, k), U(k, h * HALF, (h + 1) * HALF), start=(k == 0), stop=(k == KC - 1))
                    if h == 0 and k == 0:
                        m.then_inc(S("weight_free"), 1)
            m.then_inc(S("p2_mm"), 1)

        ar = Arena()
        rkv = arena[:, 0:6 * (PAD + T)].rearrange("p (c t) -> p c t", c=6)
        aq = ar.take(4 * T).rearrange("p (c t) -> p c t", c=4)
        ak, akx = ar.take(T), ar.take(T)
        av = ar.take(T).rearrange("p (t f) -> p t f", t=NT)
        gq, gk = ar.take(T), ar.take(T)
        gv = ar.take(2 * T).rearrange("p (t f) -> p t f", t=NT)
        at_g = ar.at
        sbias = ar.take(8 * 2 * P).rearrange("p (h k) -> p h k", h=8)
        WK = 2 * P + 4
        Sw = ar.take(8 * WK).rearrange("p (g h k) -> p g h k", g=2, h=4)
        Pw = ar.take(8 * WK).rearrange("p (g h k) -> p g h k", g=2, h=4)
        pos_f = pos_i[:, :].bitcast(F)
        pTw = pos_f.rearrange("p (k h q) -> p k h q", k=2, h=4)

        gate = [arena[:, 6 * (PAD + T) + 256:6 * (PAD + T) + 256 + HALF], sb("gate1", [P, HALF])[:, :]]

        def p2_act(act, q):
            p, h = q // 2, q % 2
            act.wait_ge(S("p2_mm"), q + 1)
            b, cols = bank(P2_BANK[q]), slice(h * HALF, (h + 1) * HALF)
            func, scale = ACT.Copy, 1.0
            if p < 4:
                dst, scale = aq[:, p, cols], 0.125
            elif p == 4:
                dst = ak[:, cols]
            elif p == 5:
                dst = av[:, 4 * h:4 * h + 4, :].rearrange("p t f -> p (t f)")
            elif p == 6:
                dst, scale = gq[:, cols], 32 ** -0.5
            elif p == 7:
                dst = gk[:, cols]
            elif p < 10:
                dst = gv[:, 4 * h:4 * h + 4, (p - 8) * P:(p - 7) * P]
                b = b.rearrange("p (t f) -> p t f", t=4)
            elif p < 16:
                dst = rkv[:, p - 10, PAD + h * HALF:PAD + (h + 1) * HALF]
            else:
                func = ACT.Silu
                if p in (20, 21):
                    dst = yT[:, 4 + p - 20, cols]
                else:
                    dst = gate[h]
                    if gate_uses(q) >= 1:
                        act.wait_ge(S("gated"), gate_uses(q))
            act.activation(dst, b, func, scale=scale).then_inc(S("p2_evac"), 1)

        GATES = [q for q in range(32, 48) if q // 2 not in (20, 21)]

        def gate_uses(q):
            return GATES.index(q) - 1

        def apply_gate(dve, q):
            p, h = q // 2, q % 2
            c = p - 16 if p < 20 else 6 + p - 22
            dst = yT[:, c, h * HALF:(h + 1) * HALF]
            dve.wait_ge(S("p2_evac"), q + 1)
            dve.tensor_tensor(dst, dst, gate[h], ALU.mult).then_inc(S("gated"), 1)

        def window(u):
            n = u // 2
            return n, u % 2, P if n == 0 else 0

        def swa_pe(pe):
            pe.wait_ge(S("akx_in"), 32)
            pe.wait_ge(S("p2_evac"), 12)
            for s in range(18):
                if s < 16:
                    n, g, lo = window(s)
                    if s >= 2:
                        pe.wait_ge(S("sw_biased"), s - 1)
                    for c in range(2):
                        for par in range(2):
                            r = slice(64 * par, 64 * par + 64)
                            src = ak if par == g else akx
                            m = pe.matmul(bank(2 * (s % 2) + par)[:, c * 2 * P + lo:(c + 1) * 2 * P], aq[r, 2 * g + c, n * P:(n + 1) * P],
                                          src[r, (n - 1) * P + lo:(n + 1) * P], start=True, stop=True)
                    m.then_inc(S("sw_scores"), 1)
                    if s < 8:
                        p2_pe(pe, 12 + s)
                if s >= 2:
                    t = s - 2
                    n, g, lo = window(t)
                    pe.wait_ge(S("sw_tcopied"), t + 1)
                    if t >= 1:
                        pe.wait_ge(S("sw_o_evac"), t)
                    for par in range(2):
                        for kt in range(lo // P, 2):
                            m = pe.matmul(PS[64 * par:64 * par + 64, 6 * HALF:6 * HALF + 2 * P], av[:, n - 1 + kt, 64 * g:64 * g + 64],
                                          pTw[:, kt, 2 * par:2 * par + 2, :].rearrange("p c q -> p (c q)"), start=(kt == lo // P), stop=(kt == 1))
                    m.then_inc(S("sw_o_mm"), 1)
                if 1 <= s <= 16:
                    t = s - 1
                    n, g, lo = window(t)
                    if t >= 1:
                        pe.wait_ge(S("sw_tcopied"), t)
                    pe.wait_ge(S("sw_probs"), t + 1)
                    for kt in range(lo // P, 2):
                        for h in range(4):
                            m = pe.transpose(bank(4 + kt)[:, h * P:(h + 1) * P], Pw[:, g, h, kt * P:(kt + 1) * P], cst("ident"))
                    m.then_inc(S("sw_turned"), 1)

        def swa_act(act):
            for s in range(17):
                if s < 16:
                    n, g, lo = window(s)
                    if s >= 2:
                        act.wait_ge(S("sw_turned"), s - 1)
                    act.wait_ge(S("sw_nmax"), s + 1)
                    for h in range(4):
                        m = act.activation(Pw[:, g, h, lo:2 * P + 1], Sw[:, g, h, lo:2 * P + 1], ACT.Exp,
                                           bias=nm[:, 4 * g + h:4 * g + h + 1], accum_out=el[:, 4 * g + h:4 * g + h + 1])
                        m.then_inc(S("sw_exp"), 1)
                    if s < 8:
                        p2_act(act, 12 + s)
                if s >= 1:
                    t = s - 1
                    n, g, lo = window(t)
                    act.wait_ge(S("sw_turned"), t + 1)
                    act.activation(pTw[:, lo // P:2, :, :].rearrange("p k h q -> p (k h q)"), bank(4 + lo // P, 2 - lo // P),
                                   ACT.Copy).then_inc(S("sw_tcopied"), 1)

        def swa_dve(dve):
            o = VEC["sinks"][0]
            for g in range(2):
                dve.tensor_copy(Sw[:, g, :, 2 * P:2 * P + 1], vec[:, o + 4 * g:o + 4 * g + 4].unsqueeze(2)).then_inc(S("sw_sink"), 1)
            dve.wait_ge(S("sw_sink"), 2)
            dve.wait_ge(S("bias_in"), 16)
            for s in range(18):
                if s < 16:
                    n, g, lo = window(s)
                    dve.wait_ge(S("sw_scores"), s + 1)
                    if s >= 2:
                        dve.wait_ge(S("sw_exp"), 4 * (s - 1))
                    dve.tensor_tensor(Sw[:, g, :, lo:2 * P], bank(2 * (s % 2), 2).rearrange("p (h k) -> p h k", h=4)[:, :, lo:],
                                      sbias[:, 4 * g:4 * g + 4, lo:], ALU.add).then_inc(S("sw_biased"), 1)
                    dve.wait_ge(S("sw_biased"), s + 1)
                    dve.reduce_max(nm[:, 4 * g:4 * g + 4], Sw[:, g, :, lo:2 * P + 1], AX, negate=True).then_inc(S("sw_nmax"), 1)
                if 1 <= s <= 16:
                    t = s - 1
                    n, g, lo = window(t)
                    dve.wait_ge(S("sw_exp"), 4 * t + 4)
                    dve.reciprocal(er[:, 4 * g:4 * g + 4], el[:, 4 * g:4 * g + 4]).then_inc(S("sw_recip"), 1)
                    dve.wait_ge(S("sw_recip"), t + 1)
                    dve.tensor_tensor(Pw[:, g, :, lo:2 * P], Pw[:, g, :, lo:2 * P],
                                      er[:, 4 * g:4 * g + 4].unsqueeze(2).broadcast_to([P, 4, 2 * P - lo]), ALU.mult)\
                       .then_inc(S("sw_probs"), 1)
                if s >= 2:
                    t = s - 2
                    n, g, lo = window(t)
                    dve.wait_ge(S("sw_o_mm"), t + 1)
                    dve.tensor_copy(yT[:, 2 * g:2 * g + 2, n * P:(n + 1) * P], bank(6)[:, :2 * P].rearrange("p (c q) -> p c q", c=2))\
                       .then_inc(S("sw_o_evac"), 1)

        CH = T // P
        ar = Arena()
        ar.at = at_g
        gb = ar.take(T)
        lv = ar.take(2 * T).rearrange("p (b t) -> p b t", b=2)
        gA = ar.take(4 * T).rearrange("p (h c t) -> p h c t", h=4, c=CH)
        g_lora = arena[:, 6 * (PAD + T):6 * (PAD + T) + 256]
        gt = gA[0:16, 0, :, :].rearrange("p c t -> p (c t)")
        gtmp, gy = gA[:, 1, :, :].rearrange("p c t -> p (c t)"), gA[:, 2, :, :].rearrange("p c t -> p (c t)")
        gS = yT[:, 4:6, :].rearrange("p a (c f) -> p (a c) f", c=4)
        g_q, g_k = lv[:, 0, :], lv[:, 1, :]
        gkt = pos_f.rearrange("p (c f) -> p c f", c=CH)
        elast = small[:, 0:CH]
        gsq = gA[:, 0:2, :, :].rearrange("p h c t -> p h (c t)")
        LEVELS = 8
        last_of = gb.rearrange("p (c t) -> p c t", c=CH)[:, :, P - 1:P]

        def gla_pe(pe, between):
            pe.wait_ge(S("glora_in"), 16)
            for h in range(2):
                for k in range(KC):
                    m = pe.matmul(PS[0:16, h * HALF:(h + 1) * HALF], g_lora[:, 16 * k:16 * k + 16], U(k, h * HALF, (h + 1) * HALF),
                                  start=(k == 0), stop=(k == KC - 1))
            m.then_inc(S("gl_down"), 1)
            pe.wait_ge(S("gl_down_taken"), 1)
            for h in range(2):
                m = pe.matmul(bank(2 + h), g_lora[0:16, P:2 * P], gt[:, h * HALF:(h + 1) * HALF], start=True, stop=True)
            m.then_inc(S("gl_gate"), 1)
            for l in range(LEVELS):
                if l == 0:
                    pe.wait_ge(S("p2_evac"), 16)
                    pe.wait_ge(S("gl_lin"), 1)
                else:
                    pe.wait_ge(S("gl_level"), 2 * l)
                for half in range(2):
                    if 2 * l + half >= 1:
                        pe.wait_ge(S("gl_taken"), 4 * (2 * l + half))
                    for cc in range(4):
                        c = 4 * half + cc
                        for h in range(4):
                            a, b = (gk, gq) if l == 0 else (lv[:, l % 2, :], lv[:, l % 2, :])
                            m = pe.matmul(bank(h)[:, cc * P:(cc + 1) * P], a[32 * h:32 * h + 32, c * P:(c + 1) * P],
                                          b[32 * h:32 * h + 32, c * P:(c + 1) * P], start=True, stop=True)
                    m.then_inc(S("gl_prod"), 1)
                for q in between[l]:
                    p2_pe(pe, q)
            pe.wait_ge(S("gl_k_dec"), 1)
            for c in range(CH):
                m = pe.transpose(bank(4 + c // 4)[:, c % 4 * P:(c % 4 + 1) * P], g_k[:, c * P:(c + 1) * P], cst("ident"))
            m.then_inc(S("gl_kt"), 1)
            pe.wait_ge(S("gl_kt_taken"), 1)
            pe.wait_ge(S("gl_taken"), 8 * LEVELS)
            for c in range(CH):
                m = pe.matmul(bank(c // 2)[:, c % 2 * 256:(c % 2 + 1) * 256], gkt[:, c, :], gv[:, c, :], start=True, stop=True)
                m.then_inc(S("gl_delta"), 1)
            pe.wait_ge(S("gl_states"), CH)
            pe.wait_ge(S("gl_q_dec"), 1)
            for hp in range(2):
                for c in range(CH):
                    o = slice(2 * hp * HALF + c * P, 2 * hp * HALF + (c + 1) * P)
                    pe.matmul(PS[:, o], gS[:, c, hp * P:(hp + 1) * P], g_q[:, c * P:(c + 1) * P], start=True, stop=False)
                    for x in range(2):
                        h = 2 * hp + x
                        m = pe.matmul(PS[64 * x:64 * x + 64, o], gv[:, c, 64 * h:64 * h + 64], gA[:, h, c, :], start=False, stop=True)
                m.then_inc(S("gl_o"), 1)
            for q in range(40, 44):
                p2_pe(pe, q)
            for hp in range(2):
                pe.wait_ge(S("gl_o_sq"), hp + 1)
                for h in range(2):
                    m = pe.matmul(bank(4 + h), cst("blk64"), gsq[:, hp, h * HALF:(h + 1) * HALF], start=True, stop=True)
                m.then_inc(S("gl_sum"), 1)
                pe.wait_ge(S("gl_root"), hp + 1)

        def gla_act(act, between):
            act.wait_ge(S("gl_down"), 1)
            act.activation(gt, PS[0:16, 0:T], ACT.Copy).then_inc(S("gl_down_taken"), 1)
            act.preload_act_table_set("natural_log_exp_and_others")
            act.wait_ge(S("gl_gate"), 1)
            act.activation(gy, bank(2, 2), ACT.Identity, bias=vcol("gk_b")).then_inc(S("gl_y"), 1)
            act.wait_ge(S("gl_y"), 1)
            act.activation(gtmp, gy, ACT.Abs).then_inc(S("gl_soft"), 1)
            act.wait_ge(S("gl_soft"), 1)
            act.activation(gtmp, gtmp, ACT.Exp, scale=-1.0).then_inc(S("gl_soft"), 1)
            act.wait_ge(S("gl_soft"), 2)
            act.activation(gtmp, gtmp, ACT.Ln, bias=1.0).then_inc(S("gl_soft"), 1)
            for l in range(1, LEVELS + 1):
                for q in between[l - 1]:
                    p2_act(act, q)
                if l < LEVELS:
                    act.wait_ge(S("gl_diff"), l)
                    act.activation(lv[:, l % 2, :], lv[:, l % 2, :], ACT.Exp, scale=1.0 / 16).then_inc(S("gl_exp"), 1)
            act.wait_ge(S("gl_end_diff"), 1)
            act.activation(g_k, g_k, ACT.Exp, scale=1.0 / 16).then_inc(S("gl_end_exp"), 1)
            act.activation(g_q, gb, ACT.Exp, scale=1.0 / 16).then_inc(S("gl_end_exp"), 1)
            act.activation(elast.unsqueeze(2), last_of, ACT.Exp, scale=1.0 / 16).then_inc(S("gl_end_exp"), 1)
            act.wait_ge(S("gl_kt"), 1)
            act.activation(gkt, bank(4, 2).rearrange("p (c f) -> p c f", c=CH), ACT.Copy).then_inc(S("gl_kt_taken"), 1)
            for hp in range(2):
                act.wait_ge(S("gl_o"), 2)
                act.activation(gsq[:, hp, :], bank(2 * hp, 2), ACT.Square).then_inc(S("gl_o_sq"), 1)
            for q in range(40, 44):
                p2_act(act, q)
            for hp in range(2):
                act.wait_ge(S("gl_sum"), hp + 1)
                act.activation(gsq[:, hp, :], bank(4, 2), ACT.Sqrt, bias=cst("eps5"), scale=1.0 / 64).then_inc(S("gl_root"), 1)

        def gla_dve(dve, between):
            dve.memset(pos_f, 1.0).then_inc(S("gl_mask"), 1)
            dve.wait_ge(S("gl_mask"), 1)
            dve.memset(pos_f.rearrange("p (c t) -> p c t", c=CH)[:, :, 0:1], 0.0).then_inc(S("gl_mask"), 1)
            dve.wait_ge(S("gl_soft"), 3)
            dve.scalar_tensor_tensor(gy, gy, 0.0, gtmp, ALU.min, ALU.subtract).then_inc(S("gl_lin"), 1)
            dve.wait_ge(S("gl_lin"), 1)
            dve.wait_ge(S("gl_mask"), 2)
            dve.tensor_tensor_scan(gb, pos_f, gy, 0.0, ALU.mult, ALU.add).then_inc(S("gl_cum"), 1)
            dve.wait_ge(S("gl_cum"), 1)

            def diff(l):
                n = 2 ** (l - 1)
                b4 = gb.rearrange("p (m h s) -> p m h s", h=2, s=n)
                d4 = lv[:, l % 2, :].rearrange("p (m h s) -> p m h s", h=2, s=n)
                ref = b4[:, :, 0, n - 1:n].broadcast_to([P, T // (2 * n), n])
                if l >= 3:
                    dve.wait_ge(S("gl_prod"), 2 * (l - 2) + 2)
                dve.tensor_tensor(d4[:, :, 1, :], b4[:, :, 1, :], ref, ALU.subtract).then_inc(S("gl_diff_up"), 1)
                dve.tensor_tensor(d4[:, :, 0, :], ref, b4[:, :, 0, :], ALU.subtract).then_inc(S("gl_diff"), 1)

            diff(1)
            for l in range(LEVELS):
                if l >= 1 and l + 1 < LEVELS:
                    diff(l + 1)
                elif l == 0:
                    pass
                for half in range(2):
                    dve.wait_ge(S("gl_prod"), 2 * l + half + 1)
                    for h in range(4):
                        dst = gA[:, h, 4 * half:4 * half + 4, :]
                        src = bank(h).rearrange("p (c t) -> p c t", c=4)
                        if l == 0:
                            dve.tensor_tensor(dst, src, cst("ident").unsqueeze(1).broadcast_to([P, 4, P]), ALU.mult)\
                               .then_inc(S("gl_taken"), 1)
                        else:
                            o = CONST["level"][0] + (l - 1) * P
                            mask = const[:, o:o + P].bitcast(I32).unsqueeze(1).broadcast_to([P, 4, P])
                            dve.copy_predicated(dst, mask, src).then_inc(S("gl_taken"), 1)
                for q in between[l]:
                    if q in GATES:
                        apply_gate(dve, q)
            dve.wait_ge(S("gl_prod"), 2 * LEVELS)
            b3 = gb.rearrange("p (c t) -> p c t", c=CH)
            dve.tensor_tensor(g_k.rearrange("p (c t) -> p c t", c=CH), last_of.broadcast_to([P, CH, P]), b3,
                              ALU.subtract).then_inc(S("gl_end_diff"), 1)
            dve.wait_ge(S("gl_end_exp"), 2)
            dve.tensor_tensor(g_k, g_k, gk, ALU.mult).then_inc(S("gl_k_dec"), 1)
            dve.tensor_tensor(g_q, g_q, gq, ALU.mult).then_inc(S("gl_q_dec"), 1)
            dve.wait_ge(S("gl_end_exp"), 3)
            dve.memset(gS[:, 0, :], 0.0).then_inc(S("gl_states"), 1)
            for c in range(CH - 1):
                dve.wait_ge(S("gl_delta"), c // 2 * 2 + 2)
                dve.wait_ge(S("gl_states"), c + 1)
                dve.tensor_tensor(small_delta, bank(c // 2)[:, c % 2 * 256:(c % 2 + 1) * 256], cst("gla_state"),
                                  ALU.mult).then_inc(S("gl_masked"), 1)
                dve.wait_ge(S("gl_masked"), c + 1)
                dve.scalar_tensor_tensor(gS[:, c + 1, :], gS[:, c, :], elast[:, c:c + 1], small_delta, ALU.mult, ALU.add)\
                   .then_inc(S("gl_states"), 1)
            dve.wait_ge(S("gl_delta"), CH)
            for hp in range(2):
                dve.wait_ge(S("gl_root"), hp + 1)
                dve.reciprocal(gsq[:, hp, :], gsq[:, hp, :]).then_inc(S("gl_rstd"), 1)
                dve.wait_ge(S("gl_rstd"), hp + 1)
                dve.scalar_tensor_tensor(yT[:, 6 + hp, :], bank(2 * hp, 2), vcol("gla_norm"), gsq[:, hp, :], ALU.mult, ALU.mult)\
                   .then_inc(S("gl_y_ready"), 1)

        KAPPA = float(np.exp(-0.5))
        TL = 4
        RW_LEVELS = range(1, 6)
        RW_STEPS = {
            "act": ["sig_w", "sig_a", "kk_sq", "kk_root", "exp_p", "exp_pinv", "exp_pm", "tok_c", "tok_b", "tok_k", "tok_v", "mbt"]
                   + [f"x{l}{b}" for l in RW_LEVELS for b in range(2)] + ["mkv", "nw0", "nw1", "nw1t", "y0", "y1", "y_sq", "y_root"],
            "pe": ["lora", "kk_sum", "bon_sum", "tr_c", "tr_b", "tr_k", "tr_v", "p_mbt", "p_mb", "p_mkt", "p_rbt", "p_rkt"]
                  + [f"{x}{l}{b}" for l in RW_LEVELS for x in ("px", "pd") for b in range(2)]
                  + ["p_mkv", "pw0", "pw1", "pw1t", "p_gt", "p_h"] + [f"ps{c}" for c in range(8)] + ["pu", "py", "y_sum", "y_var"],
            "dve": ["kk", "cum", "cum_m", "a_ka", "k_new", "kk_max", "kk_rec", "kkn", "kk_a", "bhat", "bonus", "bonus_v",
                    "tt_a", "tt", "t_a", "t", "mkt", "rbt", "rkt"] + [f"up{l}{b}" for l in RW_LEVELS for b in range(2)]
                   + ["s_start", "gt", "h"] + [f"s{c}" for c in range(8)] + ["u", "centre", "y_rec", "y_norm", "y_sum", "gated"],
            "pool": ["chat", "khat", "rhat"] + [f"ms{l}{b}" for l in RW_LEVELS for b in range(2)],
        }
        rw_next = {e: 0 for e in RW_STEPS}

        def rw(e, name, u):
            return S("rw_" + e), len(RW_STEPS[e]) * u + RW_STEPS[e].index(name) + 1

        def rw_done(e, name, ins):
            assert RW_STEPS[e][rw_next[e] % len(RW_STEPS[e])] == name, (e, name)
            rw_next[e] += 1
            ins.then_inc(S("rw_" + e), 1)

        w2a2 = g_lora
        ar = Arena()
        ar.at = 6 * (PAD + T) + 256 + HALF
        lt = ar.take(T)
        sg, cum, aa, kkn, kn, tm, chat, bhat, khat, rhat, Pt, Pinv, Pm, yv, bv = (ar.take(HALF) for _ in range(15))
        ctok, btok, ktok, vtok = (ar.take(HALF).rearrange("p (t f) -> p t f", t=TL) for _ in range(4))
        Sst = ar.take(9 * 64).rearrange("p (c v) -> p c v", c=9)
        Ub = Pm.rearrange("p (h t v) -> p h t v", h=2, t=TL)
        nw1t, GT, Hb = sg, aa.rearrange("p (t c k) -> p t c k", c=2, k=64), kkn.rearrange("p (t c k) -> p t c k", c=2, k=64)
        flat = uT[:, :, :].rearrange("p k t -> p (k t)")
        Tm, TTm, MbT, Xm, Ms, MkT, RBT, RKT = (flat[:, x * T:(x + 1) * T].rearrange("p (h t j) -> p h t j", h=2, t=TL)
                                               for x in range(8))
        nW = Xm
        mkv = flat[:, 4 * T:4 * T + HALF].rearrange("p (h t v) -> p h t v", h=2, t=TL)
        wa_raw, wa_mu, wa_rest = (arena[:, 9216 + x * T:9216 + (x + 1) * T].rearrange("p (k f) -> p k f", k=KC)
                                  for x in range(3))
        mixd = [arena[:, 12288 + x * T:12288 + (x + 1) * T] for x in range(2)]
        smask = pos_f[:, 0:HALF]

        def rw_pre_pe(pe):
            pe.wait_ge(S("wa_ready"), KC)
            for h in range(2):
                for k in range(KC):
                    pe.matmul(bank(h), wa_rest[:, k, :], U(k, h * HALF, (h + 1) * HALF), start=(k == 0), stop=False)
                    m = pe.matmul(bank(h), wa_mu[:, k, :], U(k, h * HALF - 1, (h + 1) * HALF - 1), start=False, stop=(k == KC - 1))
                m.then_inc(S("lora_mm"), 1)

        def rw_pre_act(act):
            for h in range(2):
                act.wait_ge(S("lora_mm"), h + 1)
                act.activation(lt[0:64, h * HALF:(h + 1) * HALF], bank(h)[0:64, :], ACT.Tanh).then_inc(S("lora_out"), 1)
                act.activation(lt[64:128, h * HALF:(h + 1) * HALF], bank(h)[64:128, :], ACT.Copy).then_inc(S("lora_out"), 1)

        def rw_pre_dve(dve):
            dve.wait_ge(S("wa_in"), 32)
            for k in range(KC):
                dve.tensor_scalar(wa_mu[:, k, 0:64], wa_raw[:, k, 0:64], vcol("mu_w", k), None, ALU.mult).then_inc(S("wa_part"), 1)
                dve.tensor_scalar(wa_mu[:, k, 64:128], wa_raw[:, k, 64:128], vcol("mu_a", k), None, ALU.mult).then_inc(S("wa_part"), 1)
            for k in range(KC):
                dve.wait_ge(S("wa_part"), 2 * k + 2)
                dve.tensor_tensor(wa_rest[:, k, :], wa_raw[:, k, :], wa_mu[:, k, :], ALU.subtract).then_inc(S("wa_ready"), 1)
            dve.memset(smask, 1.0).then_inc(S("rw_mask"), 1)
            dve.wait_ge(S("rw_mask"), 1)
            dve.memset(smask.rearrange("p (c t) -> p c t", t=64)[:, :, 0:1], 0.0).then_inc(S("rw_mask"), 1)
            for x in range(6):
                dve.wait_ge(S("rkv_diff"), x + 1)
                dve.scalar_tensor_tensor(rkv[:, x, PAD:], mixd[x % 2], vcol("mu_rkv", x), rkv[:, x, PAD:], ALU.mult, ALU.add)\
                   .then_inc(S("rkv_mixed"), 1)

        def rw_pre_pool(pool):
            pool.wait_ge(S("gl_y_ready"), 2)
            pool.dma_start(wa_raw.rearrange("p k f -> p (k f)"), lora_d[:, 0:T]).then_inc(S("wa_in"), 16)
            pool.dma_start(w2a2, lora_d[:, T + 256:T + 512]).then_inc(S("wa_in"), 16)
            pool.wait_ge(S("p2_evac"), 32)
            pool.wait_ge(S("rkv_pad"), 1)
            for x in range(6):
                if x >= 2:
                    pool.wait_ge(S("rkv_mixed"), x - 1)
                pool.tensor_tensor(mixd[x % 2], rkv[:, x, PAD - 1:PAD + T - 1], rkv[:, x, PAD:], ALU.subtract).then_inc(S("rkv_diff"), 1)

        def rw_rows(u):
            p, hf = u // 2, u % 2
            cols = slice(PAD + hf * HALF, PAD + (hf + 1) * HALF)
            return p, hf, rkv[:, p, cols], rkv[:, 2 + p, cols], rkv[:, 4 + p, cols]

        def rw_pe(pe, u):
            p, hf, r_, k_, v_ = rw_rows(u)
            w, done = (lambda e, n, uu=u: pe.wait_ge(*rw(e, n, uu))), (lambda n, ins: rw_done("pe", n, ins))
            if u >= 1:
                w("dve", "gated", u - 1)
            tc = slice(hf * HALF, (hf + 1) * HALF)
            pe.matmul(bank(0), w2a2[0:64, p * P:(p + 1) * P], lt[0:64, tc], start=True, stop=True)
            done("lora", pe.matmul(bank(1), w2a2[64:128, p * P:(p + 1) * P], lt[64:128, tc], start=True, stop=True))
            w("act", "kk_sq")
            done("kk_sum", pe.matmul(bank(2), cst("blk64"), tm, start=True, stop=True))
            w("dve", "bonus")
            done("bon_sum", pe.matmul(bank(3), cst("blk64"), bv, start=True, stop=True))
            for x, (n, src, e, ready) in enumerate((("tr_c", chat, "pool", "chat"), ("tr_b", bhat, "dve", "bhat"),
                                                    ("tr_k", khat, "pool", "khat"), ("tr_v", v_, None, None))):
                if e:
                    w(e, ready)
                for t in range(TL):
                    m = pe.transpose(bank(4 + x)[:, t * P:(t + 1) * P], src[:, t * P:(t + 1) * P], cst("ident"))
                done(n, m)
            w("pool", "rhat")
            for n, a, b, bk, free in (("p_mbt", bhat, chat, 0, ("act", "sig_a")), ("p_mb", chat, bhat, 2, ("dve", "bonus_v")),
                                      ("p_mkt", khat, chat, 4, ("act", "tok_b")), ("p_rbt", bhat, rhat, 6, ("act", "tok_v")),
                                      ("p_rkt", khat, rhat, 0, ("act", "mbt"))):
                w(*free)
                for t in range(TL):
                    for h in range(2):
                        r = slice(64 * h, 64 * h + 64)
                        m = pe.matmul(bank(bk + h)[:, t * P:(t + 1) * P], a[r, t * P:(t + 1) * P], b[r, t * P:(t + 1) * P],
                                      start=True, stop=True)
                done(n, m)
            for l in RW_LEVELS:
                for b in range(2):
                    if l == 1 and b == 0:
                        w("dve", "rkt")
                    if l > 1:
                        w("dve", f"up{l - 1}{b}")
                    w("pool", f"ms{l}{b}")
                    for t in range(TL):
                        m = pe.matmul(bank(b)[:, t * P:(t + 1) * P], Ms[:, b, t, :], Tm[:, b, t, :], start=True, stop=True)
                    done(f"px{l}{b}", m)
                for b in range(2):
                    w("act", f"x{l}{b}")
                    for t in range(TL):
                        if l < 5:
                            pe.matmul(bank(2 + b)[:, t * P:(t + 1) * P], TTm[:, b, t, :], Xm[:, b, t, :], start=True, stop=True)
                        m = pe.matmul(bank(4 + b)[:, t * P:(t + 1) * P], Xm[:, b, t, :], TTm[:, b, t, :], start=True, stop=True)
                    done(f"pd{l}{b}", m)
            for h in range(2):
                for t in range(TL):
                    m = pe.matmul(bank(6)[:, (TL * h + t) * 64:(TL * h + t + 1) * 64], MkT[:, h, t, :], vtok[:, t, 64 * h:64 * h + 64],
                                  start=True, stop=True)
            done("p_mkv", m)
            w("act", "mkv")
            for h in range(2):
                w("dve", f"up5{h}")
                for t in range(TL):
                    pe.matmul(bank(h)[:, t * P:t * P + 64], TTm[:, h, t, :], ctok[:, t, 64 * h:64 * h + 64], start=True, stop=True)
                    m = pe.matmul(bank(h)[:, t * P + 64:(t + 1) * P], TTm[:, h, t, :], mkv[:, h, t, :], start=True, stop=True)
                done(f"pw{h}", m)
            for h in range(2):
                for t in range(TL):
                    m = pe.matmul(PS[64 * h:64 * h + 64, 2 * HALF + t * P:2 * HALF + (t + 1) * P], ctok[:, t, 64 * h:64 * h + 64],
                                  TTm[:, h, t, :], start=True, stop=True)
            done("pw1t", m)
            w("act", "nw1")
            for h in range(2):
                for t in range(TL):
                    for cp in range(2):
                        rr = slice(64 * cp, 64 * cp + 64)
                        m = pe.matmul(PS[64 * h:64 * h + 64, (4 + cp) * HALF + t * 64:(4 + cp) * HALF + (t + 1) * 64],
                                      nW[rr, h, t, 0:64], btok[rr, t, 64 * h:64 * h + 64], start=True, stop=True)
            done("p_gt", m)
            for h in range(2):
                for t in range(TL):
                    for cp in range(2):
                        rr = slice(64 * cp, 64 * cp + 64)
                        o = PS[64 * h:64 * h + 64, (6 + cp) * HALF + t * 64:(6 + cp) * HALF + (t + 1) * 64]
                        pe.matmul(o, ktok[rr, t, 64 * h:64 * h + 64], vtok[rr, t, 64 * h:64 * h + 64], start=True, stop=False)
                        m = pe.matmul(o, btok[rr, t, 64 * h:64 * h + 64], nW[rr, h, t, 64:128], start=False, stop=True)
            done("p_h", m)
            for c in range(8):
                w("dve", "h" if c == 0 else f"s{c - 1}")
                for h in range(2):
                    r = slice(64 * h, 64 * h + 64)
                    m = pe.matmul(PS[r, h * HALF:h * HALF + 64], GT[r, c // 2, c % 2, :], Sst[r, c, :], start=True, stop=True)
                done(f"ps{c}", m)
            w("act", "nw1t")
            for t in range(TL):
                for cp in range(2):
                    for h in range(2):
                        r = slice(64 * h, 64 * h + 64)
                        m = pe.matmul(PS[64 * cp:64 * cp + 64, (2 + h) * HALF + t * 64:(2 + h) * HALF + (t + 1) * 64],
                                      nw1t[r, t * P + 64 * cp:t * P + 64 * cp + 64], Sst[r, 2 * t + cp, :], start=True, stop=True)
            done("pu", m)
            w("dve", "u")
            for h in range(2):
                r = slice(64 * h, 64 * h + 64)
                for t in range(TL):
                    o = (4 + h) * HALF + t * P
                    pe.matmul(PS[r, o:o + P], vtok[:, t, 64 * h:64 * h + 64], RKT[:, h, t, :], start=True, stop=False)
                    pe.matmul(PS[r, o:o + P], Ub[:, h, t, :], RBT[:, h, t, :], start=False, stop=False)
                    for cp in range(2):
                        m = pe.matmul(PS[r, o + 64 * cp:o + 64 * cp + 64], Sst[r, 2 * t + cp, :],
                                      rhat[r, t * P + 64 * cp:t * P + 64 * cp + 64], start=False, stop=(cp == 1))
            done("py", m)
            w("act", "y1")
            done("y_sum", pe.matmul(bank(6), cst("blk64"), yv, start=True, stop=True))
            w("act", "y_sq")
            done("y_var", pe.matmul(bank(7), cst("blk64"), tm, start=True, stop=True))

        def rw_act(act, u):
            p, hf, r_, k_, v_ = rw_rows(u)
            w, done = (lambda e, n, uu=u: act.wait_ge(*rw(e, n, uu))), (lambda n, ins: rw_done("act", n, ins))
            w("pe", "lora")
            done("sig_w", act.activation(sg, bank(0), ACT.Sigmoid, bias=vcol("w0", p)))
            done("sig_a", act.activation(aa, bank(1), ACT.Sigmoid, bias=vcol("a0", p)))
            w("dve", "kk")
            done("kk_sq", act.activation(tm, kkn, ACT.Square))
            w("pe", "kk_sum")
            done("kk_root", act.activation(tm, bank(2), ACT.Sqrt))
            w("dve", "cum_m")
            done("exp_p", act.activation(Pt, cum, ACT.Exp, scale=-KAPPA))
            done("exp_pinv", act.activation(Pinv, cum, ACT.Exp, scale=KAPPA))
            done("exp_pm", act.activation(Pm, Pm, ACT.Exp, scale=-KAPPA))
            for x, (n, tr, dst) in enumerate((("tok_c", "tr_c", ctok), ("tok_b", "tr_b", btok), ("tok_k", "tr_k", ktok),
                                              ("tok_v", "tr_v", vtok))):
                w("pe", tr)
                done(n, act.activation(dst.rearrange("p t f -> p (t f)"), bank(4 + x), ACT.Copy))
            w("pe", "p_mbt")
            done("mbt", act.activation(MbT.rearrange("p h t j -> p (h t j)"), bank(0, 2), ACT.Copy))
            for l in RW_LEVELS:
                for b in range(2):
                    w("pe", f"px{l}{b}")
                    if l > 1:
                        w("pe", f"pd{l - 1}{b}")
                    elif b == 0:
                        w("dve", "tt")
                    done(f"x{l}{b}", act.activation(Xm[:, b, :, :].rearrange("p t j -> p (t j)"), bank(b), ACT.Copy))
            w("pe", "p_mkv")
            done("mkv", act.activation(mkv.rearrange("p h t v -> p (h t v)"), bank(6), ACT.Copy))
            for h in range(2):
                w("pe", f"pw{h}")
                done(f"nw{h}", act.activation(nW[:, h, :, :].rearrange("p t j -> p (t j)"), bank(h), ACT.Copy, scale=-1.0))
            w("pe", "pw1t")
            done("nw1t", act.activation(nw1t, bank(2), ACT.Copy, scale=-1.0))
            w("pe", "py")
            for h in range(2):
                r = slice(64 * h, 64 * h + 64)
                done(f"y{h}", act.activation(yv[r, :], PS[r, (4 + h) * HALF:(5 + h) * HALF], ACT.Copy))
            w("dve", "centre")
            done("y_sq", act.activation(tm, yv, ACT.Square))
            w("pe", "y_var")
            done("y_root", act.activation(tm, bank(7), ACT.Sqrt, bias=cst("eps_ln"), scale=1.0 / 64))

        def rw_dve(dve, u):
            p, hf, r_, k_, v_ = rw_rows(u)
            w, done = (lambda e, n, uu=u: dve.wait_ge(*rw(e, n, uu))), (lambda n, ins: rw_done("dve", n, ins))

            def eight(x):
                return x.unsqueeze(1).broadcast_to([P, 8, P])

            def flat8(x):
                return x.rearrange("p h t j -> p (h t) j")

            def banks8(b):
                return bank(b, 2).rearrange("p (x j) -> p x j", x=8)

            done("kk", dve.tensor_scalar(kkn, k_, vcol("k_k", p), None, ALU.mult))
            w("act", "sig_w")
            done("cum", dve.tensor_tensor_scan(cum, smask, sg, 0.0, ALU.mult, ALU.add))
            w("dve", "cum")
            done("cum_m", dve.tensor_tensor(Pm, cum, sg, ALU.subtract))
            w("act", "sig_a")
            done("a_ka", dve.tensor_scalar(kn, aa, 1.0, vcol("k_a", p), ALU.subtract, ALU.mult))
            w("dve", "a_ka")
            done("k_new", dve.scalar_tensor_tensor(kn, kn, 1.0, k_, ALU.add, ALU.mult))
            w("act", "kk_root")
            done("kk_max", dve.tensor_scalar(tm, tm, 1e-12, None, ALU.max))
            w("dve", "kk_max")
            done("kk_rec", dve.reciprocal(tm, tm))
            w("dve", "kk_rec")
            done("kkn", dve.tensor_tensor(kkn, kkn, tm, ALU.mult))
            w("dve", "kkn")
            done("kk_a", dve.tensor_tensor(bhat, kkn, aa, ALU.mult))
            w("dve", "kk_a")
            w("act", "exp_pinv")
            done("bhat", dve.tensor_tensor(bhat, bhat, Pinv, ALU.mult))
            done("bonus", dve.scalar_tensor_tensor(bv, r_, vcol("r_k", p), kn, ALU.mult, ALU.mult))
            w("pe", "bon_sum")
            done("bonus_v", dve.tensor_tensor(bv, bank(3), v_, ALU.mult))
            w("act", "mbt")
            o = CONST["level"][0]
            done("tt_a", dve.tensor_tensor(flat8(Xm), flat8(MbT), eight(const[:, o:o + P]), ALU.mult))
            w("dve", "tt_a")
            done("tt", dve.tensor_tensor(flat8(TTm), eight(cst("ident")), flat8(Xm), ALU.subtract))
            w("pe", "p_mb")
            done("t_a", dve.tensor_tensor(flat8(Tm), banks8(2), eight(cst("first_low")), ALU.mult))
            w("dve", "t_a")
            done("t", dve.tensor_tensor(flat8(Tm), eight(cst("ident")), flat8(Tm), ALU.subtract))
            w("pe", "p_mkt")
            done("mkt", dve.tensor_tensor(flat8(MkT), banks8(4), eight(cst("strict64")), ALU.mult))
            w("pe", "p_rbt")
            done("rbt", dve.tensor_tensor(flat8(RBT), banks8(6), eight(cst("incl64")), ALU.mult))
            w("pe", "p_rkt")
            done("rkt", dve.tensor_tensor(flat8(RKT), banks8(0), eight(cst("incl64")), ALU.mult))
            for l in RW_LEVELS:
                for b in range(2):
                    w("pe", f"pd{l}{b}")
                    if l < 5:
                        t2 = Tm[:, b, :, :].rearrange("p t j -> p (t j)")
                        dve.tensor_tensor(t2, t2, bank(2 + b), ALU.subtract).then_inc(S("rw_t"), 1)
                    t2 = TTm[:, b, :, :].rearrange("p t j -> p (t j)")
                    if l < 5:
                        dve.wait_ge(S("rw_t"), 8 * u + 2 * (l - 1) + b + 1)
                    done(f"up{l}{b}", dve.tensor_tensor(t2, t2, bank(4 + b), ALU.subtract))
            if hf == 0:
                done("s_start", dve.memset(Sst[:, 0, :], 0.0))
            else:
                done("s_start", dve.tensor_copy(Sst[:, 0, :], Sst[:, 8, :]))
            w("pe", "p_gt")
            done("gt", dve.tensor_tensor(GT.rearrange("p t c k -> p c t k"), bank(4, 2).rearrange("p (c x) -> p c x", c=2)[:, :, 0:256]
                                         .rearrange("p c (t k) -> p c t k", t=TL),
                                         cst("ident64").unsqueeze(1).unsqueeze(1).broadcast_to([P, 2, TL, 64]), ALU.add))
            w("pe", "p_h")
            done("h", dve.tensor_tensor(Hb.rearrange("p t c k -> p c t k"), bank(6, 2).rearrange("p (c x) -> p c x", c=2)[:, :, 0:256]
                                        .rearrange("p c (t k) -> p c t k", t=TL),
                                        Pt.rearrange("p (t c s) -> p c t s", c=2, s=64)[:, :, :, 63:64].broadcast_to([P, 2, TL, 64]),
                                        ALU.mult))
            w("dve", "h")
            for c in range(8):
                w("pe", f"ps{c}")
                for h in range(2):
                    r = slice(64 * h, 64 * h + 64)
                    m = dve.scalar_tensor_tensor(Sst[r, c + 1, :], PS[r, h * HALF:h * HALF + 64], Pt[r, 64 * c + 63:64 * c + 64],
                                                 Hb[r, c // 2, c % 2, :], ALU.mult, ALU.add)
                    if h == 0:
                        m.then_inc(S("rw_s"), 1)
                dve.wait_ge(S("rw_s"), 8 * u + c + 1)
                done(f"s{c}", m)
            w("pe", "pu")
            done("u", dve.tensor_tensor(Ub, bank(2, 2).rearrange("p (h x) -> p h x", h=2)[:, :, 0:256].rearrange("p h (t v) -> p h t v", t=TL),
                                        nW[:, :, :, 64:128], ALU.add))
            w("pe", "y_sum")
            done("centre", dve.scalar_tensor_tensor(yv, bank(6), -1.0 / 64, yv, ALU.mult, ALU.add))
            w("act", "y_root")
            done("y_rec", dve.reciprocal(tm, tm))
            w("dve", "y_rec")
            done("y_norm", dve.scalar_tensor_tensor(yv, yv, vcol("ln_w", p), tm, ALU.mult, ALU.mult))
            w("dve", "y_norm")
            done("y_sum", dve.scalar_tensor_tensor(yv, yv, vcol("ln_b", p), bv, ALU.add, ALU.add))
            w("dve", "y_sum")
            dst = yT[:, 4 + p, hf * HALF:(hf + 1) * HALF]
            done("gated", dve.tensor_tensor(dst, dst, yv, ALU.mult))

        def rw_pool(pool, u):
            p, hf, r_, k_, v_ = rw_rows(u)
            w, done = (lambda e, n, uu=u: pool.wait_ge(*rw(e, n, uu))), (lambda n, ins: rw_done("pool", n, ins))
            w("dve", "kkn")
            w("act", "exp_pm")
            done("chat", pool.tensor_tensor(chat, kkn, Pm, ALU.mult))
            done("khat", pool.tensor_tensor(khat, kn, Pinv, ALU.mult))
            done("rhat", pool.tensor_tensor(rhat, r_, Pt, ALU.mult))
            w("act", "mbt")
            for l in RW_LEVELS:
                for b in range(2):
                    if l > 1:
                        w("pe", f"px{l - 1}{b}")
                    o = CONST["level"][0] + l * P
                    done(f"ms{l}{b}", pool.tensor_tensor(Ms[:, b, :, :], MbT[:, b, :, :],
                                                         const[:, o:o + P].unsqueeze(1).broadcast_to([P, TL, P]), ALU.mult))

        gpost = sb("gpost", [P, KC])
        small_delta = sb("small_delta", [P, 256])[:, :]
        BETWEEN = [[20 + 3 * l + x for x in range(3) if 3 * l + x < 20] for l in range(LEVELS)]

        block = ctx.enter_context(nc.Block())

        @block.sync
        def _(sync):
            sync.dma_start(const[:, :], const_d).then_inc(S("const_in"), 16)
            sync.dma_start(vec[:, :], vec_d).then_inc(S("vec_in"), 16)
            for k in range(KC):
                sync.dma_start(hT[:, k, :], xT_d[:, k, :]).then_inc(S("x_in"), 16)
            sync.dma_start(pos_i[:, :], pos_d).then_inc(S("pos_in"), 16)
            with loop(sync, 2 * UNITS) as i:
                for s in range(3):
                    sync.wait_ge(S("weight_free"), 3 * i + s + 3)
                    sync.dma_start(wring[:, s, :], w_d[bass.ds(3 * i + s, 1), :, :].rearrange("o p n -> p (o n)"))\
                        .then_inc(w_in[s], 16)
            with loop(sync, 34) as i:
                for s in range(NS):
                    sync.wait_ge(S("weight_free"), NS * i + (UNIT_PANELS + s + 3))
                    sync.dma_start(wring[:, s, :], w_d[bass.ds(NS * i + (UNIT_PANELS + s), 1), :, :].rearrange("o p n -> p (o n)"))\
                        .then_inc(w_in[s], 16)
            for k in range(KC):
                sync.wait_ge(S("final_ready"), k + 1)
                sync.dma_start(out_d[:, k, :], hT[:, k, :]).then_inc(S("stored"), 16)
            sync.wait_ge(S("stored"), 16 * KC)

        @block.vector
        def _(dve):
            dve.memset(uT[:, :, 0:PAD], 0.0).then_inc(S("pad_zero"), 1)
            dve.wait_ge(S("vec_in"), 16)
            o = VEC["lam"][0]
            dve.memset(lamt[:, :], 0.0).then_inc(S("lam_a"), 1)
            dve.wait_ge(S("lam_a"), 1)
            for x in range(2):
                dve.tensor_tensor(lamt[:, x:x + 1], vec[:, o + 2 * x:o + 2 * x + 1], vec[:, o + 2 * x + 1:o + 2 * x + 2],
                                  ALU.mult).then_inc(S("lam_prod"), 1)
            dve.tensor_scalar(gsub[:, :], vcol("g_subln"), 1.0 - LAM_INIT, None, ALU.mult).then_inc(S("gsub_ready"), 1)
            dve.wait_ge(S("pos_in"), 16)
            dve.wait_ge(S("const_in"), 16)
            dve.tensor_copy(posf, pos_i[:, :]).then_inc(S("ang_step"), 1)
            dve.wait_ge(S("ang_step"), 1)
            dve.tensor_scalar(ang, posf, cst("inv_freq"), None, ALU.mult).then_inc(S("ang_step"), 1)
            dve.wait_ge(S("ang_step"), 2)
            dve.tensor_scalar(turns, ang, 0.15915494309189535, 12582912.0, ALU.mult, ALU.add).then_inc(S("ang_step"), 1)
            dve.wait_ge(S("ang_step"), 3)
            dve.tensor_scalar(turns, turns, 12582912.0, None, ALU.subtract).then_inc(S("ang_step"), 1)
            dve.wait_ge(S("ang_step"), 4)
            dve.scalar_tensor_tensor(ang, turns, -6.28125, ang, ALU.mult, ALU.add).then_inc(S("ang_step"), 1)
            dve.wait_ge(S("ang_step"), 5)
            dve.scalar_tensor_tensor(ang, turns, -0.0019353071795864769, ang, ALU.mult, ALU.add).then_inc(S("ang_step"), 1)
            dve.wait_ge(S("ang_step"), 6)
            dve.tensor_scalar(ang, ang, 3.1415925, -3.1415925, ALU.min, ALU.max).then_inc(S("ang_step"), 1)
            dve.wait_ge(S("ang_step"), 7)
            dve.scalar_tensor_tensor(posf, ang, -1.0, ang, ALU.mult, ALU.max).then_inc(S("ang_ready"), 1)
            dve.wait_ge(S("lam_exp"), 1)
            dve.tensor_tensor(lamt[:, 4:5], lamt[:, 3:4], lamt[:, 2:3], ALU.subtract).then_inc(S("lam_a"), 1)
            dve.wait_ge(S("lam_a"), 2)
            dve.tensor_scalar(lamt[:, 5:6], lamt[:, 4:5], LAM_INIT, None, ALU.subtract).then_inc(S("lam_a"), 1)
            dve.wait_ge(S("lam_a"), 3)
            norm_dve(dve, "mix", lambda k: hT[:, k, :], lambda k: U(k), lambda k: vcol("g_mix", k), T, n_rs)
            with loop(dve, 4) as i:
                da_dve(dve, i)
            with loop(dve, 4) as j:
                sb_dve(dve, j)
            dve.wait_ge(S("sb_y_ready"), 4)
            dve.sem_inc(S("wo_evac"), 4)
            gemm_evac(dve, "wo", 8, T, add_to_h(dve, "wo"))
            norm_dve(dve, "mem", lambda k: mraw[:, k, :], lambda k: mT[:, k, :], lambda k: vcol("g_mem", k), MEM, m_rs)
            norm_dve(dve, "x", lambda k: hT[:, k, :], lambda k: U(k), lambda k: vcol("g_cross", k), T, x_rs)
            with loop(dve, 4) as i:
                x_dve(dve, i)
            dve.wait_ge(S("x_o_evac"), 16)
            dve.sem_inc(S("xo_evac"), 4)
            gemm_evac(dve, "xo", 8, T, add_to_h(dve, "xo"))
            norm_dve(dve, "mlp", lambda k: hT[:, k, :], lambda k: U(k), lambda k: vcol("g_mlp", k), T, f_rs)
            dve.wait_ge(S("xo_evac"), 20)
            dve.sem_inc(S("dn_evac"), 4)
            with loop(dve, 4) as g:
                mlp_dve(dve, g)
            norm_dve(dve, "fin", lambda k: hT[:, k, :], lambda k: hT[:, k, :], lambda k: vcol("g_final", k), T, f_rs)
            dve.wait_ge(S("proj_evac"), PROJ * UNITS + 1)
            o = VEC["ada_b"][0]
            dve.tensor_tensor(ada[:, :], ada[:, :], vec[:, o:o + 24], ALU.add).then_inc(S("ada_ready"), 1)
            dve.wait_ge(S("ada_ready"), 1)
            o = VEC["norm_pre"][0]
            dve.scalar_tensor_tensor(gpre[:, :], ada[:, 8:16], 1.0, vec[:, o:o + 8], ALU.add, ALU.mult).then_inc(S("gpre_ready"), 1)
            dve.wait_ge(S("gpre_ready"), 1)
            norm_dve(dve, "pre", lambda k: hT[:, k, :], lambda k: U(k), lambda k: gpre[:, k:k + 1], T, f_rs)
            dve.wait_ge(S("mod_ready"), KC)
            swa_dve(dve)
            gla_dve(dve, BETWEEN)
            dve.wait_ge(S("gl_y_ready"), 2)
            for q in range(44, 48):
                apply_gate(dve, q)
            rw_pre_dve(dve)
            dve.wait_ge(S("rw_mask"), 2)
            dve.wait_ge(S("rkv_mixed"), 6)
            dve.wait_ge(S("lora_mm"), 2)
            for u in range(4):
                rw_dve(dve, u)
            o = VEC["norm_post"][0]
            dve.tensor_tensor(gpost[:, :], ada[:, 16:24], vec[:, o:o + 8], ALU.mult).then_inc(S("gpost_ready"), 1)
            dve.wait_ge(S("gpost_ready"), 1)
            norm_dve(dve, "post", U, U, lambda k: gpost[:, k:k + 1], T, f_rs)

        @block.gpsimd
        def _(pool):
            with loop(pool, 4) as j:
                sb_pool(pool, j)
            pool.wait_ge(S("sb_y_ready"), 4)
            pool.dma_start(mraw, memT_d).then_inc(S("mem_in"), 16)
            pool.wait_ge(S("mod_ready"), KC)
            pool.dma_start(sbias.rearrange("p h k -> p (h k)"), bias_d).then_inc(S("bias_in"), 16)
            pool.wait_ge(S("p2_evac"), 10)
            pool.dma_start(akx[0:64, :], ak[64:128, :]).then_inc(S("akx_in"), 16)
            pool.dma_start(akx[64:128, :], ak[0:64, :]).then_inc(S("akx_in"), 16)
            pool.wait_ge(S("sw_o_evac"), 16)
            pool.dma_start(g_lora, lora_d[:, T:T + 256]).then_inc(S("glora_in"), 16)
            pool.memset(rkv[:, :, 0:PAD], 0.0).then_inc(S("rkv_pad"), 1)
            for l in range(1, LEVELS):
                n = 2 ** (l - 1)
                pool.wait_ge(S("gl_exp"), l)
                for h, src in ((1, gq), (0, gk)):
                    d4 = lv[:, l % 2, :].rearrange("p (m h s) -> p m h s", h=2, s=n)[:, :, h, :]
                    pool.tensor_tensor(d4, d4, src.rearrange("p (m h s) -> p m h s", h=2, s=n)[:, :, h, :], ALU.mult)\
                        .then_inc(S("gl_level"), 1)
            rw_pre_pool(pool)
            for u in range(4):
                rw_pool(pool, u)
            for k in range(KC):
                pool.wait_ge(*norm_out("post", k + 1))
                pool.tensor_tensor(hT[:, k, :], hT[:, k, :], U(k), ALU.add).then_inc(S("final_ready"), 1)

        @block.scalar
        def _(act):
            act.wait_ge(S("vec_in"), 16)
            act.activation(cact[:, :], vec[:, VEC["c"][0]:VEC["c"][0] + 8], ACT.Silu).then_inc(S("cact_ready"), 1)
            act.wait_ge(S("lam_sum"), 1)
            act.activation(lamt[:, 2:4], bank(0)[:, 0:2], ACT.Exp).then_inc(S("lam_exp"), 1)
            act.wait_ge(S("ang_ready"), 1)
            act.activation(sinT, ang, ACT.Sin).then_inc(S("rope_tables"), 1)
            act.activation(cosT, posf, ACT.Sin, bias=cst("half_pi"), scale=-1.0).then_inc(S("rope_tables"), 1)
            act.wait_ge(S("const_in"), 16)
            norm_act(act, "mix", lambda k: hT[:, k, :], T, n_sq, n_rs, lambda k: [("x_in", 16 * KC)])
            act.wait_ge(S("lam_exp"), 1)
            act.sem_inc(S("proj_evac"), 1)
            for c in range(PROJ):
                proj_act(act, 0, c)
            with loop(act, 4) as i:
                da_act(act, i)
            with loop(act, 3) as j:
                sb_act(act, j, False)
            sb_act(act, 3, True)
            norm_act(act, "mem", lambda k: mraw[:, k, :], MEM, m_sq, m_rs, lambda k: [("mem_in", 16)])
            act.wait_ge(S("norm_sq_summed"), KC * NORMS["mem"] + KC)

            def take_k(i, j, h, b):
                act.activation(dyn(KcT, NS * i + j, 1).rearrange("p o t -> p (o t)"), b, ACT.Copy).then_inc(S("xk_evac"), 1)

            def take_v(i, j, h, b):
                act.activation(Vc[:, :, bass.ds((NS * i + j) * P, P)], b.rearrange("p (t f) -> p t f", t=2),
                               ACT.Copy).then_inc(S("xv_evac"), 1)

            def take_q(i, j, h, b):
                act.activation(dyn(qcT, NS * i + j, 1, h * HALF, (h + 1) * HALF).rearrange("p o t -> p (o t)"), b,
                               ACT.Copy, scale=1.0 / 16).then_inc(S("xq_evac"), 1)

            act.wait_ge(S("wo_evac"), 20)
            act.sem_inc(S("xk_evac"), 4)
            gemm_evac(act, "xk", 8, MEM, take_k)
            norm_act(act, "x", lambda k: hT[:, k, :], T, x_sq, x_rs, lambda k: [])
            act.wait_ge(S("xk_evac"), 12)
            act.sem_inc(S("xv_evac"), 4)
            gemm_evac(act, "xv", 8, MEM, take_v)
            act.wait_ge(S("xv_evac"), 12)
            act.sem_inc(S("xq_evac"), 4)
            gemm_evac(act, "xq", 8, T, take_q)
            act.wait_ge(S("xq_evac"), 20)
            with loop(act, 4) as i:
                x_act(act, i)
            norm_act(act, "mlp", lambda k: hT[:, k, :], T, f_sq, f_rs, lambda k: [("xo_evac", 4 + 2 * (k + 1))])
            with loop(act, 4) as g:
                mlp_act(act, g)
            norm_act(act, "fin", lambda k: hT[:, k, :], T, f_sq, f_rs, lambda k: [("dn_evac", 4 + 48 + 2 * (k + 1))])
            norm_act(act, "pre", lambda k: hT[:, k, :], T, f_sq, f_rs, lambda k: [("norm_out", KC * NORMS["fin"] + k + 1)])
            act.wait_ge(S("ada_ready"), 1)
            for k in range(KC):
                act.wait_ge(*norm_out("pre", k + 1))
                act.activation(U(k), U(k), ACT.Identity, bias=ada[:, k:k + 1]).then_inc(S("mod_ready"), 1)
            for q in range(12):
                p2_act(act, q)
            swa_act(act)
            act.wait_ge(S("sw_o_evac"), 16)
            gla_act(act, BETWEEN)
            for q in range(44, 48):
                p2_act(act, q)
            rw_pre_act(act)
            for u in range(4):
                rw_act(act, u)

            def take_z(i, j, h, b):
                act.activation(dyn(uT, NS * i + j, 1, PAD + h * HALF, PAD + (h + 1) * HALF).rearrange("p o t -> p (o t)"), b,
                               ACT.Copy).then_inc(S("out2_evac"), 1)

            act.wait_ge(*rw("dve", "gated", 3))
            act.sem_inc(S("out2_evac"), 4)
            gemm_evac(act, "out2", 8, T, take_z)
            act.wait_ge(S("out2_evac"), 20)
            norm_act(act, "post", U, T, f_sq, f_rs, lambda k: [])

        @block.tensor
        def _(pe):
            pe.sem_inc(S("weight_free"), CREDIT)
            pe.wait_ge(S("const_in"), 16)
            pe.wait_ge(S("lam_prod"), 2)
            pe.matmul(bank(0)[:, 0:2], cst("ones"), lamt[:, 0:2], start=True, stop=True).then_inc(S("lam_sum"), 1)
            norm_pe(pe, "mix", T, n_sq)
            pe.wait_ge(S("cact_ready"), 1)
            pe.wait_ge(*norm_out("mix", KC))
            for c in range(PROJ):
                proj_pe(pe, 0, c)
            with loop(pe, 4) as i:
                da_pe(pe, i)
            with loop(pe, 3) as j:
                sb_pe(pe, j, False)
            sb_pe(pe, 3, True)
            pe.wait_ge(S("da_y_ready"), 4)
            pe.wait_ge(S("sb_y_ready"), 4)
            gemm_pe(pe, "wo", UNIT_PANELS, 8, lambda k, lo, hi: yT[:, k, lo:hi])
            norm_pe(pe, "mem", MEM, m_sq)
            pe.wait_ge(*norm_out("mem", KC))
            gemm_pe(pe, "xk", UNIT_PANELS + 8, 8, lambda k, lo, hi: mT[:, k, lo:hi], width=MEM)
            norm_pe(pe, "x", T, x_sq)
            gemm_pe(pe, "xv", UNIT_PANELS + 16, 8, lambda k, lo, hi: mT[:, k, lo:hi], width=MEM, token_major=True)
            pe.wait_ge(*norm_out("x", KC))
            gemm_pe(pe, "xq", UNIT_PANELS + 24, 8, lambda k, lo, hi: U(k, lo, hi))
            with loop(pe, 4) as i:
                x_pe(pe, i)
            pe.wait_ge(S("x_o_evac"), 16)
            gemm_pe(pe, "xo", UNIT_PANELS + 32, 8, lambda k, lo, hi: yT[:, k, lo:hi])
            norm_pe(pe, "mlp", T, f_sq)
            pe.wait_ge(*norm_out("mlp", KC))
            with loop(pe, 4) as g:
                mlp_pe(pe, g)
            norm_pe(pe, "fin", T, f_sq)
            norm_pe(pe, "pre", T, f_sq)
            pe.wait_ge(S("mod_ready"), KC)
            for q in range(12):
                p2_pe(pe, q)
            swa_pe(pe)
            gla_pe(pe, BETWEEN)
            for q in range(44, 48):
                p2_pe(pe, q)
            rw_pre_pe(pe)
            pe.wait_ge(S("lora_out"), 4)
            pe.wait_ge(S("rkv_mixed"), 6)
            pe.wait_ge(S("p2_evac"), 48)
            for u in range(4):
                rw_pe(pe, u)
            pe.wait_ge(*rw("dve", "gated", 3))
            gemm_pe(pe, "out2", G2 + 24, 8, lambda k, lo, hi: yT[:, k, lo:hi])
            norm_pe(pe, "post", T, f_sq)


def columns(v):
    v = np.asarray(v).reshape(-1)
    return v.reshape(-1, P).T


def panels(w, starts):
    w = np.asarray(w).reshape(KC, P, -1)
    return [w[:, :, s:s + P].transpose(1, 0, 2).reshape(P, KC * P) for s in starts]


def lay_out(inputs):
    g = {k: np.asarray(v) for k, v in inputs.items()}
    vec = {}
    for name, key in [("g_mix", "g_mix"), ("g_cross", "g_cross"), ("g_mem", "g_mem"), ("g_mlp", "g_mlp"),
                      ("g_final", "g_final"), ("norm_pre", "norm_pre_2"), ("norm_post", "norm_post_2"),
                      ("g_subln", "g_subln"), ("c", "c_2"), ("ada_b", "ada_b_2"), ("mu_w", "rwkv_mu_w_2"),
                      ("mu_a", "rwkv_mu_a_2"), ("mu_rkv", "rwkv_mu_rkv_2"), ("w0", "rwkv_w0_2"), ("a0", "rwkv_a0_2"),
                      ("k_k", "rwkv_k_k_2"), ("k_a", "rwkv_k_a_2"), ("r_k", "rwkv_r_k_2"), ("ln_w", "rwkv_ln_w_2"),
                      ("ln_b", "rwkv_ln_b_2"), ("gk_b", "gla_gk_b_2")]:
        vec[name] = columns(g[key])
    n = g["gla_norm_w_2"].reshape(-1)
    vec["gla_norm"] = np.concatenate([n, n])[:, None]
    lam = np.zeros((P, 4), np.float32)
    for x, key in enumerate(["lambda_q1", "lambda_k1", "lambda_q2", "lambda_k2"]):
        lam[:64, x] = g[key].reshape(-1)
    vec["lam"] = lam
    order = [4 * x + 2 * c + par for x in range(2) for par in range(2) for c in range(2)]
    vec["sinks"] = np.broadcast_to(g["attn_sinks_2"].reshape(-1)[order][None, :], (P, 8))
    wa = np.concatenate([g["rwkv_w1_2"][0], g["rwkv_a1_2"][0]], axis=1)
    gk2 = np.concatenate([g["gla_gk2_2"][0], np.zeros((P - 16, P), np.float32)], axis=0)
    lora = np.concatenate([wa.reshape(KC, P, P).transpose(1, 0, 2).reshape(P, -1),
                           g["gla_gk1_2"][0].reshape(KC, P, 16).transpose(1, 0, 2).reshape(P, -1), gk2,
                           np.concatenate([g["rwkv_w2_2"][0], g["rwkv_a2_2"][0]], axis=0)], axis=1)
    vec_a = np.concatenate([vec[name] for name in VEC], axis=1)
    win = g["w_in"][0]
    adaw = g["ada_w_2"][0]
    w = []
    for u in range(UNITS):
        if u < 4:
            w += panels(win, [u * P, 512 + u * P, 1024 + u * P])
        else:
            w += panels(win, [1536 + (u - 4) * P, 2048 + (u - 4) * P, 2560 + (u - 4) * P])
        w += panels(adaw, [(3 * u + s) * P for s in range(3)])
    every = range(0, D, P)
    w += panels(g["w_out"][0], every)
    w += panels(g["w_xkv"][0], range(0, 2 * D, P))
    w += panels(g["w_xq"][0], every)
    w += panels(g["w_xo"][0], every)
    for f in range(4):
        w += panels(g["w_up"][0], range(f * D, (f + 1) * D, P))
        w += panels(g["w_down"][0][f * D:(f + 1) * D], every)
    w2 = g["w_in_2"][0]
    w += panels(w2, [P * b for b in SECOND_ORDER])
    w += panels(g["w_out_2"][0], every)

    def feature_major(a):
        return a.T.reshape(KC, P, -1).transpose(1, 0, 2)

    return {
        "xT": np.ascontiguousarray(feature_major(g["x"][0])),
        "memT": np.ascontiguousarray(feature_major(g["mem"][0])),
        "pos": np.ascontiguousarray(np.broadcast_to(g["positions"].reshape(1, T), (P, T))),
        "vec": np.ascontiguousarray(vec_a),
        "const": constants(),
        "bias": window_bias(),
        "lora": np.ascontiguousarray(lora),
        "w": np.ascontiguousarray(np.stack(w)),
    }


SECOND_ORDER = [0, 1, 2, 3, 4, 5, 18, 19, 20, 21, 10, 11, 12, 13, 14, 15, 6, 7, 8, 9, 16, 17, 22, 23]


def kernel(**inputs):
    import concourse.bacc as bacc
    from concourse.bass_utils import run_bass_kernel_spmd

    arrays = lay_out(inputs)
    nc = bacc.Bacc("TRN2", target_bir_lowering=False, num_devices=1)
    args = [nc.dram_tensor("in_" + n, a.shape, mybir.dt.from_np(a.dtype), kind="ExternalInput").ap() for n, a in arrays.items()]
    args.append(nc.dram_tensor("out_0", (P, KC, T), mybir.dt.float32, kind="ExternalOutput").ap())
    program(nc, *args)
    r = run_bass_kernel_spmd(nc, [{"in_" + n: a for n, a in arrays.items()}], core_ids=[0])
    o = r.results[0]["out_0"]
    return o.transpose(1, 0, 2).reshape(D, T).T.reshape(1, T, D)
```

```python
import concourse.bass as bass
from concourse import mybir
from concourse.alu_op_type import AluOpType as ALU
from contextlib import ExitStack
import numpy as np

P = 128
D = 1024
T = 1024
KC = D // P
NT = T // P
HALF = 512
MEM = 256
EPS = 1e-6
NEG = -1e30
LAM_INIT = 0.2
UNITS = 8
CREDIT = 2
PAD = 8

VEC = {}
for _name, _n in [("g_mix", 8), ("g_cross", 8), ("g_mem", 8), ("g_mlp", 8), ("g_final", 8),
                  ("norm_pre", 8), ("norm_post", 8), ("g_subln", 1), ("c", 8), ("ada_b", 24),
                  ("mu_w", 8), ("mu_a", 8), ("mu_rkv", 6), ("w0", 2), ("a0", 2), ("k_k", 2), ("k_a", 2),
                  ("r_k", 2), ("ln_w", 2), ("ln_b", 2), ("gk_b", 1), ("gla_norm", 1),
                  ("lam", 4), ("sinks", 8)]:
    VEC[_name] = (sum(n for _, n in VEC.values()), _n)
NVEC = sum(n for _, n in VEC.values())

CONST = {}
for _name, _n in [("ident", 128), ("ones", 128), ("blk64", 128), ("neg_tri", 128), ("neg_ones", 128),
                  ("rot", 128), ("da_mask", 128), ("sb_mask", 128), ("sb_strict", 128),
                  ("level", 7 * 128), ("strict64", 128), ("incl64", 128), ("first_low", 128), ("gla_state", 256), ("ident64", 64),
                  ("inv_freq", 1), ("eps", 1), ("half_pi", 1), ("zero", 1), ("eps5", 1), ("eps_ln", 1)]:
    CONST[_name] = (sum(n for _, n in CONST.values()), _n)
NCONST = sum(n for _, n in CONST.values())


def constants():
    i = np.arange(P)
    c = np.zeros((P, NCONST), np.float32)

    def put(name, a):
        o, n = CONST[name]
        c[:, o:o + n] = a

    put("ident", np.eye(P))
    put("ones", 1.0)
    put("blk64", (i[:, None] // 64) == (i[None, :] // 64))
    put("neg_tri", -1.0 * (i[:, None] >= i[None, :]))
    put("neg_ones", -1.0)
    rot = np.zeros((P, P))
    for b in (0, 64):
        for m in range(8):
            rot[b + m + 8, b + m] = -1.0
            rot[b + m, b + m + 8] = 1.0
    put("rot", rot)
    put("da_mask", NEG * (i[None, :] > i[:, None]))
    put("sb_mask", NEG * (i[:, None] >= i[None, :]))
    put("sb_strict", i[:, None] < i[None, :])
    f = np.zeros(P, np.float32)
    for b in (0, 64):
        for m in range(16):
            f[b + m] = np.float32(500000.0) ** np.float32(-(2.0 * (m % 8)) / 16.0)
    j, t = i[:, None], i[None, :]
    put("level", np.concatenate([(j >> (l + 1) == t >> (l + 1)) & (j >> l & 1 == 0) & (t >> l & 1 == 1)
                                 for l in range(7)], axis=1))
    put("strict64", (j // 64 == t // 64) & (j < t))
    put("incl64", (j // 64 == t // 64) & (j <= t))
    put("first_low", (j >> 1 == t >> 1) & (j & 1 == 1) & (t & 1 == 0))
    put("ident64", i[:, None] % 64 == np.arange(64)[None, :])
    put("gla_state", (i[:, None] // 32) == (np.arange(256)[None, :] // 64))
    put("inv_freq", f[:, None])
    put("eps", EPS)
    put("half_pi", np.pi / 2)
    put("eps5", 1e-5)
    put("eps_ln", 64e-5)
    return c


def window_bias():
    q, k = np.arange(P)[:, None], np.arange(2 * P)[None, :]
    dist = q - k + P
    b = np.zeros((P, 8, 2 * P), np.float32)
    for g in range(2):
        for par in range(2):
            for c in range(2):
                head = 4 * g + 2 * c + par
                slope = np.float32(2.0) ** np.float32(-8.0 * (head + 1) / 8)
                b[:, 4 * g + 2 * par + c] = np.where((dist >= 0) & (dist < P), -slope * dist.astype(np.float32), NEG)
    return b.reshape(P, 8 * 2 * P)


def program(nc, xT_d, memT_d, pos_d, vec_d, const_d, bias_d, lora_d, w_d, out_d):
    F = mybir.dt.float32
    R = mybir.dt.float32r
    I32 = mybir.dt.int32
    ACT = mybir.ActivationFunctionType
    AX = mybir.AxisListType.X
    ctx = ExitStack()
    with ctx:
        def sb(name, shape, dt=F):
            return ctx.enter_context(nc.sbuf_tensor(name, shape, dt))

        def with_rounded(name, shape):
            n = 4 * int(np.prod(shape[1:]))
            t = ctx.enter_context(nc.sbuf_tensor(name, shape, F, align_bytes=64))
            at = nc.sbuf_base - n
            return t, nc.alloc_sbuf_tensor_at(name + "_r", shape, R, offset=at)

        sems = {}

        def S(name):
            if name not in sems:
                sems[name] = ctx.enter_context(nc.semaphore(name))
            return sems[name]

        PS = ctx.enter_context(nc.psum_tensor("PS", [P, 8 * HALF], F))

        def bank(b, n=1):
            return PS[:, b * HALF:(b + n) * HALF]

        const = sb("const", [P, NCONST])
        vec = sb("vec", [P, NVEC])

        def cst(name):
            o, n = CONST[name]
            return const[:, o:o + n]

        def vcol(name, j=0):
            return vec[:, VEC[name][0] + j:VEC[name][0] + j + 1]

        h_all, h_r = with_rounded("h", [P, KC, PAD + T])
        u_all, u_r = with_rounded("u", [P, KC, PAD + T])
        y_all, y_r = with_rounded("y", [P, KC, T])
        hT, uT, yT = h_all[:, :, PAD:PAD + T], u_all[:, :, :], y_all[:, :, :]
        NS = 4
        w_raw = sb("w_raw", [P, 2, D])
        w_hi, w_lo = sb("w_hi", [P, 2, D], R), sb("w_lo", [P, 2, D], R)
        small = sb("small", [P, 64])
        ada = sb("ada", [P, 24])
        pos_i = sb("pos_i", [P, T], I32)
        pos_f = pos_i[:, :].bitcast(F)
        arena_t, arena_rt = with_rounded("arena", [P, 17472])
        arena, arena_r = arena_t[:, :], arena_rt[:, :]

        def U(k, lo=0, hi=T):
            return uT[:, k, PAD + lo:PAD + hi]

        def pair(high, low):
            return lambda k, lo, hi: (high(k, lo, hi), low(k, lo, hi))

        def in_u(k, lo, hi):
            return u_r[:, k, PAD + lo:PAD + hi]

        def in_h(k, lo, hi):
            return h_r[:, k, PAD + lo:PAD + hi]

        def in_y(k, lo, hi):
            return y_r[:, k, lo:hi]

        def product(pe, out, a, b, start, stop):
            first = pe.matmul(out, a[0], b[0], start=start, stop=False)
            pe.matmul(out, a[0], b[1], start=False, stop=False)
            return first, pe.matmul(out, a[1], b[0], start=False, stop=stop)

        def high(e, out, x):
            return e.activation(out, x, ACT.Copy) if e.engine == mybir.EngineType.Activation else e.tensor_copy(out, x)

        def low(e, out, x, hi_part):
            return e.tensor_tensor(out, x, hi_part.bitcast(F), ALU.subtract)

        class Arena:

            def __init__(self):
                self.at = 0

            def take(self, n):
                self.at += n
                assert self.at <= 17472, self.at
                return arena[:, self.at - n:self.at]

        def W(g, k):
            return w_hi[:, g % 2, k * P:(k + 1) * P], w_lo[:, g % 2, k * P:(k + 1) * P]


        w_in = [S("w_in0"), S("w_in1")]
        UNIT_PANELS, PANELS = 6 * UNITS, w_d.shape[0]

        def panel_in(pe, g):
            pe.wait_ge(S("w_split"), g + (1 + CREDIT))

        def split_panel(pool, two, x):
            pool.wait_ge(w_in[x], 16 * two + 16)
            pool.wait_ge(S("weight_free"), 2 * two + (x + CREDIT))
            pool.tensor_tensor(w_hi[:, x, :], w_raw[:, x, :], cst("ones")[:, 0:1].broadcast_to([P, D]), ALU.mult)\
                .then_inc(S("w_high"), 1)
            pool.wait_ge(S("w_high"), 2 * two + (x + 1))
            low(pool, w_lo[:, x, :], w_raw[:, x, :], w_hi[:, x, :]).then_inc(S("w_split"), 1)

        SMALL_C, SMALL_GK, SMALL_WA = 1, 2, 4

        def loop(e, n):
            return e.Fori(0, n)

        NB = 6 * HALF
        NORMS = {n: m for m, n in enumerate(["mix", "mem", "x", "mlp", "fin", "pre", "post"])}

        def norm_out(n, k):
            return S("norm_out"), KC * NORMS[n] + k

        def norm_act(act, n, src, width, sq, rs, ready):
            m = NORMS[n]
            for k in range(KC):
                for name, v in ready(k):
                    act.wait_ge(S(name), v)
                if k >= sq.shape[1]:
                    act.wait_ge(S("norm_sq_summed"), KC * m + k + 1 - sq.shape[1])
                act.activation(sq[:, k % sq.shape[1], :width], src(k), ACT.Square).then_inc(S("norm_sq_ready"), 1)
            act.wait_ge(S("norm_sq_summed"), KC * m + KC)
            act.activation(rs[:, :width], PS[:, NB:NB + width], ACT.Sqrt, bias=cst("eps"),
                           scale=1.0 / D).then_inc(S("norm_root"), 1)

        def norm_pe(pe, n, width, sq):
            m = NORMS[n]
            for k in range(KC):
                pe.wait_ge(S("norm_sq_ready"), KC * m + k + 1)
                for h in range(0, width, HALF):
                    w = min(HALF, width)
                    mm = pe.matmul(PS[:, NB + h:NB + h + w], cst("ones"), sq[:, k % sq.shape[1], h:h + w],
                                  start=(k == 0), stop=(k == KC - 1))
                mm.then_inc(S("norm_sq_summed"), 1)

        def norm_dve(dve, n, src, dst, gain, width, rs):
            m = NORMS[n]
            dve.wait_ge(S("norm_root"), m + 1)
            dve.reciprocal(rs[:, :width], rs[:, :width]).then_inc(S("norm_rstd"), 1)
            dve.wait_ge(S("norm_rstd"), m + 1)
            for k in range(KC):
                dve.scalar_tensor_tensor(dst(k), src(k), gain(k), rs[:, :width], ALU.mult, ALU.mult)\
                   .then_inc(S("norm_out"), 1)

        def chunk_product(pe, g, b, x, h, token_major, width=T, first_half=True, ready=None):
            w = min(width, HALF)
            for t in range(w // P if token_major else 1):
                for k in range(KC):
                    if ready is not None:
                        ready(k)
                    if token_major:
                        lo = h * HALF + t * P
                        f, m = product(pe, b[:, t * P:(t + 1) * P], x(k, lo, lo + P), W(g, k), k == 0, k == KC - 1)
                    else:
                        f, m = product(pe, b[:, :w], W(g, k), x(k, h * HALF, h * HALF + w), k == 0, k == KC - 1)
                    if h == 0 and t == 0 and k == 0:
                        f.then_inc(S("weight_free"), 1)
            return m

        def panel_product(pe, n, g, banks, evac_from, x, token_major, width, ready=None):
            for h in range(max(1, width // HALF)):
                pe.wait_ge(S(n + "_evac"), evac_from + h)
                chunk_product(pe, g, banks[h], x, h, token_major, width, ready=ready if h == 0 else None)\
                    .then_inc(S(n + "_mm"), 1)

        def gemm_banks(j, halves):
            return [bank((halves * j + h) % 4) for h in range(halves)]

        def gemm_pe(pe, n, g0, count, x, operand, token_major=False, width=T):
            def chunk_split(k):
                pe.wait_ge(S("split_low"), KC * SPLITS[operand] + k + 1)

            halves = max(1, width // HALF)
            with loop(pe, count // NS) as i:
                for j in range(NS):
                    panel_in(pe, NS * i + (g0 + j))
                    panel_product(pe, n, g0 + j, gemm_banks(j, halves), halves * (NS * i + j) + 1, x, token_major, width,
                                  ready=chunk_split if j == 0 else None)

        def gemm_evac(e, n, count, width, one, done=0):
            halves = max(1, width // HALF)
            with loop(e, count // NS) as i:
                for j in range(NS):
                    for h in range(halves):
                        e.wait_ge(S(n + "_mm"), halves * (NS * i + j + done) + h + 1)
                        one(i, j, h, gemm_banks(j, halves)[h][:, :min(width, HALF)])

        def add_to_h(dve, n):
            def one(i, j, h, b):
                dst = hT[:, bass.ds(NS * i + j, 1), h * HALF:(h + 1) * HALF].rearrange("p o t -> p (o t)")
                dve.tensor_tensor(dst, dst, b, ALU.add).then_inc(S(n + "_evac"), 1)
            return one

        ar = Arena()
        raw = ar.take(6 * HALF).rearrange("p (c t) -> p c t", c=6)
        qh, kh = ar.take(T), ar.take(T)
        Vh = ar.take(T).rearrange("p (t f) -> p t f", t=NT)
        cosT, sinT = ar.take(T), ar.take(T)
        at_da = ar.at
        Pr = ar.take(4 * T).rearrange("p (b c t) -> p b c t", b=2, c=2)
        wgt = ar.take(2 * T).rearrange("p (b t) -> p b t", b=2)
        wgtT = ar.take(T)
        oT, osq = ar.take(T), ar.take(T)
        tmp = Pr[:, 0, 0, :]
        n_sq = arena[:, at_da:at_da + 2 * T].rearrange("p (b t) -> p b t", b=2)
        n_rs = arena[:, at_da + 2 * T:at_da + 3 * T]
        ang, turns, posf = (arena[:, at_da + (3 + m) * T:at_da + (4 + m) * T] for m in range(3))
        nm = sb("nm", [P, 16])
        el = sb("el", [P, 16])
        er = sb("er", [P, 16])
        lamt = sb("lamt", [P, 8])
        gsub = sb("gsub", [P, 1])
        cact = sb("cact", [P, KC])
        c_hi, c_lo = sb("c_hi", [P, KC, 2], R), sb("c_lo", [P, KC, 2], R)
        c_twice = cact[:, :].unsqueeze(2).broadcast_to([P, KC, 2])

        CHUNKS = [("q", 0), ("q", 1), ("ada", 0), ("k", 0), ("k", 1), ("ada", 1), ("v", 0), ("v", 1), ("ada", 2)]
        PROJ = len(CHUNKS)
        PANEL_OF = {"q": 0, "k": 2, "v": 4}
        u_mix = pair(in_u, in_h)

        def proj_pe(pe, u, c):
            pe.wait_ge(S("proj_evac"), PROJ * u + max(1, c))
            what, h = CHUNKS[c]
            b = bank(c % 2)
            if what == "ada":
                panel_in(pe, 6 * u + (2 * h + 1))
                for k in range(KC):
                    f, m = product(pe, b[:, 0:2], W(1, k), (c_hi[:, k, :], c_lo[:, k, :]), k == 0, k == KC - 1)
                    if k == 0:
                        f.then_inc(S("weight_free"), 1)
            else:
                if h == 0:
                    panel_in(pe, 6 * u + PANEL_OF[what])
                m = chunk_product(pe, 0, b, u_mix, h, what == "v")
            m.then_inc(S("proj_mm"), 1)

        def proj_act(act, u, c):
            act.wait_ge(S("proj_mm"), PROJ * u + c + 1)
            what, h = CHUNKS[c]
            if what == "ada":
                act.activation(ada[:, bass.ds(3 * u + h, 1)] if not isinstance(u, int) else ada[:, 3 * u + h:3 * u + h + 1],
                               bank(c % 2)[:, 0:1], ACT.Copy).then_inc(S("proj_evac"), 1)
            else:
                act.activation(raw[:, PANEL_OF[what] + h, :], bank(c % 2), ACT.Copy, scale=0.125 if what == "q" else 1.0)\
                   .then_inc(S("proj_evac"), 1)

        def rounds(t):
            return t if t <= 4 else 4 + 2 * (t - 4)

        def da_pe(pe, i):
            pe.wait_ge(S("proj_evac"), PROJ * i + 6)
            for x in range(2):
                for h in range(2):
                    m = pe.matmul(bank(2 + 2 * x + h), cst("rot"), raw[:, 2 * x + h, :], start=True, stop=True)
                m.then_inc(S("rot_ready"), 1)
            pe.wait_ge(S("qk_ready"), 2 * i + 2)

            def scores(s):
                kw = (s + 1) * P
                for c in range(2):
                    if s >= 1:
                        pe.wait_ge(S("exp_done"), 16 * i + 2 * (s - 1) + c + 1)
                    r = slice(64 * c, 64 * c + 64)
                    b = bank(2 + 2 * c, 2)
                    for lo in range(0, kw, HALF):
                        hi = min(kw, lo + HALF)
                        m = pe.matmul(b[:, lo:hi], qh[r, s * P:(s + 1) * P], kh[r, lo:hi], start=True, stop=(hi < kw))
                    m = pe.matmul(b[:, kw - P:kw], cst("ident"), cst("da_mask"), start=False, stop=True)
                    m.then_inc(S("sc_ready"), 1)

            def turn(t, rd):
                if rd == 0:
                    pe.wait_ge(S("w_ready"), 8 * i + t + 1)
                if rounds(t) + rd > 0:
                    pe.wait_ge(S("tr_copied"), 12 * i + rounds(t) + rd)
                for kb in range(4 * rd, min(4 * rd + 4, t + 1)):
                    m = pe.transpose(bank(6)[:, (kb % 4) * P:(kb % 4 + 1) * P], wgt[:, t % 2, kb * P:(kb + 1) * P], cst("ident"))
                m.then_inc(S("tr_ready"), 1)

            def values(t):
                pe.wait_ge(S("tr_copied"), 12 * i + rounds(t + 1))
                if t == 0:
                    pe.wait_ge(S("v_ready"), i + 1)
                if t == 4:
                    pe.wait_ge(S("o_evac"), 2 * i + 1)
                for kb in range(t + 1):
                    m = pe.matmul(bank(7)[:, (t % 4) * P:(t % 4 + 1) * P], Vh[:, kb, :], wgtT[:, kb * P:(kb + 1) * P],
                                  start=(kb == 0), stop=(kb == t))
                m.then_inc(S("av_ready"), 1)

            for s in range(NT + 1):
                if s in (2, 4, 6):
                    proj_pe(pe, i + 1, 3 * (s // 2) - 1)
                if s >= 2:
                    values(s - 2)
                if s < NT:
                    scores(s)
                if s >= 1:
                    turn(s - 1, 0)
                if s < 6:
                    proj_pe(pe, i + 1, s + s // 2)
                if s >= 5:
                    turn(s - 1, 1)
            values(NT - 1)
            pe.wait_ge(S("osq_ready"), i + 1)
            for h in range(2):
                m = pe.matmul(bank(6 + h), cst("ones"), osq[:, h * HALF:(h + 1) * HALF], start=True, stop=True)
            m.then_inc(S("osum_ready"), 1)

        def da_act(act, i):
            act.wait_ge(S("proj_evac"), PROJ * i + 9)
            act.activation(Vh[:, :, :].rearrange("p t f -> p (t f)"), raw[:, 4:6, :].rearrange("p c t -> p (c t)"),
                           ACT.Copy).then_inc(S("v_ready"), 1)

            def exps(s):
                kw = (s + 1) * P
                for c in range(2):
                    if s >= 2:
                        act.wait_ge(S("w_ready"), 8 * i + s - 1)
                    act.wait_ge(S("nmax_ready"), 16 * i + 2 * s + c + 1)
                    act.activation(Pr[:, s % 2, c, :kw], bank(2 + 2 * c, 2)[:, :kw], ACT.Exp, bias=nm[:, 2 * s + c:2 * s + c + 1],
                                   accum_out=el[:, 2 * s + c:2 * s + c + 1]).then_inc(S("exp_done"), 1)

            def copy_turned(t, rd):
                n = min(4, t + 1 - 4 * rd) * P
                act.wait_ge(S("tr_ready"), 12 * i + rounds(t) + rd + 1)
                act.activation(wgtT[:, 4 * P * rd:4 * P * rd + n], bank(6)[:, :n], ACT.Copy).then_inc(S("tr_copied"), 1)

            def take_o(h):
                act.wait_ge(S("av_ready"), 8 * i + 4 * h + 4)
                act.activation(oT[:, h * HALF:(h + 1) * HALF], bank(7), ACT.Copy).then_inc(S("o_evac"), 1)

            for s in range(NT + 1):
                if s in (2, 4, 6):
                    proj_act(act, i + 1, 3 * (s // 2) - 1)
                if s == 5:
                    take_o(0)
                if s < NT:
                    exps(s)
                if s >= 1:
                    copy_turned(s - 1, 0)
                if s < 6:
                    if s == 0:
                        act.wait_ge(S("qk_ready"), 2 * i + 2)
                    if s == 4:
                        act.wait_ge(S("v_ready"), i + 1)
                    proj_act(act, i + 1, s + s // 2)
                if s >= 5:
                    copy_turned(s - 1, 1)
            take_o(1)
            act.wait_ge(S("o_evac"), 2 * i + 2)
            act.activation(osq, oT, ACT.Square).then_inc(S("osq_ready"), 1)
            act.wait_ge(S("osum_ready"), i + 1)
            act.activation(osq, bank(6, 2), ACT.Sqrt, bias=cst("eps"), scale=1.0 / P).then_inc(S("oroot_ready"), 1)

        def da_dve(dve, i):
            for x, dst in enumerate((qh, kh)):
                src = raw[:, 2 * x:2 * x + 2, :].rearrange("p c t -> p (c t)")
                dve.wait_ge(S("rot_ready"), 2 * i + x + 1)
                dve.tensor_tensor(dst, src, cosT, ALU.mult).then_inc(S("rope_part"), 1)
                dve.tensor_tensor(tmp, bank(2 + 2 * x, 2), sinT, ALU.mult).then_inc(S("rope_part"), 1)
                dve.wait_ge(S("rope_part"), 4 * i + 2 * x + 2)
                dve.tensor_tensor(dst, dst, tmp, ALU.add).then_inc(S("qk_ready"), 1)
                dve.wait_ge(S("qk_ready"), 2 * i + x + 1)

            def maxima(s):
                for c in range(2):
                    dve.wait_ge(S("sc_ready"), 16 * i + 2 * s + c + 1)
                    dve.reduce_max(nm[:, 2 * s + c:2 * s + c + 1], bank(2 + 2 * c, 2)[:, :(s + 1) * P], AX,
                                   negate=True).then_inc(S("nmax_ready"), 1)

            def weights(t):
                kw = (t + 1) * P
                dve.wait_ge(S("exp_done"), 16 * i + 2 * t + 2)
                dve.reciprocal(er[:, 2 * t:2 * t + 2], el[:, 2 * t:2 * t + 2]).then_inc(S("recip_ready"), 1)
                dve.wait_ge(S("recip_ready"), 8 * i + t + 1)
                dve.tensor_scalar(Pr[:, t % 2, 1, :kw], Pr[:, t % 2, 1, :kw], er[:, 2 * t + 1:2 * t + 2], lamt[:, 5:6],
                                  ALU.mult, ALU.mult).then_inc(S("w_part"), 1)
                dve.wait_ge(S("w_part"), 8 * i + t + 1)
                if t >= 2:
                    dve.wait_ge(S("tr_ready"), 12 * i + rounds(t - 1))
                dve.scalar_tensor_tensor(wgt[:, t % 2, :kw], Pr[:, t % 2, 0, :kw], er[:, 2 * t:2 * t + 1],
                                         Pr[:, t % 2, 1, :kw], ALU.mult, ALU.add).then_inc(S("w_ready"), 1)

            for s in range(NT + 1):
                if s < NT:
                    maxima(s)
                if s >= 1:
                    weights(s - 1)
            dve.wait_ge(S("oroot_ready"), i + 1)
            dve.reciprocal(osq, osq).then_inc(S("orstd_ready"), 1)
            dve.wait_ge(S("orstd_ready"), i + 1)
            dve.scalar_tensor_tensor(yT[:, bass.ds(i, 1), :].rearrange("p o t -> p (o t)"), oT, gsub[:, 0:1], osq,
                                     ALU.mult, ALU.mult).then_inc(S("da_y_ready"), 1)

        ar = Arena()
        ar.at = at_da - 2 * T
        Rs = ar.take(2 * T).rearrange("p (h t) -> p h t", h=2)
        ab = ar.take(2 * T).rearrange("p (b t) -> p b t", b=2)
        sp = ar.take(2 * T).rearrange("p (b t) -> p b t", b=2)
        Aw = ar.take(2 * T).rearrange("p (b t) -> p b t", b=2)

        def sb_block(n):
            kb = NT - 1 - n // 2
            return kb, n % 2, T - kb * P

        def pieces(lo, hi):
            return [(a, min(a + HALF, hi)) for a in range(lo, hi, HALF)]

        SB_STEP = {2: 0, 4: 1, 5: 2, 6: 3, 8: 4, 9: 5, 10: 6, 12: 7, 13: 8}

        def sb_pe(pe, j, last):
            pe.wait_ge(S("sb_qkv"), 3 * j + 3)
            for s in range(18):
                if not last and s in (5, 9, 13):
                    proj_pe(pe, j + 5, SB_STEP[s])
                if s < 16:
                    kb, hd, w = sb_block(s)
                    if s >= 2:
                        pe.wait_ge(S("sb_a"), 16 * j + s - 1)
                    r = slice(64 * hd, 64 * hd + 64)
                    for lo, hi in pieces(0, w):
                        m = pe.matmul(bank(2 + 2 * (s % 2), 2)[:, lo:hi], kh[r, kb * P:(kb + 1) * P],
                                      qh[r, kb * P + lo:kb * P + hi], start=True, stop=True)
                    m.then_inc(S("sb_z"), 1)
                if not last and s % 2 == 0 and s in SB_STEP:
                    proj_pe(pe, j + 5, SB_STEP[s])
                if 1 <= s <= 16:
                    n = s - 1
                    kb, hd, w = sb_block(n)
                    b = bank(2 + 2 * (n % 2), 2)
                    pe.wait_ge(S("sb_sp"), 16 * j + n + 1)
                    for lo, hi in pieces(0, w):
                        pe.matmul(b[:, lo:hi], cst("neg_tri"), sp[:, n % 2, lo:hi], start=False, stop=True,
                                  skip_group_check=True)
                    if n >= 2:
                        pe.wait_ge(S("sb_sum"), 14 * j + n - 1)
                        for lo, hi in pieces(0, w):
                            lo = max(lo, P)
                            pe.matmul(b[:, lo:hi], cst("neg_ones"), Rs[:, hd, kb * P + lo:kb * P + hi],
                                      start=False, stop=True, skip_group_check=True)
                    pe.matmul(b[:, :P], cst("ident"), cst("sb_mask"), start=False, stop=True,
                              skip_group_check=True).then_inc(S("sb_e"), 1)
                if s >= 2:
                    n = s - 2
                    kb, hd, w = sb_block(n)
                    pe.wait_ge(S("sb_a"), 16 * j + n + 1)
                    for lo, hi in ((kb * P, HALF), (max(kb * P, HALF), T)):
                        if lo < hi:
                            m = pe.matmul(PS[64 * hd:64 * hd + 64, 6 * HALF + lo:6 * HALF + hi], Vh[:, kb, 64 * hd:64 * hd + 64],
                                          Aw[:, n % 2, lo - kb * P:hi - kb * P], start=(n < 2 or (lo < HALF and kb == 3)),
                                          stop=(kb == 0), skip_group_check=True)
                    m.then_inc(S("sb_av"), 1)

        def sb_act(act, j, last):
            act.preload_act_table_set("natural_log_exp_and_others")
            act.wait_ge(S("proj_evac"), PROJ * (j + 4) + 9)
            for dst, c in ((qh, 0), (kh, 2), (Vh[:, :, :].rearrange("p t f -> p (t f)"), 4)):
                act.activation(dst, raw[:, c:c + 2, :].rearrange("p c t -> p (c t)"), ACT.Copy).then_inc(S("sb_qkv"), 1)
            for s in range(17):
                if not last and s in (5, 9, 13):
                    proj_act(act, j + 5, SB_STEP[s])
                if s < 16:
                    w = sb_block(s)[2]
                    act.wait_ge(S("sb_z"), 16 * j + s + 1)
                    if s >= 2:
                        act.wait_ge(S("sb_sp_raw"), 16 * j + s - 1)
                    act.activation(ab[:, s % 2, :w], bank(2 + 2 * (s % 2), 2)[:, :w], ACT.Abs).then_inc(S("sb_abs"), 1)
                    act.wait_ge(S("sb_abs"), 16 * j + s + 1)
                    act.activation(ab[:, s % 2, :w], ab[:, s % 2, :w], ACT.Exp, scale=-1.0).then_inc(S("sb_exp"), 1)
                    act.wait_ge(S("sb_exp"), 16 * j + s + 1)
                    act.activation(ab[:, s % 2, :w], ab[:, s % 2, :w], ACT.Ln, bias=1.0).then_inc(S("sb_ln"), 1)
                if s >= 1:
                    n = s - 1
                    w = sb_block(n)[2]
                    if n >= 2:
                        act.wait_ge(S("sb_av"), 16 * j + n - 1)
                    act.wait_ge(S("sb_e"), 16 * j + n + 1)
                    act.activation(Aw[:, n % 2, :w], bank(2 + 2 * (n % 2), 2)[:, :w], ACT.Exp).then_inc(S("sb_a"), 1)
                if not last and s % 2 == 0 and s in SB_STEP:
                    if s == 2:
                        act.wait_ge(S("sb_qkv"), 3 * j + 3)
                    proj_act(act, j + 5, SB_STEP[s])
            act.wait_ge(S("sb_av"), 16 * j + 16)
            act.activation(yT[:, bass.ds(j + 4, 1), :].rearrange("p o t -> p (o t)") if not isinstance(j, int) else yT[:, j + 4, :],
                           bank(6, 2), ACT.Copy).then_inc(S("sb_y_ready"), 1)

        def sb_dve(dve, j):
            for s in range(16):
                w = sb_block(s)[2]
                dve.wait_ge(S("sb_ln"), 16 * j + s + 1)
                if s >= 2:
                    dve.wait_ge(S("sb_sum"), 14 * j + s - 1)
                dve.scalar_tensor_tensor(sp[:, s % 2, :w], bank(2 + 2 * (s % 2), 2)[:, :w], 0.0, ab[:, s % 2, :w],
                                         ALU.max, ALU.add).then_inc(S("sb_sp_raw"), 1)
                dve.wait_ge(S("sb_sp_raw"), 16 * j + s + 1)
                dve.tensor_tensor(sp[:, s % 2, :P], sp[:, s % 2, :P], cst("sb_strict"), ALU.mult).then_inc(S("sb_sp"), 1)

        def sb_pool(pool, j, last):
            pool.wait_ge(S("sb_qkv"), 3 * j + 1)
            pool.sem_inc(S("sb_zeroing"), 1)
            pool.memset(Rs[:, :, :], 0.0).then_inc(S("sb_zero"), 1)
            pool.wait_ge(S("sb_zero"), j + 1)
            for n in range(14):
                kb, hd, w = sb_block(n)
                pool.wait_ge(S("sb_e"), 16 * j + n + 1)
                pool.tensor_tensor(Rs[:, hd, kb * P:], Rs[:, hd, kb * P:], sp[:, n % 2, :w], ALU.add).then_inc(S("sb_sum"), 1)
                if not last and n % 2 == 1 and n < 12:
                    x = n // 2 + 1
                    split_panel(pool, 3 * j + (15 + x // 2), x % 2)
            pool.wait_ge(S("sb_sum"), 14 * j + 14)

        ar = Arena()
        mraw = ar.take(KC * MEM).rearrange("p (k t) -> p k t", k=KC)
        mT = ar.take(KC * MEM).rearrange("p (k t) -> p k t", k=KC)
        mem_split = pair(*[lambda k, lo, hi, t=arena_r[:, x * KC * MEM:(x + 1) * KC * MEM].rearrange("p (k t) -> p k t", k=KC):
                           t[:, k, lo:hi] for x in range(2)])
        m_rs, x_rs = ar.take(MEM), pos_f
        KcT = ar.take(KC * MEM).rearrange("p (k t) -> p k t", k=KC)
        Vc = ar.take(2 * D).rearrange("p (t f) -> p t f", t=2)
        at_x = ar.at
        qcT = ar.take(KC * T).rearrange("p (k t) -> p k t", k=KC)
        x_sq = qcT
        m_sq = KcT
        ar2 = Arena()
        kx = ar2.take(2 * MEM).rearrange("p (c t) -> p c t", c=2)
        vx = ar2.take(2 * MEM).rearrange("p (t f) -> p t f", t=2)
        Px = ar2.take(4 * MEM).rearrange("p (b q t) -> p b q t", b=2, q=2)
        pT = ar2.take(2 * T).rearrange("p (t q) -> p t q", t=2)
        assert ar2.at <= 2 * KC * MEM
        qx = uT[:, 0:2, PAD:PAD + T]

        def dyn(t, k, n, lo=0, hi=None):
            return t[:, bass.ds(k, n), lo:hi]

        def x_pe(pe, i):
            pe.wait_ge(S("x_copied"), 3 * i + 3)
            for s in range(6):
                if s < 4:
                    if s >= 2:
                        pe.wait_ge(S("x_exp"), 8 * i + 2 * s - 2)
                    for q in range(2):
                        lo = (2 * s + q) * P
                        for c in range(2):
                            m = pe.matmul(bank(s % 2)[:, q * MEM:(q + 1) * MEM], qx[:, c, lo:lo + P], kx[:, c, :],
                                          start=(c == 0), stop=(c == 1))
                    m.then_inc(S("x_scores"), 1)
                if 1 <= s <= 4:
                    t = s - 1
                    if t >= 2:
                        pe.wait_ge(S("x_tcopied"), 4 * i + t - 1)
                    pe.wait_ge(S("x_probs"), 8 * i + 2 * t + 2)
                    for kt in range(2):
                        for q in range(2):
                            m = pe.transpose(bank(2 + t % 2)[:, (2 * kt + q) * P:(2 * kt + q + 1) * P],
                                             Px[:, t % 2, q, kt * P:(kt + 1) * P], cst("ident"))
                    m.then_inc(S("x_turned"), 1)
                if s in (3, 5):
                    h = s // 4
                    pe.wait_ge(S("x_tcopied"), 4 * i + 2 * h + 2)
                    if h == 1:
                        pe.wait_ge(S("x_o_evac"), 4 * i + 2)
                    for dc in range(2):
                        for kt in range(2):
                            m = pe.matmul(bank(4 + dc), vx[:, kt, dc * P:(dc + 1) * P], pT[:, kt, h * HALF:(h + 1) * HALF],
                                          start=(kt == 0), stop=(kt == 1))
                        m.then_inc(S("x_o_mm"), 1)

        def x_act(act, i):
            act.activation(qx, dyn(qcT, 2 * i, 2), ACT.Copy).then_inc(S("x_copied"), 1)
            act.activation(kx, dyn(KcT, 2 * i, 2), ACT.Copy).then_inc(S("x_copied"), 1)
            act.activation(vx, Vc[:, :, bass.ds(i * MEM, MEM)], ACT.Copy).then_inc(S("x_copied"), 1)

            def turned(t):
                act.wait_ge(S("x_turned"), 4 * i + t + 1)
                act.activation(pT[:, :, t * MEM:(t + 1) * MEM], bank(2 + t % 2).rearrange("p (k q) -> p k q", k=2),
                               ACT.Copy).then_inc(S("x_tcopied"), 1)

            for s in range(5):
                if s < 4:
                    if s >= 2:
                        act.wait_ge(S("x_turned"), 4 * i + s - 1)
                    act.wait_ge(S("x_nmax"), 4 * i + s + 1)
                    for q in range(2):
                        act.activation(Px[:, s % 2, q, :], bank(s % 2)[:, q * MEM:(q + 1) * MEM], ACT.Exp,
                                       bias=nm[:, 2 * s + q:2 * s + q + 1], accum_out=el[:, 2 * s + q:2 * s + q + 1])\
                           .then_inc(S("x_exp"), 1)
                if s >= 1:
                    turned(s - 1)
            act.wait_ge(S("x_o_mm"), 4 * i + 4)

        def x_dve(dve, i):
            for s in range(6):
                if s < 4:
                    dve.wait_ge(S("x_scores"), 4 * i + s + 1)
                    dve.reduce_max(nm[:, 2 * s:2 * s + 2], bank(s % 2).rearrange("p (q t) -> p q t", q=2), AX,
                                   negate=True).then_inc(S("x_nmax"), 1)
                if 1 <= s <= 4:
                    t = s - 1
                    dve.wait_ge(S("x_exp"), 8 * i + 2 * t + 2)
                    dve.reciprocal(er[:, 2 * t:2 * t + 2], el[:, 2 * t:2 * t + 2]).then_inc(S("x_recip"), 1)
                    dve.wait_ge(S("x_recip"), 4 * i + t + 1)
                    for q in range(2):
                        dve.tensor_scalar(Px[:, t % 2, q, :], Px[:, t % 2, q, :], er[:, 2 * t + q:2 * t + q + 1], None,
                                          ALU.mult).then_inc(S("x_probs"), 1)
                if s in (3, 5):
                    h = s // 4
                    for dc in range(2):
                        dve.wait_ge(S("x_o_mm"), 4 * i + 2 * h + dc + 1)
                        dve.tensor_copy(yT[:, bass.ds(2 * i + dc, 1), h * HALF:(h + 1) * HALF].rearrange("p o t -> p (o t)"),
                                        bank(4 + dc)).then_inc(S("x_o_evac"), 1)

        ar = Arena()
        ul = ar.take(KC * T).rearrange("p (k t) -> p k t", k=KC)
        hid = ar.take(KC * T).rearrange("p (k t) -> p k t", k=KC)
        rl = [t[:, x * HALF:(x + 1) * HALF] for t in (ar.take(T), pos_f) for x in range(2)]
        ul_r = arena_r[:, 0:KC * T].rearrange("p (k t) -> p k t", k=KC)
        hid_r = arena_r[:, KC * T:2 * KC * T].rearrange("p (k t) -> p k t", k=KC)
        f_sq, f_rs = hid, arena[:, 2 * KC * T:2 * KC * T + T]
        u_mlp = pair(in_u, lambda k, lo, hi: ul_r[:, k, lo:hi])
        x_hid = pair(in_y, lambda k, lo, hi: hid_r[:, k, lo:hi])

        def mlp_pe(pe, g):
            for q in range(32):
                p, h = q // 2, q % 2
                if h == 0:
                    panel_in(pe, 16 * g + (88 + p))
                if q < 4 or q >= 20:
                    pe.wait_ge(S("dn_evac"), 16 * g + (q if q < 4 else q - 16) + 1)
                else:
                    pe.wait_ge(S("relu_done"), 16 * g + q - 3)
                ready = (lambda k: pe.wait_ge(S("hid_split"), 16 * g + 2 * k + 2)) if q == 16 else None
                chunk_product(pe, p, bank(q % 4), u_mlp if q < 16 else x_hid, h, False, ready=ready).then_inc(S("mlp_mm"), 1)

        def mlp_act(act, g):
            for q in range(17):
                if q < 16:
                    act.wait_ge(S("mlp_mm"), 32 * g + q + 1)
                    if q >= 4:
                        act.wait_ge(S("hid_ready"), 16 * g + q - 3)
                    act.activation(rl[q % 4], bank(q % 4), ACT.Relu).then_inc(S("relu_done"), 1)
                if q >= 1:
                    c, cols = (q - 1) // 2, slice((q - 1) % 2 * HALF, ((q - 1) % 2 + 1) * HALF)
                    act.wait_ge(S("hid_ready"), 16 * g + q)
                    high(act, y_r[:, c, cols], hid[:, c, cols]).then_inc(S("hid_high"), 1)

        def mlp_dve(dve, g):
            for q in range(17):
                if q < 16:
                    dve.wait_ge(S("relu_done"), 16 * g + q + 1)
                    dve.tensor_tensor(hid[:, q // 2, q % 2 * HALF:(q % 2 + 1) * HALF], rl[q % 4], rl[q % 4],
                                      ALU.mult).then_inc(S("hid_ready"), 1)
                if q >= 1:
                    c, cols = (q - 1) // 2, slice((q - 1) % 2 * HALF, ((q - 1) % 2 + 1) * HALF)
                    dve.wait_ge(S("hid_high"), 16 * g + q)
                    low(dve, hid_r[:, c, cols], hid[:, c, cols], y_r[:, c, cols]).then_inc(S("hid_split"), 1)
            for q in range(16):
                dve.wait_ge(S("mlp_mm"), 32 * g + 16 + q + 1)
                dst = hT[:, q // 2, q % 2 * HALF:(q % 2 + 1) * HALF]
                dve.tensor_tensor(dst, dst, bank(q % 4), ALU.add).then_inc(S("dn_evac"), 1)

        SPLITS = {n: m for m, n in enumerate(["mix", "y1", "mem", "x", "y2", "mlp", "u2", "y3"])}

        def split_act(act, n, src, hi_place, ready):
            for k in range(KC):
                act.wait_ge(*ready(k))
                high(act, hi_place(k), src(k)).then_inc(S("split_high"), 1)

        def split_dve(dve, n, src, hi_place, lo_place):
            for k in range(KC):
                dve.wait_ge(S("split_high"), KC * SPLITS[n] + k + 1)
                low(dve, lo_place(k), src(k), hi_place(k)).then_inc(S("split_low"), 1)

        def split_ready(n):
            return S("split_low"), KC * (SPLITS[n] + 1)

        def whole(place):
            return lambda k: place(k, 0, T)

        gpre = sb("gpre", [P, KC])

        G2 = 56 + UNIT_PANELS + 48
        P2_BANK = [q % 4 for q in range(12)] + [7] * 8 + [6 + q % 2 for q in range(28)]

        u_two = pair(in_h, in_u)

        def p2_pe(pe, q):
            p, h = q // 2, q % 2
            if h == 0:
                panel_in(pe, G2 + p)
            before = [x for x in range(q) if P2_BANK[x] == P2_BANK[q]]
            if before:
                pe.wait_ge(S("p2_evac"), before[-1] + 1)
            m = chunk_product(pe, G2 + p, bank(P2_BANK[q]), u_two, h, p in (5, 8, 9))
            m.then_inc(S("p2_mm"), 1)

        ar = Arena()
        rkv = arena[:, 0:6 * (PAD + T)].rearrange("p (c t) -> p c t", c=6)
        aq = ar.take(4 * T).rearrange("p (c t) -> p c t", c=4)
        ak, akx = ar.take(T), ar.take(T)
        av = ar.take(T).rearrange("p (t f) -> p t f", t=NT)
        gq, gk = ar.take(T), ar.take(T)
        gv = ar.take(2 * T).rearrange("p (t f) -> p t f", t=NT)
        at_g = ar.at
        sbias = ar.take(8 * 2 * P).rearrange("p (h k) -> p h k", h=8)
        WK = 2 * P + 4
        Sw = ar.take(8 * WK).rearrange("p (g h k) -> p g h k", g=2, h=4)
        Pw = ar.take(8 * WK).rearrange("p (g h k) -> p g h k", g=2, h=4)
        pTw = pos_f.rearrange("p (k h q) -> p k h q", k=2, h=4)

        gate = [arena[:, 6 * (PAD + T) + 256:6 * (PAD + T) + 256 + HALF], sb("gate1", [P, HALF])[:, :]]

        def p2_act(act, q):
            p, h = q // 2, q % 2
            act.wait_ge(S("p2_mm"), q + 1)
            b, cols = bank(P2_BANK[q]), slice(h * HALF, (h + 1) * HALF)
            func, scale = ACT.Copy, 1.0
            if p < 4:
                dst, scale = aq[:, p, cols], 0.125
            elif p == 4:
                dst = ak[:, cols]
            elif p == 5:
                dst = av[:, 4 * h:4 * h + 4, :].rearrange("p t f -> p (t f)")
            elif p == 6:
                dst, scale = gq[:, cols], 32 ** -0.5
            elif p == 7:
                dst = gk[:, cols]
            elif p < 10:
                dst = gv[:, 4 * h:4 * h + 4, (p - 8) * P:(p - 7) * P]
                b = b.rearrange("p (t f) -> p t f", t=4)
            elif p < 16:
                dst = rkv[:, p - 10, PAD + h * HALF:PAD + (h + 1) * HALF]
            else:
                func = ACT.Silu
                if p in (20, 21):
                    dst = yT[:, 4 + p - 20, cols]
                else:
                    dst = gate[h]
                    if gate_uses(q) >= 1:
                        act.wait_ge(S("gated"), gate_uses(q))
            act.activation(dst, b, func, scale=scale).then_inc(S("p2_evac"), 1)

        GATES = [q for q in range(32, 48) if q // 2 not in (20, 21)]

        def gate_uses(q):
            return GATES.index(q) - 1

        def apply_gate(dve, q):
            p, h = q // 2, q % 2
            c = p - 16 if p < 20 else 6 + p - 22
            dst = yT[:, c, h * HALF:(h + 1) * HALF]
            dve.wait_ge(S("p2_evac"), q + 1)
            dve.tensor_tensor(dst, dst, gate[h], ALU.mult).then_inc(S("gated"), 1)

        def window(u):
            n = u // 2
            return n, u % 2, P if n == 0 else 0

        def swa_pe(pe):
            pe.wait_ge(S("akx_in"), 32)
            pe.wait_ge(S("p2_evac"), 12)
            for s in range(18):
                if s < 16:
                    n, g, lo = window(s)
                    if s >= 2:
                        pe.wait_ge(S("sw_biased"), s - 1)
                    for c in range(2):
                        for par in range(2):
                            r = slice(64 * par, 64 * par + 64)
                            src = ak if par == g else akx
                            m = pe.matmul(bank(2 * (s % 2) + par)[:, c * 2 * P + lo:(c + 1) * 2 * P], aq[r, 2 * g + c, n * P:(n + 1) * P],
                                          src[r, (n - 1) * P + lo:(n + 1) * P], start=True, stop=True)
                    m.then_inc(S("sw_scores"), 1)
                    if s < 8:
                        p2_pe(pe, 12 + s)
                if s >= 2:
                    t = s - 2
                    n, g, lo = window(t)
                    pe.wait_ge(S("sw_tcopied"), t + 1)
                    if t >= 1:
                        pe.wait_ge(S("sw_o_evac"), t)
                    for par in range(2):
                        for kt in range(lo // P, 2):
                            m = pe.matmul(PS[64 * par:64 * par + 64, 6 * HALF:6 * HALF + 2 * P], av[:, n - 1 + kt, 64 * g:64 * g + 64],
                                          pTw[:, kt, 2 * par:2 * par + 2, :].rearrange("p c q -> p (c q)"), start=(kt == lo // P), stop=(kt == 1))
                    m.then_inc(S("sw_o_mm"), 1)
                if 1 <= s <= 16:
                    t = s - 1
                    n, g, lo = window(t)
                    if t >= 1:
                        pe.wait_ge(S("sw_tcopied"), t)
                    pe.wait_ge(S("sw_probs"), t + 1)
                    for kt in range(lo // P, 2):
                        for h in range(4):
                            m = pe.transpose(bank(4 + kt)[:, h * P:(h + 1) * P], Pw[:, g, h, kt * P:(kt + 1) * P], cst("ident"))
                    m.then_inc(S("sw_turned"), 1)

        def swa_act(act):
            for s in range(17):
                if s < 16:
                    n, g, lo = window(s)
                    if s >= 2:
                        act.wait_ge(S("sw_turned"), s - 1)
                    act.wait_ge(S("sw_nmax"), s + 1)
                    for h in range(4):
                        m = act.activation(Pw[:, g, h, lo:2 * P + 1], Sw[:, g, h, lo:2 * P + 1], ACT.Exp,
                                           bias=nm[:, 4 * g + h:4 * g + h + 1], accum_out=el[:, 4 * g + h:4 * g + h + 1])
                        m.then_inc(S("sw_exp"), 1)
                    if s < 8:
                        p2_act(act, 12 + s)
                if s >= 1:
                    t = s - 1
                    n, g, lo = window(t)
                    act.wait_ge(S("sw_turned"), t + 1)
                    act.activation(pTw[:, lo // P:2, :, :].rearrange("p k h q -> p (k h q)"), bank(4 + lo // P, 2 - lo // P),
                                   ACT.Copy).then_inc(S("sw_tcopied"), 1)

        def swa_dve(dve):
            o = VEC["sinks"][0]
            for g in range(2):
                dve.tensor_copy(Sw[:, g, :, 2 * P:2 * P + 1], vec[:, o + 4 * g:o + 4 * g + 4].unsqueeze(2)).then_inc(S("sw_sink"), 1)
            dve.wait_ge(S("sw_sink"), 2)
            dve.wait_ge(S("bias_in"), 16)
            for s in range(18):
                if s < 16:
                    n, g, lo = window(s)
                    dve.wait_ge(S("sw_scores"), s + 1)
                    if s >= 2:
                        dve.wait_ge(S("sw_exp"), 4 * (s - 1))
                    dve.tensor_tensor(Sw[:, g, :, lo:2 * P], bank(2 * (s % 2), 2).rearrange("p (h k) -> p h k", h=4)[:, :, lo:],
                                      sbias[:, 4 * g:4 * g + 4, lo:], ALU.add).then_inc(S("sw_biased"), 1)
                    dve.wait_ge(S("sw_biased"), s + 1)
                    dve.reduce_max(nm[:, 4 * g:4 * g + 4], Sw[:, g, :, lo:2 * P + 1], AX, negate=True).then_inc(S("sw_nmax"), 1)
                if 1 <= s <= 16:
                    t = s - 1
                    n, g, lo = window(t)
                    dve.wait_ge(S("sw_exp"), 4 * t + 4)
                    dve.reciprocal(er[:, 4 * g:4 * g + 4], el[:, 4 * g:4 * g + 4]).then_inc(S("sw_recip"), 1)
                    dve.wait_ge(S("sw_recip"), t + 1)
                    dve.tensor_tensor(Pw[:, g, :, lo:2 * P], Pw[:, g, :, lo:2 * P],
                                      er[:, 4 * g:4 * g + 4].unsqueeze(2).broadcast_to([P, 4, 2 * P - lo]), ALU.mult)\
                       .then_inc(S("sw_probs"), 1)
                if s >= 2:
                    t = s - 2
                    n, g, lo = window(t)
                    dve.wait_ge(S("sw_o_mm"), t + 1)
                    dve.tensor_copy(yT[:, 2 * g:2 * g + 2, n * P:(n + 1) * P], bank(6)[:, :2 * P].rearrange("p (c q) -> p c q", c=2))\
                       .then_inc(S("sw_o_evac"), 1)

        CH = T // P
        ar = Arena()
        ar.at = at_g
        gb = yT[:, 6, :]
        lv = ar.take(2 * T).rearrange("p (b t) -> p b t", b=2)
        gA = ar.take(4 * T).rearrange("p (h c t) -> p h c t", h=4, c=CH)
        g_lora = arena[:, 6 * (PAD + T):6 * (PAD + T) + 256]
        gl_hi, gl_lo = (arena_r[:, ar.at - T - x * 256:ar.at - T - x * 256 + 256] for x in range(1, 3))
        gt = gA[0:16, 0, :, :].rearrange("p c t -> p (c t)")
        gtmp, gy = gA[:, 1, :, :].rearrange("p c t -> p (c t)"), gA[:, 2, :, :].rearrange("p c t -> p (c t)")
        gS = yT[:, 4:6, :].rearrange("p a (c f) -> p (a c) f", c=4)
        g_q, g_k = lv[:, 0, :], lv[:, 1, :]
        gkt = pos_f.rearrange("p (c f) -> p c f", c=CH)
        elast = small[:, 0:CH]
        gsq = gA[:, 0:2, :, :].rearrange("p h c t -> p h (c t)")
        LEVELS = 8
        last_of = gb.rearrange("p (c t) -> p c t", c=CH)[:, :, P - 1:P]

        def gla_pe(pe, between):
            pe.wait_ge(S("small_low"), SMALL_GK)
            for h in range(2):
                for k in range(KC):
                    m = product(pe, bank(h), (gl_hi[:, 16 * k:16 * k + P], gl_lo[:, 16 * k:16 * k + P]),
                                u_two(k, h * HALF, (h + 1) * HALF), k == 0, k == KC - 1)[1]
            m.then_inc(S("gl_down"), 1)
            pe.wait_ge(S("gl_down_taken"), 1)
            for h in range(2):
                m = pe.matmul(bank(2 + h), g_lora[0:16, P:2 * P], gt[:, h * HALF:(h + 1) * HALF], start=True, stop=True)
            m.then_inc(S("gl_gate"), 1)
            for l in range(LEVELS):
                if l == 0:
                    pe.wait_ge(S("p2_evac"), 16)
                    pe.wait_ge(S("gl_lin"), 1)
                else:
                    pe.wait_ge(S("gl_level"), 2 * l)
                for half in range(2):
                    if 2 * l + half >= 1:
                        pe.wait_ge(S("gl_taken"), 4 * (2 * l + half))
                    for cc in range(4):
                        c = 4 * half + cc
                        for h in range(4):
                            a, b = (gk, gq) if l == 0 else (lv[:, l % 2, :], lv[:, l % 2, :])
                            m = pe.matmul(bank(h)[:, cc * P:(cc + 1) * P], a[32 * h:32 * h + 32, c * P:(c + 1) * P],
                                          b[32 * h:32 * h + 32, c * P:(c + 1) * P], start=True, stop=True)
                    m.then_inc(S("gl_prod"), 1)
                for q in between[l]:
                    p2_pe(pe, q)
            pe.wait_ge(S("gl_k_dec"), 1)
            for c in range(CH):
                m = pe.transpose(bank(4 + c // 4)[:, c % 4 * P:(c % 4 + 1) * P], g_k[:, c * P:(c + 1) * P], cst("ident"))
            m.then_inc(S("gl_kt"), 1)
            pe.wait_ge(S("gl_kt_taken"), 1)
            pe.wait_ge(S("gl_taken"), 8 * LEVELS)
            for c in range(CH):
                m = pe.matmul(bank(c // 2)[:, c % 2 * 256:(c % 2 + 1) * 256], gkt[:, c, :], gv[:, c, :], start=True, stop=True)
                m.then_inc(S("gl_delta"), 1)
            pe.wait_ge(S("gl_states"), CH)
            pe.wait_ge(S("gl_q_dec"), 1)
            for hp in range(2):
                for c in range(CH):
                    o = slice(2 * hp * HALF + c * P, 2 * hp * HALF + (c + 1) * P)
                    pe.matmul(PS[:, o], gS[:, c, hp * P:(hp + 1) * P], g_q[:, c * P:(c + 1) * P], start=True, stop=False)
                    for x in range(2):
                        h = 2 * hp + x
                        m = pe.matmul(PS[64 * x:64 * x + 64, o], gv[:, c, 64 * h:64 * h + 64], gA[:, h, c, :], start=False, stop=True)
                m.then_inc(S("gl_o"), 1)
            for q in range(40, 44):
                p2_pe(pe, q)
            for hp in range(2):
                pe.wait_ge(S("gl_o_sq"), hp + 1)
                for h in range(2):
                    m = pe.matmul(bank(4 + h), cst("blk64"), gsq[:, hp, h * HALF:(h + 1) * HALF], start=True, stop=True)
                m.then_inc(S("gl_sum"), 1)
                pe.wait_ge(S("gl_root"), hp + 1)

        def gla_act(act, between):
            act.dma_start(g_lora, lora_d[:, T:T + 256]).then_inc(S("glora_in"), 16)
            act.wait_ge(S("glora_in"), 16)
            high(act, gl_hi, g_lora).then_inc(S("small_high"), 1)
            act.wait_ge(S("gl_down"), 1)
            act.activation(gt, PS[0:16, 0:T], ACT.Copy).then_inc(S("gl_down_taken"), 1)
            act.preload_act_table_set("natural_log_exp_and_others")
            act.wait_ge(S("gl_gate"), 1)
            act.activation(gy, bank(2, 2), ACT.Identity, bias=vcol("gk_b")).then_inc(S("gl_y"), 1)
            act.wait_ge(S("gl_y"), 1)
            act.activation(gtmp, gy, ACT.Abs).then_inc(S("gl_soft"), 1)
            act.wait_ge(S("gl_soft"), 1)
            act.activation(gtmp, gtmp, ACT.Exp, scale=-1.0).then_inc(S("gl_soft"), 1)
            act.wait_ge(S("gl_soft"), 2)
            act.activation(gtmp, gtmp, ACT.Ln, bias=1.0).then_inc(S("gl_soft"), 1)
            for l in range(1, LEVELS + 1):
                if l < LEVELS:
                    act.wait_ge(S("gl_diff"), l)
                    act.activation(lv[:, l % 2, :], lv[:, l % 2, :], ACT.Exp, scale=1.0 / 16).then_inc(S("gl_exp"), 1)
                for q in between[l - 1]:
                    p2_act(act, q)
            act.wait_ge(S("gl_end_diff"), 1)
            act.activation(g_k, g_k, ACT.Exp, scale=1.0 / 16).then_inc(S("gl_end_exp"), 1)
            act.activation(g_q, gb, ACT.Exp, scale=1.0 / 16).then_inc(S("gl_end_exp"), 1)
            act.activation(elast.unsqueeze(2), last_of, ACT.Exp, scale=1.0 / 16).then_inc(S("gl_end_exp"), 1)
            act.wait_ge(S("gl_kt"), 1)
            act.activation(gkt, bank(4, 2).rearrange("p (c f) -> p c f", c=CH), ACT.Copy).then_inc(S("gl_kt_taken"), 1)
            for hp in range(2):
                act.wait_ge(S("gl_o"), 2)
                act.activation(gsq[:, hp, :], bank(2 * hp, 2), ACT.Square).then_inc(S("gl_o_sq"), 1)
            for q in range(40, 44):
                p2_act(act, q)
            for hp in range(2):
                act.wait_ge(S("gl_sum"), hp + 1)
                act.activation(gsq[:, hp, :], bank(4, 2), ACT.Sqrt, bias=cst("eps5"), scale=1.0 / 64).then_inc(S("gl_root"), 1)

        def gla_dve(dve, between):
            dve.memset(rkv[:, :, 0:PAD], 0.0).then_inc(S("rkv_pad"), 1)
            dve.wait_ge(S("small_high"), SMALL_GK)
            low(dve, gl_lo, g_lora, gl_hi).then_inc(S("small_low"), 1)
            dve.memset(pos_f, 1.0).then_inc(S("gl_mask"), 1)
            dve.wait_ge(S("gl_mask"), 1)
            dve.memset(pos_f.rearrange("p (c t) -> p c t", c=CH)[:, :, 0:1], 0.0).then_inc(S("gl_mask"), 1)
            dve.wait_ge(S("gl_soft"), 3)
            dve.scalar_tensor_tensor(gy, gy, 0.0, gtmp, ALU.min, ALU.subtract).then_inc(S("gl_lin"), 1)
            dve.wait_ge(S("gl_lin"), 1)
            dve.wait_ge(S("gl_mask"), 2)
            dve.tensor_tensor_scan(gb, pos_f, gy, 0.0, ALU.mult, ALU.add).then_inc(S("gl_cum"), 1)
            dve.wait_ge(S("gl_cum"), 1)

            def diff(l):
                n = 2 ** (l - 1)
                b4 = gb.rearrange("p (m h s) -> p m h s", h=2, s=n)
                d4 = lv[:, l % 2, :].rearrange("p (m h s) -> p m h s", h=2, s=n)
                ref = b4[:, :, 0, n - 1:n].broadcast_to([P, T // (2 * n), n])
                if l >= 3:
                    dve.wait_ge(S("gl_prod"), 2 * (l - 2) + 2)
                dve.tensor_tensor(d4[:, :, 1, :], b4[:, :, 1, :], ref, ALU.subtract)
                dve.tensor_tensor(d4[:, :, 0, :], ref, b4[:, :, 0, :], ALU.subtract).then_inc(S("gl_diff"), 1)

            diff(1)

            def times_qk(l):
                n = 2 ** (l - 1)
                dve.wait_ge(S("gl_exp"), l)
                for h, src in ((1, gq), (0, gk)):
                    d4 = lv[:, l % 2, :].rearrange("p (m h s) -> p m h s", h=2, s=n)[:, :, h, :]
                    dve.tensor_tensor(d4, d4, src.rearrange("p (m h s) -> p m h s", h=2, s=n)[:, :, h, :], ALU.mult)\
                       .then_inc(S("gl_level"), 1)

            for l in range(LEVELS):
                if 1 <= l < LEVELS - 1:
                    diff(l + 1)
                for half in range(2):
                    if half == 1 and l + 1 < LEVELS:
                        times_qk(l + 1)
                    dve.wait_ge(S("gl_prod"), 2 * l + half + 1)
                    for h in range(4):
                        dst = gA[:, h, 4 * half:4 * half + 4, :]
                        src = bank(h).rearrange("p (c t) -> p c t", c=4)
                        if l == 0:
                            dve.tensor_tensor(dst, src, cst("ident").unsqueeze(1).broadcast_to([P, 4, P]), ALU.mult)\
                               .then_inc(S("gl_taken"), 1)
                        else:
                            o = CONST["level"][0] + (l - 1) * P
                            mask = const[:, o:o + P].bitcast(I32).unsqueeze(1).broadcast_to([P, 4, P])
                            dve.copy_predicated(dst, mask, src).then_inc(S("gl_taken"), 1)
                for q in between[l]:
                    if q in GATES:
                        apply_gate(dve, q)
            dve.wait_ge(S("gl_prod"), 2 * LEVELS)
            b3 = gb.rearrange("p (c t) -> p c t", c=CH)
            dve.tensor_tensor(g_k.rearrange("p (c t) -> p c t", c=CH), last_of.broadcast_to([P, CH, P]), b3,
                              ALU.subtract).then_inc(S("gl_end_diff"), 1)
            dve.wait_ge(S("gl_end_exp"), 2)
            dve.tensor_tensor(g_k, g_k, gk, ALU.mult).then_inc(S("gl_k_dec"), 1)
            dve.tensor_tensor(g_q, g_q, gq, ALU.mult).then_inc(S("gl_q_dec"), 1)
            dve.wait_ge(S("gl_end_exp"), 3)
            dve.memset(gS[:, 0, :], 0.0).then_inc(S("gl_states"), 1)
            for c in range(CH - 1):
                dve.wait_ge(S("gl_delta"), c // 2 * 2 + 2)
                dve.wait_ge(S("gl_states"), c + 1)
                dve.tensor_tensor(small_delta, bank(c // 2)[:, c % 2 * 256:(c % 2 + 1) * 256], cst("gla_state"),
                                  ALU.mult).then_inc(S("gl_masked"), 1)
                dve.wait_ge(S("gl_masked"), c + 1)
                dve.scalar_tensor_tensor(gS[:, c + 1, :], gS[:, c, :], elast[:, c:c + 1], small_delta, ALU.mult, ALU.add)\
                   .then_inc(S("gl_states"), 1)
            dve.wait_ge(S("gl_delta"), CH)
            for hp in range(2):
                dve.wait_ge(S("gl_root"), hp + 1)
                dve.reciprocal(gsq[:, hp, :], gsq[:, hp, :]).then_inc(S("gl_rstd"), 1)
                dve.wait_ge(S("gl_rstd"), hp + 1)
                dve.scalar_tensor_tensor(yT[:, 6 + hp, :], bank(2 * hp, 2), vcol("gla_norm"), gsq[:, hp, :], ALU.mult, ALU.mult)\
                   .then_inc(S("gl_y_ready"), 1)

        KAPPA = float(np.exp(-0.5))
        TL = 4
        RW_LEVELS = range(1, 6)
        RW_STEPS = {
            "act": ["sig_w", "sig_a", "kk_sq", "kk_root", "exp_p", "exp_pinv", "exp_pm", "tok_c", "tok_b", "tok_k", "tok_v", "mbt"]
                   + [f"x{l}{b}" for l in RW_LEVELS for b in range(2)] + ["mkv", "nw0", "nw1", "nw1t", "y0", "y1", "y_sq", "y_root"],
            "pe": ["lora", "kk_sum", "bon_sum", "tr_c", "tr_b", "tr_k", "tr_v", "p_mbt", "p_mb", "p_mkt", "p_rbt", "p_rkt"]
                  + [f"{x}{l}{b}" for l in RW_LEVELS for x in ("px", "pd") for b in range(2)]
                  + ["p_mkv", "pw0", "pw1", "pw1t", "p_gt", "p_h"] + [f"ps{c}" for c in range(8)] + ["pu", "py", "y_sum", "y_var"],
            "dve": ["kk", "cum", "cum_m", "a_ka", "k_new", "kk_max", "kk_rec", "kkn", "kk_a", "bhat", "bonus", "bonus_v",
                    "tt_a", "tt", "t_a", "t", "mkt", "rbt", "rkt"] + [f"up{l}{b}" for l in RW_LEVELS for b in range(2)]
                   + ["s_start", "gt", "h"] + [f"s{c}" for c in range(8)] + ["u", "centre", "y_rec", "y_norm", "y_sum", "gated"],
            "pool": ["chat", "khat", "rhat"] + [f"ms{l}{b}" for l in RW_LEVELS for b in range(2)],
        }
        rw_next = {e: 0 for e in RW_STEPS}

        def rw(e, name, u):
            return S("rw_" + e), len(RW_STEPS[e]) * u + RW_STEPS[e].index(name) + 1

        def rw_done(e, name, ins):
            assert RW_STEPS[e][rw_next[e] % len(RW_STEPS[e])] == name, (e, name)
            rw_next[e] += 1
            ins.then_inc(S("rw_" + e), 1)

        w2a2 = g_lora
        ar = Arena()
        ar.at = 6 * (PAD + T) + 256 + HALF
        lt = ar.take(T)
        sg, cum, aa, kkn, kn, tm, chat, bhat, khat, rhat, Pt, Pinv, Pm = (ar.take(HALF) for _ in range(13))
        yv, bv = gate[1], pos_f[:, HALF:T]
        ctok, btok, ktok, vtok = (ar.take(HALF).rearrange("p (t f) -> p t f", t=TL) for _ in range(4))
        Sst = ar.take(9 * 64).rearrange("p (c v) -> p c v", c=9)
        Ub = Pm.rearrange("p (h t v) -> p h t v", h=2, t=TL)
        nw1t, GT, Hb = sg, aa.rearrange("p (t c k) -> p t c k", c=2, k=64), kkn.rearrange("p (t c k) -> p t c k", c=2, k=64)
        flat = uT[:, :, :].rearrange("p k t -> p (k t)")
        Tm, TTm, MbT, Xm, Ms, MkT, RBT, RKT = (flat[:, x * T:(x + 1) * T].rearrange("p (h t j) -> p h t j", h=2, t=TL)
                                               for x in range(8))
        nW = Xm
        mkv = flat[:, 4 * T:4 * T + HALF].rearrange("p (h t v) -> p h t v", h=2, t=TL)
        wa_raw, wa_mu, wa_rest = (arena[:, 9216 + x * T:9216 + (x + 1) * T].rearrange("p (k f) -> p k f", k=KC)
                                  for x in range(3))
        wa_rounded = [arena_r[:, x:x + T].rearrange("p (k f) -> p k f", k=KC) for x in (14336, 15360, 10240, 11264)]
        mu_hi, rest_hi, mu_lo, rest_lo = wa_rounded
        mixd = [arena[:, 12288 + x * T:12288 + (x + 1) * T] for x in range(2)]
        smask = pos_f[:, 0:HALF]

        def rw_pre_pe(pe):
            pe.wait_ge(S("small_low"), SMALL_WA)
            for h in range(2):
                lo, hi = h * HALF, (h + 1) * HALF
                for k in range(KC):
                    product(pe, bank(h), (rest_hi[:, k, :], rest_lo[:, k, :]), u_two(k, lo, hi), k == 0, False)
                    m = product(pe, bank(h), (mu_hi[:, k, :], mu_lo[:, k, :]), u_two(k, lo - 1, hi - 1), False, k == KC - 1)[1]
                m.then_inc(S("lora_mm"), 1)

        def wa_act(act):
            act.wait_ge(S("gl_y_ready"), 2)
            act.dma_start(wa_raw.rearrange("p k f -> p (k f)"), lora_d[:, 0:T]).then_inc(S("wa_in"), 16)
            act.dma_start(w2a2, lora_d[:, T + 256:T + 512]).then_inc(S("wa_in"), 16)

        def wa_split_act(act):
            act.wait_ge(S("wa_ready"), KC)
            for dst, src in ((mu_hi, wa_mu), (rest_hi, wa_rest)):
                high(act, dst, src).then_inc(S("small_high"), 1)

        def wa_dve(dve):
            dve.wait_ge(S("wa_in"), 32)
            for k in range(KC):
                dve.tensor_scalar(wa_mu[:, k, 0:64], wa_raw[:, k, 0:64], vcol("mu_w", k), None, ALU.mult).then_inc(S("wa_part"), 1)
                dve.tensor_scalar(wa_mu[:, k, 64:128], wa_raw[:, k, 64:128], vcol("mu_a", k), None, ALU.mult).then_inc(S("wa_part"), 1)
            for k in range(KC):
                dve.wait_ge(S("wa_part"), 2 * k + 2)
                dve.tensor_tensor(wa_rest[:, k, :], wa_raw[:, k, :], wa_mu[:, k, :], ALU.subtract).then_inc(S("wa_ready"), 1)

        def wa_split_dve(dve):
            for x, (dst, src, hi_part) in enumerate(((mu_lo, wa_mu, mu_hi), (rest_lo, wa_rest, rest_hi))):
                dve.wait_ge(S("small_high"), SMALL_WA - 1 + x)
                low(dve, dst, src, hi_part).then_inc(S("small_low"), 1)

        def rw_pre_act(act):
            for h in range(2):
                act.wait_ge(S("lora_mm"), h + 1)
                act.activation(lt[0:64, h * HALF:(h + 1) * HALF], bank(h)[0:64, :], ACT.Tanh).then_inc(S("lora_out"), 1)
                act.activation(lt[64:128, h * HALF:(h + 1) * HALF], bank(h)[64:128, :], ACT.Copy).then_inc(S("lora_out"), 1)

        def rw_pre_dve(dve):
            dve.memset(smask, 1.0).then_inc(S("rw_mask"), 1)
            dve.wait_ge(S("rw_mask"), 1)
            dve.memset(smask.rearrange("p (c t) -> p c t", t=64)[:, :, 0:1], 0.0).then_inc(S("rw_mask"), 1)
            dve.wait_ge(S("p2_evac"), 32)
            dve.wait_ge(S("rkv_pad"), 1)
            for x in range(6):
                if x >= 2:
                    dve.wait_ge(S("rkv_mixed"), x - 1)
                dve.tensor_tensor(mixd[x % 2], rkv[:, x, PAD - 1:PAD + T - 1], rkv[:, x, PAD:], ALU.subtract).then_inc(S("rkv_diff"), 1)
                dve.wait_ge(S("rkv_diff"), x + 1)
                dve.scalar_tensor_tensor(rkv[:, x, PAD:], mixd[x % 2], vcol("mu_rkv", x), rkv[:, x, PAD:], ALU.mult, ALU.add)\
                   .then_inc(S("rkv_mixed"), 1)

        def rw_rows(u):
            p, hf = u // 2, u % 2
            cols = slice(PAD + hf * HALF, PAD + (hf + 1) * HALF)
            return p, hf, rkv[:, p, cols], rkv[:, 2 + p, cols], rkv[:, 4 + p, cols]

        def rw_pe(pe, u):
            p, hf, r_, k_, v_ = rw_rows(u)
            w, done = (lambda e, n, uu=u: pe.wait_ge(*rw(e, n, uu))), (lambda n, ins: rw_done("pe", n, ins))
            if u >= 1:
                w("dve", "gated", u - 1)
            tc = slice(hf * HALF, (hf + 1) * HALF)
            pe.matmul(bank(0), w2a2[0:64, p * P:(p + 1) * P], lt[0:64, tc], start=True, stop=True)
            done("lora", pe.matmul(bank(1), w2a2[64:128, p * P:(p + 1) * P], lt[64:128, tc], start=True, stop=True))
            w("act", "kk_sq")
            done("kk_sum", pe.matmul(bank(2), cst("blk64"), tm, start=True, stop=True))
            w("dve", "bonus")
            done("bon_sum", pe.matmul(bank(3), cst("blk64"), bv, start=True, stop=True))
            for x, (n, src, e, ready) in enumerate((("tr_c", chat, "pool", "chat"), ("tr_b", bhat, "dve", "bhat"),
                                                    ("tr_k", khat, "pool", "khat"), ("tr_v", v_, None, None))):
                if e:
                    w(e, ready)
                for t in range(TL):
                    m = pe.transpose(bank(4 + x)[:, t * P:(t + 1) * P], src[:, t * P:(t + 1) * P], cst("ident"))
                done(n, m)
            w("pool", "rhat")
            for n, a, b, bk, free in (("p_mbt", bhat, chat, 0, ("act", "sig_a")), ("p_mb", chat, bhat, 2, ("dve", "bonus_v")),
                                      ("p_mkt", khat, chat, 4, ("act", "tok_b")), ("p_rbt", bhat, rhat, 6, ("act", "tok_v")),
                                      ("p_rkt", khat, rhat, 0, ("act", "mbt"))):
                w(*free)
                for t in range(TL):
                    for h in range(2):
                        r = slice(64 * h, 64 * h + 64)
                        m = pe.matmul(bank(bk + h)[:, t * P:(t + 1) * P], a[r, t * P:(t + 1) * P], b[r, t * P:(t + 1) * P],
                                      start=True, stop=True)
                done(n, m)
            for l in RW_LEVELS:
                for b in range(2):
                    if l == 1 and b == 0:
                        w("dve", "rkt")
                    if l > 1:
                        w("dve", f"up{l - 1}{b}")
                    w("pool", f"ms{l}{b}")
                    for t in range(TL):
                        m = pe.matmul(bank(b)[:, t * P:(t + 1) * P], Ms[:, b, t, :], Tm[:, b, t, :], start=True, stop=True)
                    done(f"px{l}{b}", m)
                for b in range(2):
                    w("act", f"x{l}{b}")
                    for t in range(TL):
                        if l < 5:
                            pe.matmul(bank(2 + b)[:, t * P:(t + 1) * P], TTm[:, b, t, :], Xm[:, b, t, :], start=True, stop=True)
                        m = pe.matmul(bank(4 + b)[:, t * P:(t + 1) * P], Xm[:, b, t, :], TTm[:, b, t, :], start=True, stop=True)
                    done(f"pd{l}{b}", m)
            for h in range(2):
                for t in range(TL):
                    m = pe.matmul(bank(6)[:, (TL * h + t) * 64:(TL * h + t + 1) * 64], MkT[:, h, t, :], vtok[:, t, 64 * h:64 * h + 64],
                                  start=True, stop=True)
            done("p_mkv", m)
            w("act", "mkv")
            for h in range(2):
                w("dve", f"up5{h}")
                for t in range(TL):
                    pe.matmul(bank(h)[:, t * P:t * P + 64], TTm[:, h, t, :], ctok[:, t, 64 * h:64 * h + 64], start=True, stop=True)
                    m = pe.matmul(bank(h)[:, t * P + 64:(t + 1) * P], TTm[:, h, t, :], mkv[:, h, t, :], start=True, stop=True)
                done(f"pw{h}", m)
            for h in range(2):
                for t in range(TL):
                    m = pe.matmul(PS[64 * h:64 * h + 64, 2 * HALF + t * P:2 * HALF + (t + 1) * P], ctok[:, t, 64 * h:64 * h + 64],
                                  TTm[:, h, t, :], start=True, stop=True)
            done("pw1t", m)
            w("act", "nw1")
            for h in range(2):
                for t in range(TL):
                    for cp in range(2):
                        rr = slice(64 * cp, 64 * cp + 64)
                        m = pe.matmul(PS[64 * h:64 * h + 64, (4 + cp) * HALF + t * 64:(4 + cp) * HALF + (t + 1) * 64],
                                      nW[rr, h, t, 0:64], btok[rr, t, 64 * h:64 * h + 64], start=True, stop=True)
            done("p_gt", m)
            for h in range(2):
                for t in range(TL):
                    for cp in range(2):
                        rr = slice(64 * cp, 64 * cp + 64)
                        o = PS[64 * h:64 * h + 64, (6 + cp) * HALF + t * 64:(6 + cp) * HALF + (t + 1) * 64]
                        pe.matmul(o, ktok[rr, t, 64 * h:64 * h + 64], vtok[rr, t, 64 * h:64 * h + 64], start=True, stop=False)
                        m = pe.matmul(o, btok[rr, t, 64 * h:64 * h + 64], nW[rr, h, t, 64:128], start=False, stop=True)
            done("p_h", m)
            for c in range(8):
                w("dve", "h" if c == 0 else f"s{c - 1}")
                for h in range(2):
                    r = slice(64 * h, 64 * h + 64)
                    m = pe.matmul(PS[r, h * HALF:h * HALF + 64], GT[r, c // 2, c % 2, :], Sst[r, c, :], start=True, stop=True)
                done(f"ps{c}", m)
            w("act", "nw1t")
            for t in range(TL):
                for cp in range(2):
                    for h in range(2):
                        r = slice(64 * h, 64 * h + 64)
                        m = pe.matmul(PS[64 * cp:64 * cp + 64, (2 + h) * HALF + t * 64:(2 + h) * HALF + (t + 1) * 64],
                                      nw1t[r, t * P + 64 * cp:t * P + 64 * cp + 64], Sst[r, 2 * t + cp, :], start=True, stop=True)
            done("pu", m)
            w("dve", "u")
            for h in range(2):
                r = slice(64 * h, 64 * h + 64)
                for t in range(TL):
                    o = (4 + h) * HALF + t * P
                    pe.matmul(PS[r, o:o + P], vtok[:, t, 64 * h:64 * h + 64], RKT[:, h, t, :], start=True, stop=False)
                    pe.matmul(PS[r, o:o + P], Ub[:, h, t, :], RBT[:, h, t, :], start=False, stop=False)
                    for cp in range(2):
                        m = pe.matmul(PS[r, o + 64 * cp:o + 64 * cp + 64], Sst[r, 2 * t + cp, :],
                                      rhat[r, t * P + 64 * cp:t * P + 64 * cp + 64], start=False, stop=(cp == 1))
            done("py", m)
            w("act", "y1")
            done("y_sum", pe.matmul(bank(6), cst("blk64"), yv, start=True, stop=True))
            w("act", "y_sq")
            done("y_var", pe.matmul(bank(7), cst("blk64"), tm, start=True, stop=True))

        def rw_act(act, u):
            p, hf, r_, k_, v_ = rw_rows(u)
            w, done = (lambda e, n, uu=u: act.wait_ge(*rw(e, n, uu))), (lambda n, ins: rw_done("act", n, ins))
            w("pe", "lora")
            done("sig_w", act.activation(sg, bank(0), ACT.Sigmoid, bias=vcol("w0", p)))
            done("sig_a", act.activation(aa, bank(1), ACT.Sigmoid, bias=vcol("a0", p)))
            w("dve", "kk")
            done("kk_sq", act.activation(tm, kkn, ACT.Square))
            w("pe", "kk_sum")
            done("kk_root", act.activation(tm, bank(2), ACT.Sqrt))
            w("dve", "cum_m")
            done("exp_p", act.activation(Pt, cum, ACT.Exp, scale=-KAPPA))
            done("exp_pinv", act.activation(Pinv, cum, ACT.Exp, scale=KAPPA))
            done("exp_pm", act.activation(Pm, Pm, ACT.Exp, scale=-KAPPA))
            for x, (n, tr, dst) in enumerate((("tok_c", "tr_c", ctok), ("tok_b", "tr_b", btok), ("tok_k", "tr_k", ktok),
                                              ("tok_v", "tr_v", vtok))):
                w("pe", tr)
                done(n, act.activation(dst.rearrange("p t f -> p (t f)"), bank(4 + x), ACT.Copy))
            w("pe", "p_mbt")
            done("mbt", act.activation(MbT.rearrange("p h t j -> p (h t j)"), bank(0, 2), ACT.Copy))
            for l in RW_LEVELS:
                for b in range(2):
                    w("pe", f"px{l}{b}")
                    if l > 1:
                        w("pe", f"pd{l - 1}{b}")
                    elif b == 0:
                        w("dve", "tt")
                    done(f"x{l}{b}", act.activation(Xm[:, b, :, :].rearrange("p t j -> p (t j)"), bank(b), ACT.Copy))
            w("pe", "p_mkv")
            done("mkv", act.activation(mkv.rearrange("p h t v -> p (h t v)"), bank(6), ACT.Copy))
            for h in range(2):
                w("pe", f"pw{h}")
                done(f"nw{h}", act.activation(nW[:, h, :, :].rearrange("p t j -> p (t j)"), bank(h), ACT.Copy, scale=-1.0))
            w("pe", "pw1t")
            done("nw1t", act.activation(nw1t, bank(2), ACT.Copy, scale=-1.0))
            w("pe", "py")
            for h in range(2):
                r = slice(64 * h, 64 * h + 64)
                done(f"y{h}", act.activation(yv[r, :], PS[r, (4 + h) * HALF:(5 + h) * HALF], ACT.Copy))
            w("dve", "centre")
            done("y_sq", act.activation(tm, yv, ACT.Square))
            w("pe", "y_var")
            done("y_root", act.activation(tm, bank(7), ACT.Sqrt, bias=cst("eps_ln"), scale=1.0 / 64))

        def rw_dve(dve, u):
            p, hf, r_, k_, v_ = rw_rows(u)
            w, done = (lambda e, n, uu=u: dve.wait_ge(*rw(e, n, uu))), (lambda n, ins: rw_done("dve", n, ins))

            def eight(x):
                return x.unsqueeze(1).broadcast_to([P, 8, P])

            def flat8(x):
                return x.rearrange("p h t j -> p (h t) j")

            def banks8(b):
                return bank(b, 2).rearrange("p (x j) -> p x j", x=8)

            done("kk", dve.tensor_scalar(kkn, k_, vcol("k_k", p), None, ALU.mult))
            w("act", "sig_w")
            done("cum", dve.tensor_tensor_scan(cum, smask, sg, 0.0, ALU.mult, ALU.add))
            w("dve", "cum")
            done("cum_m", dve.tensor_tensor(Pm, cum, sg, ALU.subtract))
            w("act", "sig_a")
            done("a_ka", dve.tensor_scalar(kn, aa, 1.0, vcol("k_a", p), ALU.subtract, ALU.mult))
            w("dve", "a_ka")
            done("k_new", dve.scalar_tensor_tensor(kn, kn, 1.0, k_, ALU.add, ALU.mult))
            w("act", "kk_root")
            done("kk_max", dve.tensor_scalar(tm, tm, 1e-12, None, ALU.max))
            w("dve", "kk_max")
            done("kk_rec", dve.reciprocal(tm, tm))
            w("dve", "kk_rec")
            done("kkn", dve.tensor_tensor(kkn, kkn, tm, ALU.mult))
            w("dve", "kkn")
            done("kk_a", dve.tensor_tensor(bhat, kkn, aa, ALU.mult))
            w("dve", "kk_a")
            w("act", "exp_pinv")
            done("bhat", dve.tensor_tensor(bhat, bhat, Pinv, ALU.mult))
            done("bonus", dve.scalar_tensor_tensor(bv, r_, vcol("r_k", p), kn, ALU.mult, ALU.mult))
            w("pe", "bon_sum")
            done("bonus_v", dve.tensor_tensor(bv, bank(3), v_, ALU.mult))
            w("act", "mbt")
            o = CONST["level"][0]
            done("tt_a", dve.tensor_tensor(flat8(Xm), flat8(MbT), eight(const[:, o:o + P]), ALU.mult))
            w("dve", "tt_a")
            done("tt", dve.tensor_tensor(flat8(TTm), eight(cst("ident")), flat8(Xm), ALU.subtract))
            w("pe", "p_mb")
            done("t_a", dve.tensor_tensor(flat8(Tm), banks8(2), eight(cst("first_low")), ALU.mult))
            w("dve", "t_a")
            done("t", dve.tensor_tensor(flat8(Tm), eight(cst("ident")), flat8(Tm), ALU.subtract))
            w("pe", "p_mkt")
            done("mkt", dve.tensor_tensor(flat8(MkT), banks8(4), eight(cst("strict64")), ALU.mult))
            w("pe", "p_rbt")
            done("rbt", dve.tensor_tensor(flat8(RBT), banks8(6), eight(cst("incl64")), ALU.mult))
            w("pe", "p_rkt")
            done("rkt", dve.tensor_tensor(flat8(RKT), banks8(0), eight(cst("incl64")), ALU.mult))
            for l in RW_LEVELS:
                for b in range(2):
                    w("pe", f"pd{l}{b}")
                    if l < 5:
                        t2 = Tm[:, b, :, :].rearrange("p t j -> p (t j)")
                        dve.tensor_tensor(t2, t2, bank(2 + b), ALU.subtract).then_inc(S("rw_t"), 1)
                    t2 = TTm[:, b, :, :].rearrange("p t j -> p (t j)")
                    if l < 5:
                        dve.wait_ge(S("rw_t"), 8 * u + 2 * (l - 1) + b + 1)
                    done(f"up{l}{b}", dve.tensor_tensor(t2, t2, bank(4 + b), ALU.subtract))
            if hf == 0:
                done("s_start", dve.memset(Sst[:, 0, :], 0.0))
            else:
                done("s_start", dve.tensor_copy(Sst[:, 0, :], Sst[:, 8, :]))
            w("pe", "p_gt")
            done("gt", dve.tensor_tensor(GT.rearrange("p t c k -> p c t k"), bank(4, 2).rearrange("p (c x) -> p c x", c=2)[:, :, 0:256]
                                         .rearrange("p c (t k) -> p c t k", t=TL),
                                         cst("ident64").unsqueeze(1).unsqueeze(1).broadcast_to([P, 2, TL, 64]), ALU.add))
            w("pe", "p_h")
            done("h", dve.tensor_tensor(Hb.rearrange("p t c k -> p c t k"), bank(6, 2).rearrange("p (c x) -> p c x", c=2)[:, :, 0:256]
                                        .rearrange("p c (t k) -> p c t k", t=TL),
                                        Pt.rearrange("p (t c s) -> p c t s", c=2, s=64)[:, :, :, 63:64].broadcast_to([P, 2, TL, 64]),
                                        ALU.mult))
            w("dve", "h")
            for c in range(8):
                w("pe", f"ps{c}")
                for h in range(2):
                    r = slice(64 * h, 64 * h + 64)
                    m = dve.scalar_tensor_tensor(Sst[r, c + 1, :], PS[r, h * HALF:h * HALF + 64], Pt[r, 64 * c + 63:64 * c + 64],
                                                 Hb[r, c // 2, c % 2, :], ALU.mult, ALU.add)
                    if h == 0:
                        m.then_inc(S("rw_s"), 1)
                dve.wait_ge(S("rw_s"), 8 * u + c + 1)
                done(f"s{c}", m)
            w("pe", "pu")
            done("u", dve.tensor_tensor(Ub, bank(2, 2).rearrange("p (h x) -> p h x", h=2)[:, :, 0:256].rearrange("p h (t v) -> p h t v", t=TL),
                                        nW[:, :, :, 64:128], ALU.add))
            w("pe", "y_sum")
            done("centre", dve.scalar_tensor_tensor(yv, bank(6), -1.0 / 64, yv, ALU.mult, ALU.add))
            w("act", "y_root")
            done("y_rec", dve.reciprocal(tm, tm))
            w("dve", "y_rec")
            done("y_norm", dve.scalar_tensor_tensor(yv, yv, vcol("ln_w", p), tm, ALU.mult, ALU.mult))
            w("dve", "y_norm")
            done("y_sum", dve.scalar_tensor_tensor(yv, yv, vcol("ln_b", p), bv, ALU.add, ALU.add))
            w("dve", "y_sum")
            dst = yT[:, 4 + p, hf * HALF:(hf + 1) * HALF]
            done("gated", dve.tensor_tensor(dst, dst, yv, ALU.mult))

        def rw_pool(pool, u):
            p, hf, r_, k_, v_ = rw_rows(u)
            w, done = (lambda e, n, uu=u: pool.wait_ge(*rw(e, n, uu))), (lambda n, ins: rw_done("pool", n, ins))
            w("dve", "kkn")
            w("act", "exp_pm")
            done("chat", pool.tensor_tensor(chat, kkn, Pm, ALU.mult))
            done("khat", pool.tensor_tensor(khat, kn, Pinv, ALU.mult))
            done("rhat", pool.tensor_tensor(rhat, r_, Pt, ALU.mult))
            w("act", "mbt")
            for l in RW_LEVELS:
                for b in range(2):
                    if l > 1:
                        w("pe", f"px{l - 1}{b}")
                    o = CONST["level"][0] + l * P
                    done(f"ms{l}{b}", pool.tensor_tensor(Ms[:, b, :, :], MbT[:, b, :, :],
                                                         const[:, o:o + P].unsqueeze(1).broadcast_to([P, TL, P]), ALU.mult))

        Y3 = [[0, 1], [2, 3, 4], [6, 7], [5]]

        def y3_place(u, k):
            return KC * SPLITS["y3"] + sum(len(ks) for ks in Y3[:u]) + Y3[u].index(k) + 1

        def y3_act(act, u):
            for k in Y3[u]:
                if k in (4, 5):
                    act.wait_ge(*rw("dve", "gated", u))
                high(act, in_h(k, 0, T), yT[:, k, :]).then_inc(S("split_high"), 1)

        def y3_dve(dve, u):
            for k in Y3[u]:
                dve.wait_ge(S("split_high"), y3_place(u, k))
                low(dve, in_y(k, 0, T), yT[:, k, :], in_h(k, 0, T)).then_inc(S("split_low"), 1)

        Z = arena[:, 0:KC * T].rearrange("p (k t) -> p k t", k=KC)
        gpost = sb("gpost", [P, KC])
        small_delta = yT[:, 7, 0:256]
        BETWEEN = [[20 + 3 * l + x for x in range(3) if 3 * l + x < 20] for l in range(LEVELS)]

        park_d = nc.dram_tensor("parked_stream", (P, KC, T), F, kind="Internal").ap()
        block = ctx.enter_context(nc.Block())

        @block.sync
        def _(sync):
            sync.dma_start(const[:, :], const_d).then_inc(S("const_in"), 16)
            sync.dma_start(vec[:, :], vec_d).then_inc(S("vec_in"), 16)
            for k in range(KC):
                sync.dma_start(hT[:, k, :], xT_d[:, k, :]).then_inc(S("x_in"), 16)
            sync.dma_start(pos_i[:, :], pos_d).then_inc(S("pos_in"), 16)
            with loop(sync, PANELS // 2) as i:
                for x in range(2):
                    sync.wait_ge(S("w_split"), 2 * i + (x + 1))
                    sync.dma_start(w_raw[:, x, :], w_d[bass.ds(2 * i + x, 1), :, :].rearrange("o p n -> p (o n)"))\
                        .then_inc(w_in[x], 16)
            for k in range(KC):
                sync.wait_ge(S("final_ready"), k + 1)
                sync.dma_start(out_d[:, k, :], Z[:, k, :]).then_inc(S("stored"), 16)
            sync.wait_ge(S("stored"), 16 * KC)

        @block.vector
        def _(dve):
            dve.memset(u_r[:, :, 0:PAD].bitcast(F), 0.0)
            dve.memset(h_r[:, :, 0:PAD].bitcast(F), 0.0)
            dve.wait_ge(S("vec_in"), 16)
            o = VEC["lam"][0]
            dve.memset(lamt[:, :], 0.0).then_inc(S("lam_a"), 1)
            dve.wait_ge(S("lam_a"), 1)
            for x in range(2):
                dve.tensor_tensor(lamt[:, x:x + 1], vec[:, o + 2 * x:o + 2 * x + 1], vec[:, o + 2 * x + 1:o + 2 * x + 2],
                                  ALU.mult).then_inc(S("lam_prod"), 1)
            dve.tensor_scalar(gsub[:, :], vcol("g_subln"), 1.0 - LAM_INIT, None, ALU.mult)
            dve.wait_ge(S("pos_in"), 16)
            dve.wait_ge(S("const_in"), 16)
            dve.tensor_copy(posf, pos_i[:, :]).then_inc(S("ang_step"), 1)
            dve.wait_ge(S("ang_step"), 1)
            dve.tensor_scalar(ang, posf, cst("inv_freq"), None, ALU.mult).then_inc(S("ang_step"), 1)
            dve.wait_ge(S("ang_step"), 2)
            dve.tensor_scalar(turns, ang, 0.15915494309189535, 12582912.0, ALU.mult, ALU.add).then_inc(S("ang_step"), 1)
            dve.wait_ge(S("ang_step"), 3)
            dve.tensor_scalar(turns, turns, 12582912.0, None, ALU.subtract).then_inc(S("ang_step"), 1)
            dve.wait_ge(S("ang_step"), 4)
            dve.scalar_tensor_tensor(ang, turns, -6.28125, ang, ALU.mult, ALU.add).then_inc(S("ang_step"), 1)
            dve.wait_ge(S("ang_step"), 5)
            dve.scalar_tensor_tensor(ang, turns, -0.0019353071795864769, ang, ALU.mult, ALU.add).then_inc(S("ang_step"), 1)
            dve.wait_ge(S("ang_step"), 6)
            dve.tensor_scalar(ang, ang, 3.1415925, -3.1415925, ALU.min, ALU.max).then_inc(S("ang_step"), 1)
            dve.wait_ge(S("ang_step"), 7)
            dve.scalar_tensor_tensor(posf, ang, -1.0, ang, ALU.mult, ALU.max).then_inc(S("ang_ready"), 1)
            dve.wait_ge(S("lam_exp"), 1)
            dve.tensor_tensor(lamt[:, 4:5], lamt[:, 3:4], lamt[:, 2:3], ALU.subtract).then_inc(S("lam_a"), 1)
            dve.wait_ge(S("lam_a"), 2)
            dve.tensor_scalar(lamt[:, 5:6], lamt[:, 4:5], LAM_INIT, None, ALU.subtract).then_inc(S("lam_a"), 1)
            dve.wait_ge(S("lam_a"), 3)
            dve.wait_ge(S("small_high"), SMALL_C)
            dve.tensor_tensor(c_lo[:, :, :], c_twice, c_hi[:, :, :].bitcast(F), ALU.subtract).then_inc(S("small_low"), 1)
            norm_dve(dve, "mix", lambda k: hT[:, k, :], lambda k: hT[:, k, :], lambda k: vcol("g_mix", k), T, n_rs)
            split_dve(dve, "mix", lambda k: hT[:, k, :], whole(in_u), whole(in_h))
            with loop(dve, 4) as i:
                da_dve(dve, i)
            with loop(dve, 4) as j:
                sb_dve(dve, j)
            split_dve(dve, "y1", lambda k: yT[:, k, :], whole(in_u), whole(in_y))
            dve.wait_ge(S("sb_y_ready"), 4)
            dve.wait_ge(S("x_in"), 16 * (KC + 1))
            dve.sem_inc(S("wo_evac"), 4)
            gemm_evac(dve, "wo", 8, T, add_to_h(dve, "wo"))
            norm_dve(dve, "mem", lambda k: mraw[:, k, :], lambda k: mT[:, k, :], lambda k: vcol("g_mem", k), MEM, m_rs)
            split_dve(dve, "mem", lambda k: mT[:, k, :], lambda k: mem_split(k, 0, MEM)[0], lambda k: mem_split(k, 0, MEM)[1])
            norm_dve(dve, "x", lambda k: hT[:, k, :], lambda k: yT[:, k, :], lambda k: vcol("g_cross", k), T, x_rs)
            split_dve(dve, "x", lambda k: yT[:, k, :], whole(in_u), whole(in_y))
            with loop(dve, 4) as i:
                x_dve(dve, i)
            split_dve(dve, "y2", lambda k: yT[:, k, :], whole(in_u), whole(in_y))
            dve.wait_ge(S("x_o_evac"), 16)
            dve.sem_inc(S("xo_evac"), 4)
            gemm_evac(dve, "xo", 8, T, add_to_h(dve, "xo"))
            norm_dve(dve, "mlp", lambda k: hT[:, k, :], lambda k: ul[:, k, :], lambda k: vcol("g_mlp", k), T, f_rs)
            split_dve(dve, "mlp", lambda k: ul[:, k, :], whole(in_u), lambda k: ul_r[:, k, :])
            dve.wait_ge(S("xo_evac"), 20)
            dve.sem_inc(S("dn_evac"), 4)
            with loop(dve, 4) as g:
                mlp_dve(dve, g)
            norm_dve(dve, "fin", lambda k: hT[:, k, :], lambda k: hT[:, k, :], lambda k: vcol("g_final", k), T, f_rs)
            dve.wait_ge(S("proj_evac"), PROJ * UNITS + 1)
            o = VEC["ada_b"][0]
            dve.tensor_tensor(ada[:, :], ada[:, :], vec[:, o:o + 24], ALU.add).then_inc(S("ada_ready"), 1)
            dve.wait_ge(S("ada_ready"), 1)
            o = VEC["norm_pre"][0]
            dve.scalar_tensor_tensor(gpre[:, :], ada[:, 8:16], 1.0, vec[:, o:o + 8], ALU.add, ALU.mult).then_inc(S("gpre_ready"), 1)
            dve.wait_ge(S("gpre_ready"), 1)
            norm_dve(dve, "pre", lambda k: hT[:, k, :], lambda k: U(k), lambda k: gpre[:, k:k + 1], T, f_rs)
            for k in range(KC):
                dve.wait_ge(S("split_high"), KC * SPLITS["u2"] + k + 1)
                dve.scalar_tensor_tensor(in_u(k, 0, T), U(k), ada[:, k:k + 1], in_h(k, 0, T).bitcast(F), ALU.add, ALU.subtract)\
                   .then_inc(S("split_low"), 1)
            swa_dve(dve)
            gla_dve(dve, BETWEEN)
            dve.wait_ge(S("gl_y_ready"), 2)
            wa_dve(dve)
            for q in range(44, 48):
                if q == 46:
                    wa_split_dve(dve)
                apply_gate(dve, q)
            rw_pre_dve(dve)
            dve.wait_ge(S("rw_mask"), 2)
            dve.wait_ge(S("rkv_mixed"), 6)
            dve.wait_ge(S("lora_mm"), 2)
            for u in range(4):
                rw_dve(dve, u)
                y3_dve(dve, u)
            o = VEC["norm_post"][0]
            dve.tensor_tensor(gpost[:, :], ada[:, 16:24], vec[:, o:o + 8], ALU.mult).then_inc(S("gpost_ready"), 1)
            dve.wait_ge(S("gpost_ready"), 1)
            norm_dve(dve, "post", lambda k: Z[:, k, :], lambda k: Z[:, k, :], lambda k: gpost[:, k:k + 1], T, f_rs)

        @block.gpsimd
        def _(pool):
            pool.sem_inc(S("w_split"), CREDIT)
            pool.wait_ge(S("const_in"), 16)
            with loop(pool, 15) as i:
                for x in range(2):
                    split_panel(pool, i, x)
            split_panel(pool, 15, 0)
            with loop(pool, 3) as j:
                sb_pool(pool, j, False)
            sb_pool(pool, 3, True)
            split_panel(pool, UNIT_PANELS // 2, 1)
            with loop(pool, (G2 + 24 - UNIT_PANELS - 2) // 2) as i:
                for x in range(2):
                    split_panel(pool, i + (UNIT_PANELS // 2 + 1), x)
            split_panel(pool, G2 // 2 + 12, 0)
            for u in range(4):
                rw_pool(pool, u)
            split_panel(pool, G2 // 2 + 12, 1)
            with loop(pool, 3) as i:
                for x in range(2):
                    split_panel(pool, i + (G2 // 2 + 13), x)
            pool.wait_ge(S("parked"), 16 * (KC + 1))
            for k in range(KC):
                pool.wait_ge(*norm_out("post", k + 1))
                pool.tensor_tensor(Z[:, k, :], Z[:, k, :], U(k), ALU.add).then_inc(S("final_ready"), 1)

        @block.scalar
        def _(act):
            act.wait_ge(S("vec_in"), 16)
            act.activation(cact[:, :], vec[:, VEC["c"][0]:VEC["c"][0] + 8], ACT.Silu).then_inc(S("cact_ready"), 1)
            act.wait_ge(S("cact_ready"), 1)
            act.activation(c_hi[:, :, :], c_twice, ACT.Copy).then_inc(S("small_high"), 1)
            act.wait_ge(S("lam_sum"), 1)
            act.activation(lamt[:, 2:4], bank(0)[:, 0:2], ACT.Exp).then_inc(S("lam_exp"), 1)
            act.wait_ge(S("ang_ready"), 1)
            act.activation(sinT, ang, ACT.Sin)
            act.activation(cosT, posf, ACT.Sin, bias=cst("half_pi"), scale=-1.0)
            act.wait_ge(S("const_in"), 16)
            norm_act(act, "mix", lambda k: hT[:, k, :], T, n_sq, n_rs, lambda k: [("x_in", 16 * KC)])
            split_act(act, "mix", lambda k: hT[:, k, :], whole(in_u), lambda k: norm_out("mix", k + 1))
            act.wait_ge(S("lam_exp"), 1)
            act.sem_inc(S("proj_evac"), 1)
            for c in range(PROJ):
                proj_act(act, 0, c)
            with loop(act, 4) as i:
                da_act(act, i)
            with loop(act, 3) as j:
                sb_act(act, j, False)
            act.wait_ge(S("proj_mm"), PROJ * UNITS)
            act.dma_start(hT, xT_d).then_inc(S("x_in"), 16)
            sb_act(act, 3, True)
            act.wait_ge(S("sb_y_ready"), 4)
            act.dma_start(mraw, memT_d).then_inc(S("mem_in"), 16)
            split_act(act, "y1", lambda k: yT[:, k, :], whole(in_u),
                      lambda k: (S("da_y_ready"), k + 1) if k < 4 else (S("sb_y_ready"), k - 3))
            norm_act(act, "mem", lambda k: mraw[:, k, :], MEM, m_sq, m_rs, lambda k: [("mem_in", 16)])
            split_act(act, "mem", lambda k: mT[:, k, :], lambda k: mem_split(k, 0, MEM)[0], lambda k: norm_out("mem", KC))

            def take_k(i, j, h, b):
                act.activation(dyn(KcT, NS * i + j, 1).rearrange("p o t -> p (o t)"), b, ACT.Copy).then_inc(S("xk_evac"), 1)

            def take_v(i, j, h, b):
                act.activation(Vc[:, :, bass.ds((NS * i + j) * P, P)], b.rearrange("p (t f) -> p t f", t=2),
                               ACT.Copy).then_inc(S("xv_evac"), 1)

            def take_q(i, j, h, b):
                act.activation(dyn(qcT, NS * i + j, 1, h * HALF, (h + 1) * HALF).rearrange("p o t -> p (o t)"), b,
                               ACT.Copy, scale=1.0 / 16).then_inc(S("xq_evac"), 1)

            act.wait_ge(S("wo_evac"), 20)
            act.sem_inc(S("xk_evac"), 4)
            gemm_evac(act, "xk", 8, MEM, take_k)
            norm_act(act, "x", lambda k: hT[:, k, :], T, x_sq, x_rs, lambda k: [])
            split_act(act, "x", lambda k: yT[:, k, :], whole(in_u), lambda k: norm_out("x", k + 1))
            act.wait_ge(S("xk_evac"), 12)
            act.sem_inc(S("xv_evac"), 4)
            gemm_evac(act, "xv", 8, MEM, take_v)
            act.wait_ge(S("xv_evac"), 12)
            act.sem_inc(S("xq_evac"), 4)
            gemm_evac(act, "xq", 8, T, take_q)
            act.wait_ge(S("xq_evac"), 20)
            with loop(act, 4) as i:
                x_act(act, i)
            split_act(act, "y2", lambda k: yT[:, k, :], whole(in_u), lambda k: (S("x_o_evac"), 4 * (k // 2) + 3 + k % 2))
            norm_act(act, "mlp", lambda k: hT[:, k, :], T, f_sq, f_rs, lambda k: [("xo_evac", 4 + 2 * (k + 1))])
            split_act(act, "mlp", lambda k: ul[:, k, :], whole(in_u), lambda k: norm_out("mlp", k + 1))
            with loop(act, 4) as g:
                mlp_act(act, g)
            norm_act(act, "fin", lambda k: hT[:, k, :], T, ul, f_rs, lambda k: [("dn_evac", 4 + 48 + 2 * (k + 1))])
            norm_act(act, "pre", lambda k: hT[:, k, :], T, ul, f_rs, lambda k: [("norm_out", KC * NORMS["fin"] + k + 1)])
            for k in range(KC):
                act.dma_start(park_d[:, k, :], hT[:, k, :]).then_inc(S("parked"), 16)
            act.wait_ge(S("ada_ready"), 1)
            act.wait_ge(S("parked"), 16 * KC)
            for k in range(KC):
                act.wait_ge(*norm_out("pre", k + 1))
                act.activation(in_h(k, 0, T), U(k), ACT.Identity, bias=ada[:, k:k + 1]).then_inc(S("split_high"), 1)
            act.wait_ge(*split_ready("mlp"))
            act.dma_start(sbias.rearrange("p h k -> p (h k)"), bias_d).then_inc(S("bias_in"), 16)
            for q in range(12):
                p2_act(act, q)
                if q == 9:
                    act.wait_ge(S("p2_evac"), 10)
                    act.dma_start(akx[0:64, :], ak[64:128, :]).then_inc(S("akx_in"), 16)
                    act.dma_start(akx[64:128, :], ak[0:64, :]).then_inc(S("akx_in"), 16)
            swa_act(act)
            act.wait_ge(S("sw_o_evac"), 16)
            gla_act(act, BETWEEN)
            wa_act(act)
            for q in range(44, 48):
                if q == 46:
                    wa_split_act(act)
                p2_act(act, q)
            rw_pre_act(act)
            for u in range(4):
                rw_act(act, u)
                y3_act(act, u)

            def take_z(i, j, h, b):
                act.activation(Z[:, bass.ds(NS * i + j, 1), h * HALF:(h + 1) * HALF].rearrange("p o t -> p (o t)"), b,
                               ACT.Copy).then_inc(S("out2_evac"), 1)

            act.wait_ge(*rw("dve", "gated", 3))
            act.dma_start(uT[:, :, PAD:], park_d).then_inc(S("parked"), 16)
            act.sem_inc(S("out2_evac"), 4)
            gemm_evac(act, "out2", 8, T, take_z)
            act.wait_ge(S("out2_evac"), 20)
            norm_act(act, "post", lambda k: Z[:, k, :], T, f_sq, f_rs, lambda k: [])

        @block.tensor
        def _(pe):
            pe.sem_inc(S("weight_free"), CREDIT)
            pe.wait_ge(S("const_in"), 16)
            pe.wait_ge(S("lam_prod"), 2)
            pe.matmul(bank(0)[:, 0:2], cst("ones"), lamt[:, 0:2], start=True, stop=True).then_inc(S("lam_sum"), 1)
            norm_pe(pe, "mix", T, n_sq)
            pe.wait_ge(S("small_low"), SMALL_C)
            pe.wait_ge(*split_ready("mix"))
            for c in range(PROJ):
                proj_pe(pe, 0, c)
            with loop(pe, 4) as i:
                da_pe(pe, i)
            with loop(pe, 3) as j:
                sb_pe(pe, j, False)
            sb_pe(pe, 3, True)
            gemm_pe(pe, "wo", UNIT_PANELS, 8, pair(in_u, in_y), "y1")
            norm_pe(pe, "mem", MEM, m_sq)
            gemm_pe(pe, "xk", UNIT_PANELS + 8, 8, mem_split, "mem", width=MEM)
            norm_pe(pe, "x", T, x_sq)
            gemm_pe(pe, "xv", UNIT_PANELS + 16, 8, mem_split, "mem", width=MEM, token_major=True)
            gemm_pe(pe, "xq", UNIT_PANELS + 24, 8, pair(in_u, in_y), "x")
            with loop(pe, 4) as i:
                x_pe(pe, i)
            gemm_pe(pe, "xo", UNIT_PANELS + 32, 8, pair(in_u, in_y), "y2")
            norm_pe(pe, "mlp", T, f_sq)
            pe.wait_ge(*split_ready("mlp"))
            with loop(pe, 4) as g:
                mlp_pe(pe, g)
            norm_pe(pe, "fin", T, ul)
            norm_pe(pe, "pre", T, ul)
            pe.wait_ge(*split_ready("u2"))
            for q in range(12):
                p2_pe(pe, q)
            swa_pe(pe)
            gla_pe(pe, BETWEEN)
            for q in range(44, 48):
                p2_pe(pe, q)
            rw_pre_pe(pe)
            pe.wait_ge(S("lora_out"), 4)
            pe.wait_ge(S("rkv_mixed"), 6)
            pe.wait_ge(S("p2_evac"), 48)
            for u in range(4):
                rw_pe(pe, u)
            pe.wait_ge(*split_ready("y3"))
            gemm_pe(pe, "out2", G2 + 24, 8, pair(in_h, in_y), "y3")
            norm_pe(pe, "post", T, f_sq)


def columns(v):
    v = np.asarray(v).reshape(-1)
    return v.reshape(-1, P).T


def panels(w, starts):
    w = np.asarray(w).reshape(KC, P, -1)
    return [w[:, :, s:s + P].transpose(1, 0, 2).reshape(P, KC * P) for s in starts]


def lay_out(inputs):
    g = {k: np.asarray(v) for k, v in inputs.items()}
    vec = {}
    for name, key in [("g_mix", "g_mix"), ("g_cross", "g_cross"), ("g_mem", "g_mem"), ("g_mlp", "g_mlp"),
                      ("g_final", "g_final"), ("norm_pre", "norm_pre_2"), ("norm_post", "norm_post_2"),
                      ("g_subln", "g_subln"), ("c", "c_2"), ("ada_b", "ada_b_2"), ("mu_w", "rwkv_mu_w_2"),
                      ("mu_a", "rwkv_mu_a_2"), ("mu_rkv", "rwkv_mu_rkv_2"), ("w0", "rwkv_w0_2"), ("a0", "rwkv_a0_2"),
                      ("k_k", "rwkv_k_k_2"), ("k_a", "rwkv_k_a_2"), ("r_k", "rwkv_r_k_2"), ("ln_w", "rwkv_ln_w_2"),
                      ("ln_b", "rwkv_ln_b_2"), ("gk_b", "gla_gk_b_2")]:
        vec[name] = columns(g[key])
    n = g["gla_norm_w_2"].reshape(-1)
    vec["gla_norm"] = np.concatenate([n, n])[:, None]
    lam = np.zeros((P, 4), np.float32)
    for x, key in enumerate(["lambda_q1", "lambda_k1", "lambda_q2", "lambda_k2"]):
        lam[:64, x] = g[key].reshape(-1)
    vec["lam"] = lam
    order = [4 * x + 2 * c + par for x in range(2) for par in range(2) for c in range(2)]
    vec["sinks"] = np.broadcast_to(g["attn_sinks_2"].reshape(-1)[order][None, :], (P, 8))
    wa = np.concatenate([g["rwkv_w1_2"][0], g["rwkv_a1_2"][0]], axis=1)
    gk2 = np.concatenate([g["gla_gk2_2"][0], np.zeros((P - 16, P), np.float32)], axis=0)
    lora = np.concatenate([wa.reshape(KC, P, P).transpose(1, 0, 2).reshape(P, -1),
                           g["gla_gk1_2"][0].reshape(KC, P, 16).transpose(1, 0, 2).reshape(P, -1), gk2,
                           np.concatenate([g["rwkv_w2_2"][0], g["rwkv_a2_2"][0]], axis=0)], axis=1)
    vec_a = np.concatenate([vec[name] for name in VEC], axis=1)
    win = g["w_in"][0]
    adaw = g["ada_w_2"][0]
    w = []
    for u in range(UNITS):
        first, n = (0, u) if u < 4 else (1536, u - 4)
        for s in range(3):
            w += panels(win, [first + 512 * s + n * P]) + panels(adaw, [(3 * u + s) * P])
    every = range(0, D, P)
    w += panels(g["w_out"][0], every)
    w += panels(g["w_xkv"][0], range(0, 2 * D, P))
    w += panels(g["w_xq"][0], every)
    w += panels(g["w_xo"][0], every)
    for f in range(4):
        w += panels(g["w_up"][0], range(f * D, (f + 1) * D, P))
        w += panels(g["w_down"][0][f * D:(f + 1) * D], every)
    w2 = g["w_in_2"][0]
    w += panels(w2, [P * b for b in SECOND_ORDER])
    w += panels(g["w_out_2"][0], every)

    def feature_major(a):
        return a.T.reshape(KC, P, -1).transpose(1, 0, 2)

    return {
        "xT": np.ascontiguousarray(feature_major(g["x"][0])),
        "memT": np.ascontiguousarray(feature_major(g["mem"][0])),
        "pos": np.ascontiguousarray(np.broadcast_to(g["positions"].reshape(1, T), (P, T))),
        "vec": np.ascontiguousarray(vec_a),
        "const": constants(),
        "bias": window_bias(),
        "lora": np.ascontiguousarray(lora),
        "w": np.ascontiguousarray(np.stack(w)),
    }


SECOND_ORDER = [0, 1, 2, 3, 4, 5, 18, 19, 20, 21, 10, 11, 12, 13, 14, 15, 6, 7, 8, 9, 16, 17, 22, 23]


def kernel(**inputs):
    import concourse.bacc as bacc
    from concourse.bass_utils import run_bass_kernel_spmd

    arrays = lay_out(inputs)
    nc = bacc.Bacc("TRN2", target_bir_lowering=False, num_devices=1)
    args = [nc.dram_tensor("in_" + n, a.shape, mybir.dt.from_np(a.dtype), kind="ExternalInput").ap() for n, a in arrays.items()]
    args.append(nc.dram_tensor("out_0", (P, KC, T), mybir.dt.float32, kind="ExternalOutput").ap())
    program(nc, *args)
    r = run_bass_kernel_spmd(nc, [{"in_" + n: a for n, a in arrays.items()}], core_ids=[0])
    o = r.results[0]["out_0"]
    return o.transpose(1, 0, 2).reshape(D, T).T.reshape(1, T, D)
```

```python
import concourse.bass as bass
from concourse import mybir
from concourse.alu_op_type import AluOpType as ALU
from contextlib import ExitStack
import numpy as np

P = 128
D = 1024
T = 1024
KC = D // P
NT = T // P
HALF = 512
MEM = 256
EPS = 1e-6
NEG = -1e30
LAM_INIT = 0.2
UNITS = 8
CREDIT = 2
PAD = 8

VEC = {}
for _name, _n in [("g_mix", 8), ("g_cross", 8), ("g_mem", 8), ("g_mlp", 8), ("g_final", 8),
                  ("norm_pre", 8), ("norm_post", 8), ("g_subln", 1), ("c", 8), ("ada_b", 24),
                  ("mu_w", 8), ("mu_a", 8), ("mu_rkv", 6), ("w0", 2), ("a0", 2), ("k_k", 2), ("k_a", 2),
                  ("r_k", 2), ("ln_w", 2), ("ln_b", 2), ("gk_b", 1), ("gla_norm", 1),
                  ("lam", 4), ("sinks", 8)]:
    VEC[_name] = (sum(n for _, n in VEC.values()), _n)
NVEC = sum(n for _, n in VEC.values())

CONST = {}
for _name, _n in [("ident", 128), ("ones", 128), ("blk64", 128), ("neg_tri", 128), ("neg_ones", 128),
                  ("rot", 128), ("da_mask", 128), ("sb_mask", 128), ("sb_strict", 128),
                  ("level", 7 * 128), ("strict64", 128), ("incl64", 128), ("first_low", 128), ("gla_state", 256), ("ident64", 64),
                  ("inv_freq", 1), ("eps", 1), ("half_pi", 1), ("zero", 1), ("eps5", 1), ("eps_ln", 1)]:
    CONST[_name] = (sum(n for _, n in CONST.values()), _n)
NCONST = sum(n for _, n in CONST.values())


def constants():
    i = np.arange(P)
    c = np.zeros((P, NCONST), np.float32)

    def put(name, a):
        o, n = CONST[name]
        c[:, o:o + n] = a

    put("ident", np.eye(P))
    put("ones", 1.0)
    put("blk64", (i[:, None] // 64) == (i[None, :] // 64))
    put("neg_tri", -1.0 * (i[:, None] >= i[None, :]))
    put("neg_ones", -1.0)
    rot = np.zeros((P, P))
    for b in (0, 64):
        for m in range(8):
            rot[b + m + 8, b + m] = -1.0
            rot[b + m, b + m + 8] = 1.0
    put("rot", rot)
    put("da_mask", NEG * (i[None, :] > i[:, None]))
    put("sb_mask", NEG * (i[:, None] >= i[None, :]))
    put("sb_strict", i[:, None] < i[None, :])
    f = np.zeros(P, np.float32)
    for b in (0, 64):
        for m in range(16):
            f[b + m] = np.float32(500000.0) ** np.float32(-(2.0 * (m % 8)) / 16.0)
    j, t = i[:, None], i[None, :]
    put("level", np.concatenate([(j >> (l + 1) == t >> (l + 1)) & (j >> l & 1 == 0) & (t >> l & 1 == 1)
                                 for l in range(7)], axis=1))
    put("strict64", (j // 64 == t // 64) & (j < t))
    put("incl64", (j // 64 == t // 64) & (j <= t))
    put("first_low", (j >> 1 == t >> 1) & (j & 1 == 1) & (t & 1 == 0))
    put("ident64", i[:, None] % 64 == np.arange(64)[None, :])
    put("gla_state", (i[:, None] // 32) == (np.arange(256)[None, :] // 64))
    put("inv_freq", f[:, None])
    put("eps", EPS)
    put("half_pi", np.pi / 2)
    put("eps5", 1e-5)
    put("eps_ln", 64e-5)
    return c


def window_bias():
    q, k = np.arange(P)[:, None], np.arange(2 * P)[None, :]
    dist = q - k + P
    b = np.zeros((P, 8, 2 * P), np.float32)
    for g in range(2):
        for par in range(2):
            for c in range(2):
                head = 4 * g + 2 * c + par
                slope = np.float32(2.0) ** np.float32(-8.0 * (head + 1) / 8)
                b[:, 4 * g + 2 * par + c] = np.where((dist >= 0) & (dist < P), -slope * dist.astype(np.float32), NEG)
    return b.reshape(P, 8 * 2 * P)


def program(nc, xT_d, memT_d, pos_d, vec_d, const_d, bias_d, lora_d, w_d, out_d):
    F = mybir.dt.float32
    R = mybir.dt.float32r
    I32 = mybir.dt.int32
    ACT = mybir.ActivationFunctionType
    AX = mybir.AxisListType.X
    ctx = ExitStack()
    with ctx:
        def sb(name, shape, dt=F):
            return ctx.enter_context(nc.sbuf_tensor(name, shape, dt))

        def with_rounded(name, shape):
            n = 4 * int(np.prod(shape[1:]))
            t = ctx.enter_context(nc.sbuf_tensor(name, shape, F, align_bytes=64))
            at = nc.sbuf_base - n
            return t, nc.alloc_sbuf_tensor_at(name + "_r", shape, R, offset=at)

        sems = {}

        def S(name):
            if name not in sems:
                sems[name] = ctx.enter_context(nc.semaphore(name))
            return sems[name]

        PS = ctx.enter_context(nc.psum_tensor("PS", [P, 8 * HALF], F))

        def bank(b, n=1):
            return PS[:, b * HALF:(b + n) * HALF]

        const = sb("const", [P, NCONST])
        vec = sb("vec", [P, NVEC])

        def cst(name):
            o, n = CONST[name]
            return const[:, o:o + n]

        def vcol(name, j=0):
            return vec[:, VEC[name][0] + j:VEC[name][0] + j + 1]

        h_all, h_r = with_rounded("h", [P, KC, PAD + T])
        u_all, u_r = with_rounded("u", [P, KC, PAD + T])
        y_all, y_r = with_rounded("y", [P, KC, T])
        hT, uT, yT = h_all[:, :, PAD:PAD + T], u_all[:, :, :], y_all[:, :, :]
        NS = 4
        w_raw = sb("w_raw", [P, 2, D])
        w_hi, w_lo = sb("w_hi", [P, 2, D], R), sb("w_lo", [P, 2, D], R)
        small = sb("small", [P, 64])
        ada = sb("ada", [P, 24])
        pos_i = sb("pos_i", [P, T], I32)
        pos_f = pos_i[:, :].bitcast(F)
        arena_t, arena_rt = with_rounded("arena", [P, 17472])
        arena, arena_r = arena_t[:, :], arena_rt[:, :]

        def U(k, lo=0, hi=T):
            return uT[:, k, PAD + lo:PAD + hi]

        def pair(high, low):
            return lambda k, lo, hi: (high(k, lo, hi), low(k, lo, hi))

        def in_u(k, lo, hi):
            return u_r[:, k, PAD + lo:PAD + hi]

        def in_h(k, lo, hi):
            return h_r[:, k, PAD + lo:PAD + hi]

        def in_y(k, lo, hi):
            return y_r[:, k, lo:hi]

        def product(pe, out, a, b, start, stop):
            first = pe.matmul(out, a[0], b[0], start=start, stop=False)
            pe.matmul(out, a[0], b[1], start=False, stop=False)
            return first, pe.matmul(out, a[1], b[0], start=False, stop=stop)

        def high(e, out, x):
            return e.activation(out, x, ACT.Copy)

        def low(e, out, x, hi_part):
            return e.tensor_tensor(out, x, hi_part.bitcast(F), ALU.subtract)

        class Arena:

            def __init__(self):
                self.at = 0

            def take(self, n):
                self.at += n
                assert self.at <= 17472, self.at
                return arena[:, self.at - n:self.at]

        def W(g, k):
            return w_hi[:, g % 2, k * P:(k + 1) * P], w_lo[:, g % 2, k * P:(k + 1) * P]


        w_in = [S("w_in0"), S("w_in1")]
        UNIT_MAIN = 3 * UNITS
        LATER = w_d.shape[0] - 2 * UNIT_MAIN

        def panel_in(pe, m):
            pe.wait_ge(S("w_split"), m + (1 + CREDIT))

        def split_panel(pool, m, raw, came, place):
            pool.wait_ge(w_in[raw], 16 * came + 16)
            pool.tensor_tensor(w_hi[:, place, :], w_raw[:, raw, :], cst("ones")[:, 0:1].broadcast_to([P, D]), ALU.mult)\
                .then_inc(S("w_high"), 1)
            pool.wait_ge(S("w_high"), m + 1)
            low(pool, w_lo[:, place, :], w_raw[:, raw, :], w_hi[:, place, :]).then_inc(S("w_split"), 1)

        def split_unit_panel(pool, u, what):
            if what == "next q":
                pool.wait_ge(S("proj_mm"), PROJ * u + 8)
                split_panel(pool, 3 * u + 3, 0, 3 * u + 3, 0)
            else:
                s = 1 if what == "k" else 2
                pool.wait_ge(S("weight_free"), 3 * u + (s + CREDIT))
                split_panel(pool, 3 * u + s, 0, 3 * u + s, s % 2)

        def split_later_panel(pool, two, x):
            pool.wait_ge(S("weight_free"), 2 * two + (UNIT_MAIN + x + CREDIT))
            split_panel(pool, 2 * two + (UNIT_MAIN + x), x, two + UNIT_MAIN, x)

        SMALL_GK, SMALL_WA = 1, 3

        def loop(e, n):
            return e.Fori(0, n)

        NB = 6 * HALF
        NORMS = {n: m for m, n in enumerate(["mix", "mem", "x", "mlp", "fin", "pre", "post"])}
        NORM_PIECES = {"mix": 2 * KC, "mem": KC, "x": 2 * KC, "mlp": 2 * KC, "fin": KC, "pre": 2 * KC, "post": KC}

        def norm_out(n, k):
            return S("norm_out"), sum(NORM_PIECES[x] for x in NORMS if NORMS[x] < NORMS[n]) + k

        def norm_act(act, n, src, width, sq, rs, ready):
            norm_squares(act, n, src, width, sq, ready)
            norm_rstd(act, n, width, rs)

        def norm_squares(act, n, src, width, sq, ready):
            m = NORMS[n]
            act.preload_act_table_set("natural_log_exp_and_others")
            for k in range(KC):
                for sem, v in ready(k):
                    act.wait_ge(sem, v)
                if k >= sq.shape[1]:
                    act.wait_ge(S("norm_sq_summed"), KC * m + k + 1 - sq.shape[1])
                act.activation(sq[:, k % sq.shape[1], :width], src(k), ACT.Square).then_inc(S("norm_sq_ready"), 1)

        def norm_rstd(act, n, width, rs):
            m = NORMS[n]
            act.wait_ge(S("norm_sq_summed"), KC * m + KC)
            act.activation(rs[:, :width], PS[:, NB:NB + width], ACT.Ln, bias=cst("eps"), scale=1.0 / D)\
               .then_inc(S("norm_log"), 1)
            act.wait_ge(S("norm_log"), m + 1)
            act.activation(rs[:, :width], rs[:, :width], ACT.Exp, scale=-0.5).then_inc(S("norm_rstd"), 1)

        def norm_pe(pe, n, width, sq):
            m = NORMS[n]
            for k in range(KC):
                pe.wait_ge(S("norm_sq_ready"), KC * m + k + 1)
                for h in range(0, width, HALF):
                    w = min(HALF, width)
                    mm = pe.matmul(PS[:, NB + h:NB + h + w], cst("ones"), sq[:, k % sq.shape[1], h:h + w],
                                  start=(k == 0), stop=(k == KC - 1))
                mm.then_inc(S("norm_sq_summed"), 1)

        def norm_dve(dve, n, src, dst, gain, width, rs):
            m = NORMS[n]
            dve.wait_ge(S("norm_rstd"), m + 1)
            for k in range(KC):
                dve.scalar_tensor_tensor(dst(k), src(k), gain(k), rs[:, :width], ALU.mult, ALU.mult)\
                   .then_inc(S("norm_out"), 1)

        SPLIT_PIECES = {"mix": 2 * KC, "y1": 2 * KC, "mem": KC, "x": 2 * KC, "y2": 2 * KC, "mlp": 2 * KC, "u2": 2 * KC, "y3": KC}

        def split_from(n):
            names = list(SPLIT_PIECES)
            return sum(SPLIT_PIECES[x] for x in names[:names.index(n)])

        def split_ready(n, pieces=None):
            return S("split_low"), split_from(n) + (SPLIT_PIECES[n] if pieces is None else pieces)

        def wait_split(pe, n, h):
            return lambda k: pe.wait_ge(*split_ready(n, KC * h + k + 1))

        def split_act(act, n, src, hi_place, ready, width=T, shift=None):
            for h in range(SPLIT_PIECES[n] // KC):
                lo, hi = h * HALF, min(width, (h + 1) * HALF)
                for k in range(KC):
                    act.wait_ge(*ready(KC * h + k + 1, k))
                    if shift is None:
                        high(act, hi_place(k, lo, hi), src(k, lo, hi)).then_inc(S("split_high"), 1)
                    else:
                        act.activation(hi_place(k, lo, hi), src(k, lo, hi), ACT.Identity, bias=shift(k)).then_inc(S("split_high"), 1)

        def split_dve(dve, n, src, hi_place, lo_place, width=T, norm=None, shift=None):
            for h in range(SPLIT_PIECES[n] // KC):
                lo, hi = h * HALF, min(width, (h + 1) * HALF)
                for k in range(KC + 1):
                    if norm is not None and k < KC:
                        dve.scalar_tensor_tensor(src(k, lo, hi), norm[0](k, lo, hi), norm[1](k), norm[2][:, lo:hi], ALU.mult, ALU.mult)\
                           .then_inc(S("norm_out"), 1)
                    if k >= 1:
                        dve.wait_ge(S("split_high"), split_from(n) + KC * h + k)
                        hi_part = hi_place(k - 1, lo, hi)
                        if shift is None:
                            low(dve, lo_place(k - 1, lo, hi), src(k - 1, lo, hi), hi_part).then_inc(S("split_low"), 1)
                        else:
                            dve.scalar_tensor_tensor(lo_place(k - 1, lo, hi), src(k - 1, lo, hi), shift(k - 1), hi_part.bitcast(F),
                                                     ALU.add, ALU.subtract).then_inc(S("split_low"), 1)

        def norm_split_dve(dve, n, source, src, gain, rs, hi_place, lo_place, operand, width=T, shift=None):
            dve.wait_ge(S("norm_rstd"), NORMS[n] + 1)
            split_dve(dve, operand, src, hi_place, lo_place, width, (source, gain, rs), shift)

        def in_(t):
            return lambda k, lo, hi: t[:, k, lo:hi]

        def chunk_product(pe, g, b, x, h, width=T, ready=None):
            w = min(width, HALF)
            for k in range(KC):
                if ready is not None:
                    ready(k)
                f, m = product(pe, b[:, :w], W(g, k), x(k, h * HALF, h * HALF + w), k == 0, k == KC - 1)
                if h == 0 and k == 0:
                    f.then_inc(S("weight_free"), 1)
            return m

        def panel_product(pe, n, g, banks, evac_from, x, width, operand):
            for h in range(max(1, width // HALF)):
                pe.wait_ge(S(n + "_evac"), evac_from + h)
                chunk_product(pe, g, banks[h], x, h, width, ready=wait_split(pe, operand, h) if operand else None)\
                    .then_inc(S(n + "_mm"), 1)

        def gemm_banks(j, halves):
            return [bank((halves * j + h) % 4) for h in range(halves)]

        def gemm_pe(pe, n, g0, count, x, operand, width=T):
            halves = max(1, width // HALF)
            with loop(pe, count // NS) as i:
                for j in range(NS):
                    panel_in(pe, NS * i + (g0 + j))
                    panel_product(pe, n, g0 + j, gemm_banks(j, halves), halves * (NS * i + j) + 1, x, width,
                                  operand=operand if j == 0 else None)

        def gemm_evac(e, n, count, width, one, done=0):
            halves = max(1, width // HALF)
            with loop(e, count // NS) as i:
                for j in range(NS):
                    for h in range(halves):
                        e.wait_ge(S(n + "_mm"), halves * (NS * i + j + done) + h + 1)
                        one(i, j, h, gemm_banks(j, halves)[h][:, :min(width, HALF)])

        def add_to_h(dve, n):
            def one(i, j, h, b):
                dst = hT[:, bass.ds(NS * i + j, 1), h * HALF:(h + 1) * HALF].rearrange("p o t -> p (o t)")
                dve.tensor_tensor(dst, dst, b, ALU.add).then_inc(S(n + "_evac"), 1)
            return one

        ar = Arena()
        raw = ar.take(6 * HALF).rearrange("p (c t) -> p c t", c=6)
        qh, kh = ar.take(T), ar.take(T)
        Vh = ar.take(T).rearrange("p (t f) -> p t f", t=NT)
        cosT, sinT = ar.take(T), ar.take(T)
        at_da = ar.at
        Pr = ar.take(4 * T).rearrange("p (b c t) -> p b c t", b=2, c=2)
        wgt = ar.take(2 * T).rearrange("p (b t) -> p b t", b=2)
        wgtT = ar.take(T)
        oT, osq = ar.take(T), ar.take(T)
        tmp = Pr[:, 0, 0, :]
        n_sq = arena[:, at_da:at_da + 2 * T].rearrange("p (b t) -> p b t", b=2)
        n_rs = arena[:, at_da + 2 * T:at_da + 3 * T]
        ang, turns, posf = (arena[:, at_da + (3 + m) * T:at_da + (4 + m) * T] for m in range(3))
        nm = sb("nm", [P, 16])
        el = sb("el", [P, 16])
        er = sb("er", [P, 16])
        lamt = sb("lamt", [P, 8])
        gsub = sb("gsub", [P, 1])
        cact = sb("cact", [P, KC])

        CHUNKS = [("q", 0), ("q", 1), ("ada", 0), ("k", 0), ("k", 1), ("ada", 1), ("v", 0), ("v", 1), ("ada", 2)]
        PROJ = len(CHUNKS)
        UNIT_PANEL = {"q": 0, "k": 1, "v": 2}
        u_mix = pair(in_u, in_h)

        def proj_pe(pe, u, c):
            pe.wait_ge(S("proj_evac"), PROJ * u + max(1, c))
            what, h = CHUNKS[c]
            b = bank(c % 2)
            if what == "ada":
                pe.wait_ge(w_in[1], 48 * u + 16 * (h + 1))
                for k in range(KC):
                    m = pe.matmul(b[:, 0:1], w_raw[:, 1, k * P:(k + 1) * P], cact[:, k:k + 1], start=(k == 0), stop=(k == KC - 1))
            else:
                if h == 0:
                    panel_in(pe, 3 * u + UNIT_PANEL[what])
                first = isinstance(u, int) and what == "q"
                m = chunk_product(pe, UNIT_PANEL[what], b, u_mix, h, ready=wait_split(pe, "mix", h) if first else None)
            m.then_inc(S("proj_mm"), 1)

        def proj_act(act, u, c):
            act.wait_ge(S("proj_mm"), PROJ * u + c + 1)
            what, h = CHUNKS[c]
            if what == "ada":
                act.activation(ada[:, bass.ds(3 * u + h, 1)] if not isinstance(u, int) else ada[:, 3 * u + h:3 * u + h + 1],
                               bank(c % 2)[:, 0:1], ACT.Copy).then_inc(S("proj_evac"), 1)
            else:
                act.activation(raw[:, 2 * UNIT_PANEL[what] + h, :], bank(c % 2), ACT.Copy, scale=0.125 if what == "q" else 1.0)\
                   .then_inc(S("proj_evac"), 1)

        def rounds(t):
            return t if t <= 4 else 4 + 2 * (t - 4)

        def turn_tiles(pe, b, src, n=4):
            for t in range(n):
                m = pe.transpose(bank(b)[:, t * P:(t + 1) * P], src[:, t * P:(t + 1) * P], cst("ident"))
            return m

        V_MEM, V_WINDOW, V_LINEAR = UNITS + 1, UNITS + 2, UNITS + 3

        def turn_values(pe):
            for h in range(2):
                m = turn_tiles(pe, 6 + h, raw[:, 4 + h, :])
            m.then_inc(S("v_turned"), 1)

        DA_STEP = {1: [1], 2: [2], 3: [3], 4: [4, 5], 6: [6], 7: [7], 8: [8]}

        def da_pe(pe, i):
            pe.wait_ge(S("proj_evac"), PROJ * i + 6)
            for x in range(2):
                for h in range(2):
                    m = pe.matmul(bank(2 + 2 * x + h), cst("rot"), raw[:, 2 * x + h, :], start=True, stop=True)
                m.then_inc(S("rot_ready"), 1)
            pe.wait_ge(S("proj_evac"), PROJ * i + 9)
            pe.wait_ge(S("olog_ready"), i + 1)
            turn_values(pe)
            proj_pe(pe, i + 1, 0)
            pe.wait_ge(S("qk_ready"), 2 * i + 2)

            def scores(s):
                kw = (s + 1) * P
                for c in range(2):
                    if s >= 1:
                        pe.wait_ge(S("exp_done"), 16 * i + 2 * (s - 1) + c + 1)
                    r = slice(64 * c, 64 * c + 64)
                    b = bank(2 + 2 * c, 2)
                    for lo in range(0, kw, HALF):
                        hi = min(kw, lo + HALF)
                        m = pe.matmul(b[:, lo:hi], qh[r, s * P:(s + 1) * P], kh[r, lo:hi], start=True, stop=(hi < kw))
                    m = pe.matmul(b[:, kw - P:kw], cst("ident"), cst("da_mask"), start=False, stop=True)
                    m.then_inc(S("sc_ready"), 1)

            def turn(t, rd):
                if t == 0:
                    pe.wait_ge(S("v_ready"), i + 1)
                if rd == 0:
                    pe.wait_ge(S("w_ready"), 8 * i + t + 1)
                if rounds(t) + rd > 0:
                    pe.wait_ge(S("tr_copied"), 12 * i + rounds(t) + rd)
                for kb in range(4 * rd, min(4 * rd + 4, t + 1)):
                    m = pe.transpose(bank(6)[:, (kb % 4) * P:(kb % 4 + 1) * P], wgt[:, t % 2, kb * P:(kb + 1) * P], cst("ident"))
                m.then_inc(S("tr_ready"), 1)

            def values(t):
                pe.wait_ge(S("tr_copied"), 12 * i + rounds(t + 1))
                if t == 4:
                    pe.wait_ge(S("o_evac"), 2 * i + 1)
                for kb in range(t + 1):
                    m = pe.matmul(bank(7)[:, (t % 4) * P:(t % 4 + 1) * P], Vh[:, kb, :], wgtT[:, kb * P:(kb + 1) * P],
                                  start=(kb == 0), stop=(kb == t))
                m.then_inc(S("av_ready"), 1)

            for s in range(NT + 1):
                if s < NT:
                    scores(s)
                if s >= 2:
                    values(s - 2)
                if s < NT:
                    for c in DA_STEP.get(s, []):
                        proj_pe(pe, i + 1, c)
                if s >= 1:
                    turn(s - 1, 0)
                if s >= 5:
                    turn(s - 1, 1)
            for c in DA_STEP[NT]:
                proj_pe(pe, i + 1, c)
            values(NT - 1)
            pe.wait_ge(S("osq_ready"), i + 1)
            for h in range(2):
                m = pe.matmul(bank(6 + h), cst("ones"), osq[:, h * HALF:(h + 1) * HALF], start=True, stop=True)
            m.then_inc(S("osum_ready"), 1)

        def da_act(act, i):
            act.preload_act_table_set("natural_log_exp_and_others")
            act.wait_ge(S("v_turned"), i + 1)
            act.activation(Vh[:, :, :].rearrange("p t f -> p (t f)"), bank(6, 2), ACT.Copy).then_inc(S("v_ready"), 1)

            def exps(s):
                kw = (s + 1) * P
                for c in range(2):
                    if s >= 2:
                        act.wait_ge(S("w_ready"), 8 * i + s - 1)
                    act.wait_ge(S("nmax_ready"), 16 * i + 2 * s + c + 1)
                    act.activation(Pr[:, s % 2, c, :kw], bank(2 + 2 * c, 2)[:, :kw], ACT.Exp, bias=nm[:, 2 * s + c:2 * s + c + 1],
                                   accum_out=el[:, 2 * s + c:2 * s + c + 1]).then_inc(S("exp_done"), 1)

            def copy_turned(t, rd):
                n = min(4, t + 1 - 4 * rd) * P
                act.wait_ge(S("tr_ready"), 12 * i + rounds(t) + rd + 1)
                act.activation(wgtT[:, 4 * P * rd:4 * P * rd + n], bank(6)[:, :n], ACT.Copy).then_inc(S("tr_copied"), 1)

            def take_o(h):
                act.wait_ge(S("av_ready"), 8 * i + 4 * h + 4)
                act.activation(oT[:, h * HALF:(h + 1) * HALF], bank(7), ACT.Copy).then_inc(S("o_evac"), 1)

            act.wait_ge(S("qk_ready"), 2 * i + 2)
            proj_act(act, i + 1, 0)
            for s in range(NT + 1):
                if s < NT:
                    exps(s)
                if s == 5:
                    take_o(0)
                if s < NT:
                    for c in DA_STEP.get(s, []):
                        proj_act(act, i + 1, c)
                if s >= 1:
                    copy_turned(s - 1, 0)
                if s >= 5:
                    copy_turned(s - 1, 1)
            for c in DA_STEP[NT]:
                proj_act(act, i + 1, c)
            take_o(1)
            act.wait_ge(S("o_evac"), 2 * i + 2)
            act.activation(osq, oT, ACT.Square).then_inc(S("osq_ready"), 1)
            act.wait_ge(S("osum_ready"), i + 1)
            act.activation(osq, bank(6, 2), ACT.Ln, bias=cst("eps"), scale=1.0 / P).then_inc(S("olog_ready"), 1)
            act.wait_ge(S("olog_ready"), i + 2)
            act.activation(osq, osq, ACT.Exp, scale=-0.5).then_inc(S("orstd_ready"), 1)

        def da_dve(dve, i):
            for x, dst in enumerate((qh, kh)):
                src = raw[:, 2 * x:2 * x + 2, :].rearrange("p c t -> p (c t)")
                dve.wait_ge(S("rot_ready"), 2 * i + x + 1)
                dve.tensor_tensor(dst, src, cosT, ALU.mult).then_inc(S("rope_part"), 1)
                dve.tensor_tensor(tmp, bank(2 + 2 * x, 2), sinT, ALU.mult).then_inc(S("rope_part"), 1)
                dve.wait_ge(S("rope_part"), 4 * i + 2 * x + 2)
                dve.tensor_tensor(dst, dst, tmp, ALU.add).then_inc(S("qk_ready"), 1)
                dve.wait_ge(S("qk_ready"), 2 * i + x + 1)

            def maxima(s):
                for c in range(2):
                    dve.wait_ge(S("sc_ready"), 16 * i + 2 * s + c + 1)
                    dve.reduce_max(nm[:, 2 * s + c:2 * s + c + 1], bank(2 + 2 * c, 2)[:, :(s + 1) * P], AX,
                                   negate=True).then_inc(S("nmax_ready"), 1)

            def weights(t):
                kw = (t + 1) * P
                dve.wait_ge(S("exp_done"), 16 * i + 2 * t + 2)
                dve.reciprocal(er[:, 2 * t:2 * t + 2], el[:, 2 * t:2 * t + 2]).then_inc(S("recip_ready"), 1)
                dve.wait_ge(S("recip_ready"), 8 * i + t + 1)
                dve.tensor_scalar(Pr[:, t % 2, 1, :kw], Pr[:, t % 2, 1, :kw], er[:, 2 * t + 1:2 * t + 2], lamt[:, 5:6],
                                  ALU.mult, ALU.mult).then_inc(S("w_part"), 1)
                dve.wait_ge(S("w_part"), 8 * i + t + 1)
                if t >= 2:
                    dve.wait_ge(S("tr_ready"), 12 * i + rounds(t - 1))
                dve.scalar_tensor_tensor(wgt[:, t % 2, :kw], Pr[:, t % 2, 0, :kw], er[:, 2 * t:2 * t + 1],
                                         Pr[:, t % 2, 1, :kw], ALU.mult, ALU.add).then_inc(S("w_ready"), 1)

            for s in range(NT + 1):
                if s < NT:
                    maxima(s)
                if s >= 1:
                    weights(s - 1)
            dve.wait_ge(S("orstd_ready"), i + 1)
            dve.scalar_tensor_tensor(yT[:, bass.ds(i, 1), :].rearrange("p o t -> p (o t)"), oT, gsub[:, 0:1], osq,
                                     ALU.mult, ALU.mult).then_inc(S("da_y_ready"), 1)

        ar = Arena()
        ar.at = at_da - 2 * T
        Rs = ar.take(2 * T).rearrange("p (h t) -> p h t", h=2)
        ab = ar.take(2 * T).rearrange("p (b t) -> p b t", b=2)
        sp = ar.take(2 * T).rearrange("p (b t) -> p b t", b=2)
        Aw = ar.take(2 * T).rearrange("p (b t) -> p b t", b=2)

        def sb_block(n):
            kb = NT - 1 - n // 2
            return kb, n % 2, T - kb * P

        def pieces(lo, hi):
            return [(a, min(a + HALF, hi)) for a in range(lo, hi, HALF)]

        SB_STEP = {4: 1, 5: 2, 6: 3, 8: 4, 9: 5, 10: 6, 12: 7, 13: 8}

        def sb_pe(pe, j, last):
            if not last:
                proj_pe(pe, j + 5, 0)
            pe.wait_ge(S("proj_evac"), PROJ * (j + 4) + 9)
            pe.wait_ge(S("sb_qkv"), 3 * j + 2)
            turn_values(pe)
            for s in range(18):
                if not last and s in (5, 9, 13):
                    proj_pe(pe, j + 5, SB_STEP[s])
                if s < 16:
                    kb, hd, w = sb_block(s)
                    if s >= 2:
                        pe.wait_ge(S("sb_a"), 16 * j + s - 1)
                    r = slice(64 * hd, 64 * hd + 64)
                    for lo, hi in pieces(0, w):
                        m = pe.matmul(bank(2 + 2 * (s % 2), 2)[:, lo:hi], kh[r, kb * P:(kb + 1) * P],
                                      qh[r, kb * P + lo:kb * P + hi], start=True, stop=True)
                    m.then_inc(S("sb_z"), 1)
                if not last and s % 2 == 0 and s in SB_STEP:
                    proj_pe(pe, j + 5, SB_STEP[s])
                if 1 <= s <= 16:
                    n = s - 1
                    kb, hd, w = sb_block(n)
                    b = bank(2 + 2 * (n % 2), 2)
                    pe.wait_ge(S("sb_sp"), 16 * j + n + 1)
                    for lo, hi in pieces(0, w):
                        pe.matmul(b[:, lo:hi], cst("neg_tri"), sp[:, n % 2, lo:hi], start=False, stop=True,
                                  skip_group_check=True)
                    if n >= 2:
                        pe.wait_ge(S("sb_sum"), 14 * j + n - 1)
                        for lo, hi in pieces(0, w):
                            lo = max(lo, P)
                            pe.matmul(b[:, lo:hi], cst("neg_ones"), Rs[:, hd, kb * P + lo:kb * P + hi],
                                      start=False, stop=True, skip_group_check=True)
                    pe.matmul(b[:, :P], cst("ident"), cst("sb_mask"), start=False, stop=True,
                              skip_group_check=True).then_inc(S("sb_e"), 1)
                if s >= 2:
                    n = s - 2
                    kb, hd, w = sb_block(n)
                    if n == 0:
                        pe.wait_ge(S("sb_qkv"), 3 * j + 3)
                    pe.wait_ge(S("sb_a"), 16 * j + n + 1)
                    for lo, hi in ((kb * P, HALF), (max(kb * P, HALF), T)):
                        if lo < hi:
                            m = pe.matmul(PS[64 * hd:64 * hd + 64, 6 * HALF + lo:6 * HALF + hi], Vh[:, kb, 64 * hd:64 * hd + 64],
                                          Aw[:, n % 2, lo - kb * P:hi - kb * P], start=(n < 2 or (lo < HALF and kb == 3)),
                                          stop=(kb == 0), skip_group_check=True)
                    m.then_inc(S("sb_av"), 1)

        def sb_act(act, j, last):
            act.preload_act_table_set("natural_log_exp_and_others")
            act.wait_ge(S("proj_evac"), PROJ * (j + 4) + 9)
            for dst, c in ((qh, 0), (kh, 2)):
                act.activation(dst, raw[:, c:c + 2, :].rearrange("p c t -> p (c t)"), ACT.Copy).then_inc(S("sb_qkv"), 1)
            act.wait_ge(S("v_turned"), j + 5)
            act.activation(Vh[:, :, :].rearrange("p t f -> p (t f)"), bank(6, 2), ACT.Copy).then_inc(S("sb_qkv"), 1)
            if not last:
                act.wait_ge(S("sb_qkv"), 3 * j + 3)
                proj_act(act, j + 5, 0)
            for s in range(17):
                if not last and s in (5, 9, 13):
                    proj_act(act, j + 5, SB_STEP[s])
                if s < 16:
                    w = sb_block(s)[2]
                    act.wait_ge(S("sb_z"), 16 * j + s + 1)
                    if s >= 2:
                        act.wait_ge(S("sb_sp_raw"), 16 * j + s - 1)
                    act.activation(ab[:, s % 2, :w], bank(2 + 2 * (s % 2), 2)[:, :w], ACT.Abs).then_inc(S("sb_abs"), 1)
                    act.wait_ge(S("sb_abs"), 16 * j + s + 1)
                    act.activation(ab[:, s % 2, :w], ab[:, s % 2, :w], ACT.Exp, scale=-1.0).then_inc(S("sb_exp"), 1)
                    act.wait_ge(S("sb_exp"), 16 * j + s + 1)
                    act.activation(ab[:, s % 2, :w], ab[:, s % 2, :w], ACT.Ln, bias=1.0).then_inc(S("sb_ln"), 1)
                if s >= 1:
                    n = s - 1
                    w = sb_block(n)[2]
                    if n >= 2:
                        act.wait_ge(S("sb_av"), 16 * j + n - 1)
                    act.wait_ge(S("sb_e"), 16 * j + n + 1)
                    act.activation(Aw[:, n % 2, :w], bank(2 + 2 * (n % 2), 2)[:, :w], ACT.Exp).then_inc(S("sb_a"), 1)
                if not last and s % 2 == 0 and s in SB_STEP:
                    proj_act(act, j + 5, SB_STEP[s])
            act.wait_ge(S("sb_av"), 16 * j + 16)
            act.activation(yT[:, bass.ds(j + 4, 1), :].rearrange("p o t -> p (o t)") if not isinstance(j, int) else yT[:, j + 4, :],
                           bank(6, 2), ACT.Copy).then_inc(S("sb_y_ready"), 1)

        def sb_dve(dve, j):
            for s in range(16):
                w = sb_block(s)[2]
                dve.wait_ge(S("sb_ln"), 16 * j + s + 1)
                if s >= 2:
                    dve.wait_ge(S("sb_sum"), 14 * j + s - 1)
                dve.scalar_tensor_tensor(sp[:, s % 2, :w], bank(2 + 2 * (s % 2), 2)[:, :w], 0.0, ab[:, s % 2, :w],
                                         ALU.max, ALU.add).then_inc(S("sb_sp_raw"), 1)
                dve.wait_ge(S("sb_sp_raw"), 16 * j + s + 1)
                dve.tensor_tensor(sp[:, s % 2, :P], sp[:, s % 2, :P], cst("sb_strict"), ALU.mult).then_inc(S("sb_sp"), 1)

        SB_SPLITS = {1: "k", 5: "v", 11: "next q"}

        def sb_pool(pool, j, last):
            pool.wait_ge(S("sb_qkv"), 3 * j + 1)
            pool.sem_inc(S("sb_zeroing"), 1)
            pool.memset(Rs[:, :, :], 0.0).then_inc(S("sb_zero"), 1)
            pool.wait_ge(S("sb_zero"), j + 1)
            for n in range(14):
                kb, hd, w = sb_block(n)
                pool.wait_ge(S("sb_e"), 16 * j + n + 1)
                pool.tensor_tensor(Rs[:, hd, kb * P:], Rs[:, hd, kb * P:], sp[:, n % 2, :w], ALU.add).then_inc(S("sb_sum"), 1)
                if not last and n in SB_SPLITS:
                    split_unit_panel(pool, j + 5, SB_SPLITS[n])
            pool.wait_ge(S("sb_sum"), 14 * j + 14)

        ar = Arena()
        mraw = ar.take(KC * MEM).rearrange("p (k t) -> p k t", k=KC)
        mT = ar.take(KC * MEM).rearrange("p (k t) -> p k t", k=KC)
        mem_split_high, mem_split_low = (in_(arena_r[:, x * KC * MEM:(x + 1) * KC * MEM].rearrange("p (k t) -> p k t", k=KC))
                                         for x in range(2))
        mem_split = pair(mem_split_high, mem_split_low)
        m_rs, x_rs = ar.take(MEM), pos_f
        KcT = ar.take(KC * MEM).rearrange("p (k t) -> p k t", k=KC)
        Vc = ar.take(2 * D).rearrange("p (t f) -> p t f", t=2)
        VcT = arena[:, ar.at:ar.at + KC * MEM].rearrange("p (k t) -> p k t", k=KC)
        qcT = ar.take(KC * T).rearrange("p (k t) -> p k t", k=KC)
        x_sq = qcT
        m_sq = KcT
        ar2 = Arena()
        kx = ar2.take(2 * MEM).rearrange("p (c t) -> p c t", c=2)
        vx = ar2.take(2 * MEM).rearrange("p (t f) -> p t f", t=2)
        Px = ar2.take(4 * MEM).rearrange("p (b q t) -> p b q t", b=2, q=2)
        pT = ar2.take(2 * T).rearrange("p (t q) -> p t q", t=2)
        assert ar2.at <= 2 * KC * MEM
        qx = uT[:, 0:2, PAD:PAD + T]

        def dyn(t, k, n, lo=0, hi=None):
            return t[:, bass.ds(k, n), lo:hi]

        def x_pe(pe, i):
            pe.wait_ge(S("x_copied"), 3 * i + 3)
            for s in range(6):
                if s < 4:
                    if s >= 2:
                        pe.wait_ge(S("x_exp"), 8 * i + 2 * s - 2)
                    for q in range(2):
                        lo = (2 * s + q) * P
                        for c in range(2):
                            m = pe.matmul(bank(s % 2)[:, q * MEM:(q + 1) * MEM], qx[:, c, lo:lo + P], kx[:, c, :],
                                          start=(c == 0), stop=(c == 1))
                    m.then_inc(S("x_scores"), 1)
                if 1 <= s <= 4:
                    t = s - 1
                    if t >= 2:
                        pe.wait_ge(S("x_tcopied"), 4 * i + t - 1)
                    pe.wait_ge(S("x_probs"), 8 * i + 2 * t + 2)
                    for kt in range(2):
                        for q in range(2):
                            m = pe.transpose(bank(2 + t % 2)[:, (2 * kt + q) * P:(2 * kt + q + 1) * P],
                                             Px[:, t % 2, q, kt * P:(kt + 1) * P], cst("ident"))
                    m.then_inc(S("x_turned"), 1)
                if s in (3, 5):
                    h = s // 4
                    pe.wait_ge(S("x_tcopied"), 4 * i + 2 * h + 2)
                    if h == 1:
                        pe.wait_ge(S("x_o_evac"), 4 * i + 2)
                    for dc in range(2):
                        for kt in range(2):
                            m = pe.matmul(bank(4 + dc), vx[:, kt, dc * P:(dc + 1) * P], pT[:, kt, h * HALF:(h + 1) * HALF],
                                          start=(kt == 0), stop=(kt == 1))
                        m.then_inc(S("x_o_mm"), 1)

        def x_act(act, i):
            act.activation(qx, dyn(qcT, 2 * i, 2), ACT.Copy).then_inc(S("x_copied"), 1)
            act.activation(kx, dyn(KcT, 2 * i, 2), ACT.Copy).then_inc(S("x_copied"), 1)
            act.activation(vx, Vc[:, :, bass.ds(i * MEM, MEM)], ACT.Copy).then_inc(S("x_copied"), 1)

            def turned(t):
                act.wait_ge(S("x_turned"), 4 * i + t + 1)
                act.activation(pT[:, :, t * MEM:(t + 1) * MEM], bank(2 + t % 2).rearrange("p (k q) -> p k q", k=2),
                               ACT.Copy).then_inc(S("x_tcopied"), 1)

            for s in range(5):
                if s < 4:
                    if s >= 2:
                        act.wait_ge(S("x_turned"), 4 * i + s - 1)
                    act.wait_ge(S("x_nmax"), 4 * i + s + 1)
                    for q in range(2):
                        act.activation(Px[:, s % 2, q, :], bank(s % 2)[:, q * MEM:(q + 1) * MEM], ACT.Exp,
                                       bias=nm[:, 2 * s + q:2 * s + q + 1], accum_out=el[:, 2 * s + q:2 * s + q + 1])\
                           .then_inc(S("x_exp"), 1)
                if s >= 1:
                    turned(s - 1)
            act.wait_ge(S("x_o_mm"), 4 * i + 4)

        def x_dve(dve, i):
            for s in range(6):
                if s < 4:
                    dve.wait_ge(S("x_scores"), 4 * i + s + 1)
                    dve.reduce_max(nm[:, 2 * s:2 * s + 2], bank(s % 2).rearrange("p (q t) -> p q t", q=2), AX,
                                   negate=True).then_inc(S("x_nmax"), 1)
                if 1 <= s <= 4:
                    t = s - 1
                    dve.wait_ge(S("x_exp"), 8 * i + 2 * t + 2)
                    dve.reciprocal(er[:, 2 * t:2 * t + 2], el[:, 2 * t:2 * t + 2]).then_inc(S("x_recip"), 1)
                    dve.wait_ge(S("x_recip"), 4 * i + t + 1)
                    for q in range(2):
                        dve.tensor_scalar(Px[:, t % 2, q, :], Px[:, t % 2, q, :], er[:, 2 * t + q:2 * t + q + 1], None,
                                          ALU.mult).then_inc(S("x_probs"), 1)
                if s in (3, 5):
                    h = s // 4
                    for dc in range(2):
                        dve.wait_ge(S("x_o_mm"), 4 * i + 2 * h + dc + 1)
                        dve.tensor_copy(yT[:, bass.ds(2 * i + dc, 1), h * HALF:(h + 1) * HALF].rearrange("p o t -> p (o t)"),
                                        bank(4 + dc)).then_inc(S("x_o_evac"), 1)

        ar = Arena()
        ul = ar.take(KC * T).rearrange("p (k t) -> p k t", k=KC)
        hid = ar.take(KC * T).rearrange("p (k t) -> p k t", k=KC)
        rl = [t[:, x * HALF:(x + 1) * HALF] for t in (ar.take(T), pos_f) for x in range(2)]
        ul_r = arena_r[:, 0:KC * T].rearrange("p (k t) -> p k t", k=KC)
        hid_r = arena_r[:, KC * T:2 * KC * T].rearrange("p (k t) -> p k t", k=KC)
        f_sq, f_rs = hid, arena[:, 2 * KC * T:2 * KC * T + T]
        u_mlp = pair(in_u, lambda k, lo, hi: ul_r[:, k, lo:hi])
        x_hid = pair(in_y, lambda k, lo, hi: hid_r[:, k, lo:hi])

        def mlp_pe(pe, g):
            for q in range(32):
                p, h = q // 2, q % 2
                if h == 0:
                    panel_in(pe, 16 * g + (UNIT_MAIN + 40 + p))
                if q < 4 or q >= 20:
                    pe.wait_ge(S("dn_evac"), 16 * g + (q if q < 4 else q - 16) + 1)
                else:
                    pe.wait_ge(S("relu_done"), 16 * g + q - 3)
                ready = None
                if p == 0:
                    ready = wait_split(pe, "mlp", h)
                if p == 8:
                    ready = lambda k, h=h: pe.wait_ge(S("hid_split"), 16 * g + 2 * k + h + 1)
                chunk_product(pe, p, bank(q % 4), u_mlp if q < 16 else x_hid, h, ready=ready).then_inc(S("mlp_mm"), 1)

        def mlp_act(act, g):
            for q in range(17):
                if q < 16:
                    act.wait_ge(S("mlp_mm"), 32 * g + q + 1)
                    if q >= 4:
                        act.wait_ge(S("hid_ready"), 16 * g + q - 3)
                    act.activation(rl[q % 4], bank(q % 4), ACT.Relu).then_inc(S("relu_done"), 1)
                if q >= 1:
                    c, cols = (q - 1) // 2, slice((q - 1) % 2 * HALF, ((q - 1) % 2 + 1) * HALF)
                    act.wait_ge(S("hid_ready"), 16 * g + q)
                    high(act, y_r[:, c, cols], hid[:, c, cols]).then_inc(S("hid_high"), 1)

        def mlp_dve(dve, g):
            for q in range(17):
                if q < 16:
                    dve.wait_ge(S("relu_done"), 16 * g + q + 1)
                    dve.tensor_tensor(hid[:, q // 2, q % 2 * HALF:(q % 2 + 1) * HALF], rl[q % 4], rl[q % 4],
                                      ALU.mult).then_inc(S("hid_ready"), 1)
                if q >= 1:
                    c, cols = (q - 1) // 2, slice((q - 1) % 2 * HALF, ((q - 1) % 2 + 1) * HALF)
                    dve.wait_ge(S("hid_high"), 16 * g + q)
                    low(dve, hid_r[:, c, cols], hid[:, c, cols], y_r[:, c, cols]).then_inc(S("hid_split"), 1)
            for q in range(16):
                dve.wait_ge(S("mlp_mm"), 32 * g + 16 + q + 1)
                dst = hT[:, q // 2, q % 2 * HALF:(q % 2 + 1) * HALF]
                dve.tensor_tensor(dst, dst, bank(q % 4), ALU.add).then_inc(S("dn_evac"), 1)

        gpre = sb("gpre", [P, KC])

        G2 = UNIT_MAIN + 104
        P2_BANK = [q % 4 for q in range(12)] + [7] * 8 + [6 + q % 2 for q in range(28)]

        u_two = pair(in_h, in_u)

        def p2_pe(pe, q):
            p, h = q // 2, q % 2
            if h == 0:
                panel_in(pe, G2 + p)
            before = [x for x in range(q) if P2_BANK[x] == P2_BANK[q]]
            if before:
                pe.wait_ge(S("p2_evac"), before[-1] + 1)
            m = chunk_product(pe, G2 + p, bank(P2_BANK[q]), u_two, h, ready=wait_split(pe, "u2", h) if p == 0 else None)
            m.then_inc(S("p2_mm"), 1)

        ar = Arena()
        rkv = arena[:, 0:6 * (PAD + T)].rearrange("p (c t) -> p c t", c=6)
        aq = ar.take(4 * T).rearrange("p (c t) -> p c t", c=4)
        ak, akx = ar.take(T), ar.take(T)
        av = ar.take(T).rearrange("p (t f) -> p t f", t=NT)
        gq, gk = ar.take(T), ar.take(T)
        gv = ar.take(2 * T).rearrange("p (t f) -> p t f", t=NT)
        avT, gvT = yT[:, 4, :], yT[:, 5:7, :]
        at_g = ar.at
        sbias = ar.take(8 * 2 * P).rearrange("p (h k) -> p h k", h=8)
        WK = 2 * P + 4
        Sw = ar.take(8 * WK).rearrange("p (g h k) -> p g h k", g=2, h=4)
        Pw = ar.take(8 * WK).rearrange("p (g h k) -> p g h k", g=2, h=4)
        pTw = pos_f.rearrange("p (k h q) -> p k h q", k=2, h=4)

        gate = [arena[:, 6 * (PAD + T) + 256:6 * (PAD + T) + 256 + HALF], sb("gate1", [P, HALF])[:, :]]

        def p2_act(act, q):
            p, h = q // 2, q % 2
            act.wait_ge(S("p2_mm"), q + 1)
            b, cols = bank(P2_BANK[q]), slice(h * HALF, (h + 1) * HALF)
            func, scale = ACT.Copy, 1.0
            if p < 4:
                dst, scale = aq[:, p, cols], 0.125
            elif p == 4:
                dst = ak[:, cols]
            elif p == 5:
                dst = avT[:, cols]
            elif p == 6:
                dst, scale = gq[:, cols], 32 ** -0.5
            elif p == 7:
                dst = gk[:, cols]
            elif p < 10:
                dst = gvT[:, p - 8, cols]
            elif p < 16:
                dst = rkv[:, p - 10, PAD + h * HALF:PAD + (h + 1) * HALF]
            else:
                func = ACT.Silu
                if p in (20, 21):
                    dst = yT[:, 4 + p - 20, cols]
                else:
                    dst = gate[h]
                    if gate_uses(q) >= 1:
                        act.wait_ge(S("gated"), gate_uses(q))
            act.activation(dst, b, func, scale=scale).then_inc(S("p2_evac"), 1)

        GATES = [q for q in range(32, 48) if q // 2 not in (20, 21)]

        def gate_uses(q):
            return GATES.index(q) - 1

        def apply_gate(dve, q):
            p, h = q // 2, q % 2
            c = p - 16 if p < 20 else 6 + p - 22
            dst = yT[:, c, h * HALF:(h + 1) * HALF]
            dve.wait_ge(S("p2_evac"), q + 1)
            dve.tensor_tensor(dst, dst, gate[h], ALU.mult).then_inc(S("gated"), 1)

        def window(u):
            n = u // 2
            return n, u % 2, P if n == 0 else 0

        def swa_pe(pe):
            pe.wait_ge(S("akx_in"), 32)
            pe.wait_ge(S("p2_evac"), 12)
            for h in range(2):
                m = turn_tiles(pe, 4 + h, avT[:, h * HALF:(h + 1) * HALF])
            m.then_inc(S("v_turned"), 1)
            for s in range(18):
                if s < 16:
                    n, g, lo = window(s)
                    if s >= 2:
                        pe.wait_ge(S("sw_biased"), s - 1)
                    for c in range(2):
                        for par in range(2):
                            r = slice(64 * par, 64 * par + 64)
                            src = ak if par == g else akx
                            m = pe.matmul(bank(2 * (s % 2) + par)[:, c * 2 * P + lo:(c + 1) * 2 * P], aq[r, 2 * g + c, n * P:(n + 1) * P],
                                          src[r, (n - 1) * P + lo:(n + 1) * P], start=True, stop=True)
                    m.then_inc(S("sw_scores"), 1)
                    if s < 8:
                        p2_pe(pe, 12 + s)
                if s >= 2:
                    t = s - 2
                    n, g, lo = window(t)
                    pe.wait_ge(S("sw_tcopied"), t + 1)
                    if t >= 1:
                        pe.wait_ge(S("sw_o_evac"), t)
                    for par in range(2):
                        for kt in range(lo // P, 2):
                            m = pe.matmul(PS[64 * par:64 * par + 64, 6 * HALF:6 * HALF + 2 * P], av[:, n - 1 + kt, 64 * g:64 * g + 64],
                                          pTw[:, kt, 2 * par:2 * par + 2, :].rearrange("p c q -> p (c q)"), start=(kt == lo // P), stop=(kt == 1))
                    m.then_inc(S("sw_o_mm"), 1)
                if 1 <= s <= 16:
                    t = s - 1
                    n, g, lo = window(t)
                    if t >= 1:
                        pe.wait_ge(S("sw_tcopied"), t)
                    else:
                        pe.wait_ge(S("v_copied"), 5)
                    pe.wait_ge(S("sw_probs"), t + 1)
                    for kt in range(lo // P, 2):
                        for h in range(4):
                            m = pe.transpose(bank(4 + kt)[:, h * P:(h + 1) * P], Pw[:, g, h, kt * P:(kt + 1) * P], cst("ident"))
                    m.then_inc(S("sw_turned"), 1)

        def swa_act(act):
            act.wait_ge(S("v_turned"), V_WINDOW)
            act.activation(av.rearrange("p t f -> p (t f)"), bank(4, 2), ACT.Copy).then_inc(S("v_copied"), 1)
            for s in range(17):
                if s < 16:
                    n, g, lo = window(s)
                    if s >= 2:
                        act.wait_ge(S("sw_turned"), s - 1)
                    act.wait_ge(S("sw_nmax"), s + 1)
                    for h in range(4):
                        m = act.activation(Pw[:, g, h, lo:2 * P + 1], Sw[:, g, h, lo:2 * P + 1], ACT.Exp,
                                           bias=nm[:, 4 * g + h:4 * g + h + 1], accum_out=el[:, 4 * g + h:4 * g + h + 1])
                        m.then_inc(S("sw_exp"), 1)
                    if s < 8:
                        p2_act(act, 12 + s)
                if s >= 1:
                    t = s - 1
                    n, g, lo = window(t)
                    act.wait_ge(S("sw_turned"), t + 1)
                    act.activation(pTw[:, lo // P:2, :, :].rearrange("p k h q -> p (k h q)"), bank(4 + lo // P, 2 - lo // P),
                                   ACT.Copy).then_inc(S("sw_tcopied"), 1)

        def swa_dve(dve):
            o = VEC["sinks"][0]
            for g in range(2):
                dve.tensor_copy(Sw[:, g, :, 2 * P:2 * P + 1], vec[:, o + 4 * g:o + 4 * g + 4].unsqueeze(2)).then_inc(S("sw_sink"), 1)
            dve.wait_ge(S("sw_sink"), 2)
            dve.wait_ge(S("bias_in"), 16)
            for s in range(18):
                if s < 16:
                    n, g, lo = window(s)
                    dve.wait_ge(S("sw_scores"), s + 1)
                    if s >= 2:
                        dve.wait_ge(S("sw_exp"), 4 * (s - 1))
                    dve.tensor_tensor(Sw[:, g, :, lo:2 * P], bank(2 * (s % 2), 2).rearrange("p (h k) -> p h k", h=4)[:, :, lo:],
                                      sbias[:, 4 * g:4 * g + 4, lo:], ALU.add).then_inc(S("sw_biased"), 1)
                    dve.wait_ge(S("sw_biased"), s + 1)
                    dve.reduce_max(nm[:, 4 * g:4 * g + 4], Sw[:, g, :, lo:2 * P + 1], AX, negate=True).then_inc(S("sw_nmax"), 1)
                if 1 <= s <= 16:
                    t = s - 1
                    n, g, lo = window(t)
                    dve.wait_ge(S("sw_exp"), 4 * t + 4)
                    dve.reciprocal(er[:, 4 * g:4 * g + 4], el[:, 4 * g:4 * g + 4]).then_inc(S("sw_recip"), 1)
                    dve.wait_ge(S("sw_recip"), t + 1)
                    dve.tensor_tensor(Pw[:, g, :, lo:2 * P], Pw[:, g, :, lo:2 * P],
                                      er[:, 4 * g:4 * g + 4].unsqueeze(2).broadcast_to([P, 4, 2 * P - lo]), ALU.mult)\
                       .then_inc(S("sw_probs"), 1)
                if s >= 2:
                    t = s - 2
                    n, g, lo = window(t)
                    dve.wait_ge(S("sw_o_mm"), t + 1)
                    dve.tensor_copy(yT[:, 2 * g:2 * g + 2, n * P:(n + 1) * P], bank(6)[:, :2 * P].rearrange("p (c q) -> p c q", c=2))\
                       .then_inc(S("sw_o_evac"), 1)

        CH = T // P
        ar = Arena()
        ar.at = at_g
        gb = yT[:, 6, :]
        lv = ar.take(2 * T).rearrange("p (b t) -> p b t", b=2)
        gA = ar.take(4 * T).rearrange("p (h c t) -> p h c t", h=4, c=CH)
        g_lora = arena[:, 6 * (PAD + T):6 * (PAD + T) + 256]
        gl_hi, gl_lo = (arena_r[:, ar.at - T - x * 256:ar.at - T - x * 256 + 256] for x in range(1, 3))
        gt = gA[0:16, 0, :, :].rearrange("p c t -> p (c t)")
        gtmp, gy = gA[:, 1, :, :].rearrange("p c t -> p (c t)"), gA[:, 2, :, :].rearrange("p c t -> p (c t)")
        gS = yT[:, 4:6, :].rearrange("p a (c f) -> p (a c) f", c=4)
        g_q, g_k = lv[:, 0, :], lv[:, 1, :]
        gkt = pos_f.rearrange("p (c f) -> p c f", c=CH)
        elast = small[:, 0:CH]
        gsq = gA[:, 0:2, :, :].rearrange("p h c t -> p h (c t)")
        LEVELS = 8
        last_of = gb.rearrange("p (c t) -> p c t", c=CH)[:, :, P - 1:P]

        def gla_pe(pe, between):
            pe.wait_ge(S("p2_evac"), 20)
            pe.wait_ge(S("sw_tcopied"), 16)
            pe.wait_ge(S("sw_o_evac"), 16)
            for x in range(2):
                for h in range(2):
                    m = turn_tiles(pe, 4 + 2 * x + h, gvT[:, x, h * HALF:(h + 1) * HALF])
            m.then_inc(S("v_turned"), 1)
            pe.wait_ge(S("small_low"), SMALL_GK)
            for h in range(2):
                for k in range(KC):
                    m = product(pe, bank(h), (gl_hi[:, 16 * k:16 * k + P], gl_lo[:, 16 * k:16 * k + P]),
                                u_two(k, h * HALF, (h + 1) * HALF), k == 0, k == KC - 1)[1]
            m.then_inc(S("gl_down"), 1)
            pe.wait_ge(S("gl_down_taken"), 1)
            for h in range(2):
                m = pe.matmul(bank(2 + h), g_lora[0:16, P:2 * P], gt[:, h * HALF:(h + 1) * HALF], start=True, stop=True)
            m.then_inc(S("gl_gate"), 1)
            for l in range(LEVELS):
                if l == 0:
                    pe.wait_ge(S("p2_evac"), 16)
                    pe.wait_ge(S("gl_lin"), 1)
                else:
                    pe.wait_ge(S("gl_level"), 2 * l)
                for half in range(2):
                    if 2 * l + half >= 1:
                        pe.wait_ge(S("gl_taken"), 4 * (2 * l + half))
                    for cc in range(4):
                        c = 4 * half + cc
                        for h in range(4):
                            a, b = (gk, gq) if l == 0 else (lv[:, l % 2, :], lv[:, l % 2, :])
                            m = pe.matmul(bank(h)[:, cc * P:(cc + 1) * P], a[32 * h:32 * h + 32, c * P:(c + 1) * P],
                                          b[32 * h:32 * h + 32, c * P:(c + 1) * P], start=True, stop=True)
                    m.then_inc(S("gl_prod"), 1)
                if l == 0:
                    pe.wait_ge(S("v_copied"), 9)
                for q in between[l]:
                    p2_pe(pe, q)
            pe.wait_ge(S("gl_qk_dec"), 1)
            for c in range(CH):
                m = pe.transpose(bank(4 + c // 4)[:, c % 4 * P:(c % 4 + 1) * P], g_k[:, c * P:(c + 1) * P], cst("ident"))
            m.then_inc(S("gl_kt"), 1)
            pe.wait_ge(S("gl_kt_taken"), 1)
            pe.wait_ge(S("gl_taken"), 8 * LEVELS)
            for c in range(CH):
                m = pe.matmul(bank(c // 2)[:, c % 2 * 256:(c % 2 + 1) * 256], gkt[:, c, :], gv[:, c, :], start=True, stop=True)
                m.then_inc(S("gl_delta"), 1)
            pe.wait_ge(S("gl_states"), CH)
            pe.wait_ge(S("gl_qk_dec"), 2)
            for hp in range(2):
                for c in range(CH):
                    o = slice(2 * hp * HALF + c * P, 2 * hp * HALF + (c + 1) * P)
                    pe.matmul(PS[:, o], gS[:, c, hp * P:(hp + 1) * P], g_q[:, c * P:(c + 1) * P], start=True, stop=False)
                    for x in range(2):
                        h = 2 * hp + x
                        m = pe.matmul(PS[64 * x:64 * x + 64, o], gv[:, c, 64 * h:64 * h + 64], gA[:, h, c, :], start=False, stop=True)
                m.then_inc(S("gl_o"), 1)
            for q in range(40, 44):
                p2_pe(pe, q)
            for hp in range(2):
                pe.wait_ge(S("gl_o_sq"), hp + 1)
                for h in range(2):
                    m = pe.matmul(bank(4 + h), cst("blk64"), gsq[:, hp, h * HALF:(h + 1) * HALF], start=True, stop=True)
                m.then_inc(S("gl_sum"), 1)
                pe.wait_ge(S("gl_log"), hp + 1)

        def gla_act(act, between):
            act.dma_start(g_lora, lora_d[:, T:T + 256]).then_inc(S("glora_in"), 16)
            act.wait_ge(S("v_turned"), V_LINEAR)
            for x in range(2):
                for h in range(2):
                    act.activation(gv[:, 4 * h:4 * h + 4, x * P:(x + 1) * P], bank(4 + 2 * x + h).rearrange("p (t f) -> p t f", t=4),
                                   ACT.Copy).then_inc(S("v_copied"), 1)
            act.wait_ge(S("glora_in"), 16)
            high(act, gl_hi, g_lora).then_inc(S("small_high"), 1)
            act.wait_ge(S("gl_down"), 1)
            act.activation(gt, PS[0:16, 0:T], ACT.Copy).then_inc(S("gl_down_taken"), 1)
            act.preload_act_table_set("natural_log_exp_and_others")
            act.wait_ge(S("gl_gate"), 1)
            act.activation(gy, bank(2, 2), ACT.Identity, bias=vcol("gk_b")).then_inc(S("gl_soft"), 1)
            act.wait_ge(S("gl_soft"), 1)
            act.activation(gtmp, gy, ACT.Abs).then_inc(S("gl_soft"), 1)
            act.wait_ge(S("gl_soft"), 2)
            act.activation(gtmp, gtmp, ACT.Exp, scale=-1.0).then_inc(S("gl_soft"), 1)
            act.wait_ge(S("gl_soft"), 3)
            act.activation(gtmp, gtmp, ACT.Ln, bias=1.0).then_inc(S("gl_soft"), 1)
            for l in range(1, LEVELS + 1):
                if l < LEVELS:
                    act.wait_ge(S("gl_diff"), l)
                    act.activation(lv[:, l % 2, :], lv[:, l % 2, :], ACT.Exp, scale=1.0 / 16).then_inc(S("gl_exp"), 1)
                for q in between[l - 1]:
                    p2_act(act, q)
            act.wait_ge(S("gl_end_diff"), 1)
            act.activation(g_k, g_k, ACT.Exp, scale=1.0 / 16).then_inc(S("gl_end_exp"), 1)
            act.activation(g_q, gb, ACT.Exp, scale=1.0 / 16).then_inc(S("gl_end_exp"), 1)
            act.activation(elast.unsqueeze(2), last_of, ACT.Exp, scale=1.0 / 16).then_inc(S("gl_end_exp"), 1)
            act.wait_ge(S("gl_kt"), 1)
            act.activation(gkt, bank(4, 2).rearrange("p (c f) -> p c f", c=CH), ACT.Copy).then_inc(S("gl_kt_taken"), 1)
            for hp in range(2):
                act.wait_ge(S("gl_o"), 2)
                act.activation(gsq[:, hp, :], bank(2 * hp, 2), ACT.Square).then_inc(S("gl_o_sq"), 1)
            for q in range(40, 44):
                p2_act(act, q)
            for hp in range(2):
                act.wait_ge(S("gl_sum"), hp + 1)
                if hp == 0:
                    act.preload_act_table_set("natural_log_exp_and_others")
                act.activation(gsq[:, hp, :], bank(4, 2), ACT.Ln, bias=cst("eps5"), scale=1.0 / 64).then_inc(S("gl_log"), 1)
                act.wait_ge(S("gl_log"), hp + 1)
                act.activation(gsq[:, hp, :], gsq[:, hp, :], ACT.Exp, scale=-0.5).then_inc(S("gl_rstd"), 1)

        def gla_dve(dve, between):
            dve.memset(rkv[:, :, 0:PAD], 0.0).then_inc(S("rkv_pad"), 1)
            dve.wait_ge(S("small_high"), SMALL_GK)
            low(dve, gl_lo, g_lora, gl_hi).then_inc(S("small_low"), 1)
            dve.memset(pos_f, 1.0).then_inc(S("gl_mask"), 1)
            dve.wait_ge(S("gl_mask"), 1)
            dve.memset(pos_f.rearrange("p (c t) -> p c t", c=CH)[:, :, 0:1], 0.0).then_inc(S("gl_mask"), 1)
            dve.wait_ge(S("gl_soft"), 4)
            dve.scalar_tensor_tensor(gy, gy, 0.0, gtmp, ALU.min, ALU.subtract).then_inc(S("gl_lin"), 1)
            dve.wait_ge(S("gl_lin"), 1)
            dve.wait_ge(S("gl_mask"), 2)
            dve.wait_ge(S("v_turned"), V_LINEAR)
            dve.tensor_tensor_scan(gb, pos_f, gy, 0.0, ALU.mult, ALU.add).then_inc(S("gl_cum"), 1)
            dve.wait_ge(S("gl_cum"), 1)

            def diff(l):
                n = 2 ** (l - 1)
                b4 = gb.rearrange("p (m h s) -> p m h s", h=2, s=n)
                d4 = lv[:, l % 2, :].rearrange("p (m h s) -> p m h s", h=2, s=n)
                ref = b4[:, :, 0, n - 1:n].broadcast_to([P, T // (2 * n), n])
                if l >= 3:
                    dve.wait_ge(S("gl_prod"), 2 * (l - 2) + 2)
                dve.tensor_tensor(d4[:, :, 1, :], b4[:, :, 1, :], ref, ALU.subtract)
                dve.tensor_tensor(d4[:, :, 0, :], ref, b4[:, :, 0, :], ALU.subtract).then_inc(S("gl_diff"), 1)

            diff(1)

            def times_qk(l):
                n = 2 ** (l - 1)
                dve.wait_ge(S("gl_exp"), l)
                for h, src in ((1, gq), (0, gk)):
                    d4 = lv[:, l % 2, :].rearrange("p (m h s) -> p m h s", h=2, s=n)[:, :, h, :]
                    dve.tensor_tensor(d4, d4, src.rearrange("p (m h s) -> p m h s", h=2, s=n)[:, :, h, :], ALU.mult)\
                       .then_inc(S("gl_level"), 1)

            for l in range(LEVELS):
                if 1 <= l < LEVELS - 1:
                    diff(l + 1)
                for half in range(2):
                    if half == 1 and l + 1 < LEVELS:
                        times_qk(l + 1)
                    dve.wait_ge(S("gl_prod"), 2 * l + half + 1)
                    for h in range(4):
                        dst = gA[:, h, 4 * half:4 * half + 4, :]
                        src = bank(h).rearrange("p (c t) -> p c t", c=4)
                        if l == 0:
                            dve.tensor_tensor(dst, src, cst("ident").unsqueeze(1).broadcast_to([P, 4, P]), ALU.mult)\
                               .then_inc(S("gl_taken"), 1)
                        else:
                            o = CONST["level"][0] + (l - 1) * P
                            mask = const[:, o:o + P].bitcast(I32).unsqueeze(1).broadcast_to([P, 4, P])
                            dve.copy_predicated(dst, mask, src).then_inc(S("gl_taken"), 1)
                for q in between[l]:
                    if q in GATES:
                        apply_gate(dve, q)
            dve.wait_ge(S("gl_prod"), 2 * LEVELS)
            b3 = gb.rearrange("p (c t) -> p c t", c=CH)
            dve.tensor_tensor(g_k.rearrange("p (c t) -> p c t", c=CH), last_of.broadcast_to([P, CH, P]), b3,
                              ALU.subtract).then_inc(S("gl_end_diff"), 1)
            dve.wait_ge(S("gl_end_exp"), 2)
            dve.tensor_tensor(g_k, g_k, gk, ALU.mult).then_inc(S("gl_qk_dec"), 1)
            dve.tensor_tensor(g_q, g_q, gq, ALU.mult).then_inc(S("gl_qk_dec"), 1)
            dve.wait_ge(S("gl_end_exp"), 3)
            dve.memset(gS[:, 0, :], 0.0).then_inc(S("gl_states"), 1)
            for c in range(CH - 1):
                dve.wait_ge(S("gl_delta"), c // 2 * 2 + 2)
                dve.wait_ge(S("gl_states"), c + 1)
                dve.tensor_tensor(small_delta, bank(c // 2)[:, c % 2 * 256:(c % 2 + 1) * 256], cst("gla_state"),
                                  ALU.mult).then_inc(S("gl_masked"), 1)
                dve.wait_ge(S("gl_masked"), c + 1)
                dve.scalar_tensor_tensor(gS[:, c + 1, :], gS[:, c, :], elast[:, c:c + 1], small_delta, ALU.mult, ALU.add)\
                   .then_inc(S("gl_states"), 1)
            dve.wait_ge(S("gl_delta"), CH)
            for hp in range(2):
                dve.wait_ge(S("gl_rstd"), hp + 1)
                dve.scalar_tensor_tensor(yT[:, 6 + hp, :], bank(2 * hp, 2), vcol("gla_norm"), gsq[:, hp, :], ALU.mult, ALU.mult)\
                   .then_inc(S("gl_y_ready"), 1)

        KAPPA = float(np.exp(-0.5))
        TL = 4
        RW_LEVELS = range(1, 6)
        RW_STEPS = {
            "act": ["sig_w", "sig_a", "kk_sq", "kk_root", "exp_p", "exp_pinv", "exp_pm", "tok_c", "tok_b", "tok_k", "tok_v", "mbt"]
                   + [f"x{l}{b}" for l in RW_LEVELS for b in range(2)] + ["mkv", "nw0", "nw1", "nw1t", "y0", "y1", "y_sq", "y_log", "y_rstd"],
            "pe": ["lora", "kk_sum", "bon_sum", "tr_c", "tr_b", "tr_k", "tr_v", "p_mbt", "p_mb", "p_mkt", "p_rbt", "p_rkt"]
                  + [f"{x}{l}{b}" for l in RW_LEVELS for x in ("px", "pd") for b in range(2)]
                  + ["p_mkv", "pw0", "pw1", "pw1t", "p_gt", "p_h"] + [f"ps{c}" for c in range(8)] + ["pu", "py", "y_sum", "y_var"],
            "dve": ["kk", "cum", "cum_m", "a_ka", "k_new", "kk_max", "kk_rec", "kkn", "kk_a", "bhat", "bonus", "bonus_v",
                    "tt_a", "tt", "t_a", "t", "mkt", "rbt", "rkt"] + [f"up{l}{b}" for l in RW_LEVELS for b in range(2)]
                   + ["s_start", "gt", "h"] + [f"s{c}" for c in range(8)] + ["u", "centre", "y_norm", "y_sum", "gated"],
            "pool": ["chat", "khat", "rhat"] + [f"ms{l}{b}" for l in RW_LEVELS for b in range(2)],
        }
        rw_next = {e: 0 for e in RW_STEPS}

        def rw(e, name, u):
            return S("rw_" + e), len(RW_STEPS[e]) * u + RW_STEPS[e].index(name) + 1

        def rw_done(e, name, ins):
            assert RW_STEPS[e][rw_next[e] % len(RW_STEPS[e])] == name, (e, name)
            rw_next[e] += 1
            ins.then_inc(S("rw_" + e), 1)

        w2a2 = g_lora
        ar = Arena()
        ar.at = 6 * (PAD + T) + 256 + HALF
        lt = ar.take(T)
        sg, cum, aa, kkn, kn, tm, chat, bhat, khat, rhat, Pt, Pinv, Pm = (ar.take(HALF) for _ in range(13))
        yv, bv = gate[1], pos_f[:, HALF:T]
        ctok, btok, ktok, vtok = (ar.take(HALF).rearrange("p (t f) -> p t f", t=TL) for _ in range(4))
        Sst = ar.take(9 * 64).rearrange("p (c v) -> p c v", c=9)
        Ub = Pm.rearrange("p (h t v) -> p h t v", h=2, t=TL)
        nw1t, GT, Hb = sg, aa.rearrange("p (t c k) -> p t c k", c=2, k=64), kkn.rearrange("p (t c k) -> p t c k", c=2, k=64)
        flat = uT[:, :, :].rearrange("p k t -> p (k t)")
        Tm, TTm, MbT, Xm, Ms, MkT, RBT, RKT = (flat[:, x * T:(x + 1) * T].rearrange("p (h t j) -> p h t j", h=2, t=TL)
                                               for x in range(8))
        nW = Xm
        mkv = flat[:, 4 * T:4 * T + HALF].rearrange("p (h t v) -> p h t v", h=2, t=TL)
        wa_raw, wa_mu, wa_rest = (arena[:, 9216 + x * T:9216 + (x + 1) * T].rearrange("p (k f) -> p k f", k=KC)
                                  for x in range(3))
        wa_rounded = [arena_r[:, x:x + T].rearrange("p (k f) -> p k f", k=KC) for x in (14336, 15360, 10240, 11264)]
        mu_hi, rest_hi, mu_lo, rest_lo = wa_rounded
        mixd = [arena[:, 12288 + x * T:12288 + (x + 1) * T] for x in range(2)]
        smask = pos_f[:, 0:HALF]

        def rw_pre_pe(pe):
            pe.wait_ge(S("small_low"), SMALL_WA)
            for h in range(2):
                lo, hi = h * HALF, (h + 1) * HALF
                for k in range(KC):
                    product(pe, bank(h), (rest_hi[:, k, :], rest_lo[:, k, :]), u_two(k, lo, hi), k == 0, False)
                    m = product(pe, bank(h), (mu_hi[:, k, :], mu_lo[:, k, :]), u_two(k, lo - 1, hi - 1), False, k == KC - 1)[1]
                m.then_inc(S("lora_mm"), 1)

        def wa_act(act):
            act.wait_ge(S("gl_y_ready"), 2)
            act.dma_start(wa_raw.rearrange("p k f -> p (k f)"), lora_d[:, 0:T]).then_inc(S("wa_in"), 16)
            act.dma_start(w2a2, lora_d[:, T + 256:T + 512]).then_inc(S("wa_in"), 16)

        def wa_split_act(act):
            act.wait_ge(S("wa_ready"), KC)
            for dst, src in ((mu_hi, wa_mu), (rest_hi, wa_rest)):
                high(act, dst, src).then_inc(S("small_high"), 1)

        def wa_dve(dve):
            dve.wait_ge(S("wa_in"), 32)
            for k in range(KC):
                dve.tensor_scalar(wa_mu[:, k, 0:64], wa_raw[:, k, 0:64], vcol("mu_w", k), None, ALU.mult).then_inc(S("wa_part"), 1)
                dve.tensor_scalar(wa_mu[:, k, 64:128], wa_raw[:, k, 64:128], vcol("mu_a", k), None, ALU.mult).then_inc(S("wa_part"), 1)
            for k in range(KC):
                dve.wait_ge(S("wa_part"), 2 * k + 2)
                dve.tensor_tensor(wa_rest[:, k, :], wa_raw[:, k, :], wa_mu[:, k, :], ALU.subtract).then_inc(S("wa_ready"), 1)

        def wa_split_dve(dve):
            for x, (dst, src, hi_part) in enumerate(((mu_lo, wa_mu, mu_hi), (rest_lo, wa_rest, rest_hi))):
                dve.wait_ge(S("small_high"), SMALL_WA - 1 + x)
                low(dve, dst, src, hi_part).then_inc(S("small_low"), 1)

        def rw_pre_act(act):
            for h in range(2):
                act.wait_ge(S("lora_mm"), h + 1)
                act.activation(lt[0:64, h * HALF:(h + 1) * HALF], bank(h)[0:64, :], ACT.Tanh).then_inc(S("lora_out"), 1)
                act.activation(lt[64:128, h * HALF:(h + 1) * HALF], bank(h)[64:128, :], ACT.Copy).then_inc(S("lora_out"), 1)

        def rw_pre_dve(dve):
            dve.memset(smask, 1.0).then_inc(S("rw_mask"), 1)
            dve.wait_ge(S("rw_mask"), 1)
            dve.memset(smask.rearrange("p (c t) -> p c t", t=64)[:, :, 0:1], 0.0).then_inc(S("rw_mask"), 1)
            dve.wait_ge(S("p2_evac"), 32)
            dve.wait_ge(S("rkv_pad"), 1)
            for x in range(6):
                if x >= 2:
                    dve.wait_ge(S("rkv_mixed"), x - 1)
                dve.tensor_tensor(mixd[x % 2], rkv[:, x, PAD - 1:PAD + T - 1], rkv[:, x, PAD:], ALU.subtract).then_inc(S("rkv_diff"), 1)
                dve.wait_ge(S("rkv_diff"), x + 1)
                dve.scalar_tensor_tensor(rkv[:, x, PAD:], mixd[x % 2], vcol("mu_rkv", x), rkv[:, x, PAD:], ALU.mult, ALU.add)\
                   .then_inc(S("rkv_mixed"), 1)

        def rw_rows(u):
            p, hf = u // 2, u % 2
            cols = slice(PAD + hf * HALF, PAD + (hf + 1) * HALF)
            return p, hf, rkv[:, p, cols], rkv[:, 2 + p, cols], rkv[:, 4 + p, cols]

        def rw_pe(pe, u):
            p, hf, r_, k_, v_ = rw_rows(u)
            w, done = (lambda e, n, uu=u: pe.wait_ge(*rw(e, n, uu))), (lambda n, ins: rw_done("pe", n, ins))
            if u >= 1:
                w("dve", "gated", u - 1)
            tc = slice(hf * HALF, (hf + 1) * HALF)
            pe.matmul(bank(0), w2a2[0:64, p * P:(p + 1) * P], lt[0:64, tc], start=True, stop=True)
            done("lora", pe.matmul(bank(1), w2a2[64:128, p * P:(p + 1) * P], lt[64:128, tc], start=True, stop=True))
            w("act", "kk_sq")
            done("kk_sum", pe.matmul(bank(2), cst("blk64"), tm, start=True, stop=True))
            w("dve", "bonus")
            done("bon_sum", pe.matmul(bank(3), cst("blk64"), bv, start=True, stop=True))
            for x, (n, src, e, ready) in enumerate((("tr_c", chat, "pool", "chat"), ("tr_b", bhat, "dve", "bhat"),
                                                    ("tr_k", khat, "pool", "khat"), ("tr_v", v_, None, None))):
                if e:
                    w(e, ready)
                for t in range(TL):
                    m = pe.transpose(bank(4 + x)[:, t * P:(t + 1) * P], src[:, t * P:(t + 1) * P], cst("ident"))
                done(n, m)
            w("pool", "rhat")
            for n, a, b, bk, free in (("p_mbt", bhat, chat, 0, ("act", "sig_a")), ("p_mb", chat, bhat, 2, ("dve", "bonus_v")),
                                      ("p_mkt", khat, chat, 4, ("act", "tok_b")), ("p_rbt", bhat, rhat, 6, ("act", "tok_v")),
                                      ("p_rkt", khat, rhat, 0, ("act", "mbt"))):
                w(*free)
                for t in range(TL):
                    for h in range(2):
                        r = slice(64 * h, 64 * h + 64)
                        m = pe.matmul(bank(bk + h)[:, t * P:(t + 1) * P], a[r, t * P:(t + 1) * P], b[r, t * P:(t + 1) * P],
                                      start=True, stop=True)
                done(n, m)
            for l in RW_LEVELS:
                for b in range(2):
                    if l == 1 and b == 0:
                        w("dve", "rkt")
                    if l > 1:
                        w("dve", f"up{l - 1}{b}")
                    w("pool", f"ms{l}{b}")
                    for t in range(TL):
                        m = pe.matmul(bank(b)[:, t * P:(t + 1) * P], Ms[:, b, t, :], Tm[:, b, t, :], start=True, stop=True)
                    done(f"px{l}{b}", m)
                for b in range(2):
                    w("act", f"x{l}{b}")
                    for t in range(TL):
                        if l < 5:
                            pe.matmul(bank(2 + b)[:, t * P:(t + 1) * P], TTm[:, b, t, :], Xm[:, b, t, :], start=True, stop=True)
                        m = pe.matmul(bank(4 + b)[:, t * P:(t + 1) * P], Xm[:, b, t, :], TTm[:, b, t, :], start=True, stop=True)
                    done(f"pd{l}{b}", m)
            for h in range(2):
                for t in range(TL):
                    m = pe.matmul(bank(6)[:, (TL * h + t) * 64:(TL * h + t + 1) * 64], MkT[:, h, t, :], vtok[:, t, 64 * h:64 * h + 64],
                                  start=True, stop=True)
            done("p_mkv", m)
            w("act", "mkv")
            for h in range(2):
                w("dve", f"up5{h}")
                for t in range(TL):
                    pe.matmul(bank(h)[:, t * P:t * P + 64], TTm[:, h, t, :], ctok[:, t, 64 * h:64 * h + 64], start=True, stop=True)
                    m = pe.matmul(bank(h)[:, t * P + 64:(t + 1) * P], TTm[:, h, t, :], mkv[:, h, t, :], start=True, stop=True)
                done(f"pw{h}", m)
            for h in range(2):
                for t in range(TL):
                    m = pe.matmul(PS[64 * h:64 * h + 64, 2 * HALF + t * P:2 * HALF + (t + 1) * P], ctok[:, t, 64 * h:64 * h + 64],
                                  TTm[:, h, t, :], start=True, stop=True)
            done("pw1t", m)
            w("act", "nw1")
            for h in range(2):
                for t in range(TL):
                    for cp in range(2):
                        rr = slice(64 * cp, 64 * cp + 64)
                        m = pe.matmul(PS[64 * h:64 * h + 64, (4 + cp) * HALF + t * 64:(4 + cp) * HALF + (t + 1) * 64],
                                      nW[rr, h, t, 0:64], btok[rr, t, 64 * h:64 * h + 64], start=True, stop=True)
            done("p_gt", m)
            for h in range(2):
                for t in range(TL):
                    for cp in range(2):
                        rr = slice(64 * cp, 64 * cp + 64)
                        o = PS[64 * h:64 * h + 64, (6 + cp) * HALF + t * 64:(6 + cp) * HALF + (t + 1) * 64]
                        pe.matmul(o, ktok[rr, t, 64 * h:64 * h + 64], vtok[rr, t, 64 * h:64 * h + 64], start=True, stop=False)
                        m = pe.matmul(o, btok[rr, t, 64 * h:64 * h + 64], nW[rr, h, t, 64:128], start=False, stop=True)
            done("p_h", m)
            for c in range(8):
                w("dve", "h" if c == 0 else f"s{c - 1}")
                for h in range(2):
                    r = slice(64 * h, 64 * h + 64)
                    m = pe.matmul(PS[r, h * HALF:h * HALF + 64], GT[r, c // 2, c % 2, :], Sst[r, c, :], start=True, stop=True)
                done(f"ps{c}", m)
            w("act", "nw1t")
            for t in range(TL):
                for cp in range(2):
                    for h in range(2):
                        r = slice(64 * h, 64 * h + 64)
                        m = pe.matmul(PS[64 * cp:64 * cp + 64, (2 + h) * HALF + t * 64:(2 + h) * HALF + (t + 1) * 64],
                                      nw1t[r, t * P + 64 * cp:t * P + 64 * cp + 64], Sst[r, 2 * t + cp, :], start=True, stop=True)
            done("pu", m)
            w("dve", "u")
            for h in range(2):
                r = slice(64 * h, 64 * h + 64)
                for t in range(TL):
                    o = (4 + h) * HALF + t * P
                    pe.matmul(PS[r, o:o + P], vtok[:, t, 64 * h:64 * h + 64], RKT[:, h, t, :], start=True, stop=False)
                    pe.matmul(PS[r, o:o + P], Ub[:, h, t, :], RBT[:, h, t, :], start=False, stop=False)
                    for cp in range(2):
                        m = pe.matmul(PS[r, o + 64 * cp:o + 64 * cp + 64], Sst[r, 2 * t + cp, :],
                                      rhat[r, t * P + 64 * cp:t * P + 64 * cp + 64], start=False, stop=(cp == 1))
            done("py", m)
            w("act", "y1")
            done("y_sum", pe.matmul(bank(6), cst("blk64"), yv, start=True, stop=True))
            w("act", "y_sq")
            done("y_var", pe.matmul(bank(7), cst("blk64"), tm, start=True, stop=True))

        def rw_act(act, u):
            p, hf, r_, k_, v_ = rw_rows(u)
            w, done = (lambda e, n, uu=u: act.wait_ge(*rw(e, n, uu))), (lambda n, ins: rw_done("act", n, ins))
            w("pe", "lora")
            done("sig_w", act.activation(sg, bank(0), ACT.Sigmoid, bias=vcol("w0", p)))
            done("sig_a", act.activation(aa, bank(1), ACT.Sigmoid, bias=vcol("a0", p)))
            w("dve", "kk")
            done("kk_sq", act.activation(tm, kkn, ACT.Square))
            w("pe", "kk_sum")
            done("kk_root", act.activation(tm, bank(2), ACT.Sqrt))
            w("dve", "cum_m")
            done("exp_p", act.activation(Pt, cum, ACT.Exp, scale=-KAPPA))
            done("exp_pinv", act.activation(Pinv, cum, ACT.Exp, scale=KAPPA))
            done("exp_pm", act.activation(Pm, Pm, ACT.Exp, scale=-KAPPA))
            for x, (n, tr, dst) in enumerate((("tok_c", "tr_c", ctok), ("tok_b", "tr_b", btok), ("tok_k", "tr_k", ktok),
                                              ("tok_v", "tr_v", vtok))):
                w("pe", tr)
                done(n, act.activation(dst.rearrange("p t f -> p (t f)"), bank(4 + x), ACT.Copy))
            w("pe", "p_mbt")
            done("mbt", act.activation(MbT.rearrange("p h t j -> p (h t j)"), bank(0, 2), ACT.Copy))
            for l in RW_LEVELS:
                for b in range(2):
                    w("pe", f"px{l}{b}")
                    if l > 1:
                        w("pe", f"pd{l - 1}{b}")
                    elif b == 0:
                        w("dve", "tt")
                    done(f"x{l}{b}", act.activation(Xm[:, b, :, :].rearrange("p t j -> p (t j)"), bank(b), ACT.Copy))
            w("pe", "p_mkv")
            done("mkv", act.activation(mkv.rearrange("p h t v -> p (h t v)"), bank(6), ACT.Copy))
            for h in range(2):
                w("pe", f"pw{h}")
                done(f"nw{h}", act.activation(nW[:, h, :, :].rearrange("p t j -> p (t j)"), bank(h), ACT.Copy, scale=-1.0))
            w("pe", "pw1t")
            done("nw1t", act.activation(nw1t, bank(2), ACT.Copy, scale=-1.0))
            w("pe", "py")
            for h in range(2):
                r = slice(64 * h, 64 * h + 64)
                done(f"y{h}", act.activation(yv[r, :], PS[r, (4 + h) * HALF:(5 + h) * HALF], ACT.Copy))
            w("dve", "centre")
            act.preload_act_table_set("natural_log_exp_and_others")
            done("y_sq", act.activation(tm, yv, ACT.Square))
            w("pe", "y_var")
            done("y_log", act.activation(tm, bank(7), ACT.Ln, bias=cst("eps_ln"), scale=1.0 / 64))
            w("act", "y_log")
            done("y_rstd", act.activation(tm, tm, ACT.Exp, scale=-0.5))

        def rw_dve(dve, u):
            p, hf, r_, k_, v_ = rw_rows(u)
            w, done = (lambda e, n, uu=u: dve.wait_ge(*rw(e, n, uu))), (lambda n, ins: rw_done("dve", n, ins))

            def eight(x):
                return x.unsqueeze(1).broadcast_to([P, 8, P])

            def flat8(x):
                return x.rearrange("p h t j -> p (h t) j")

            def banks8(b):
                return bank(b, 2).rearrange("p (x j) -> p x j", x=8)

            done("kk", dve.tensor_scalar(kkn, k_, vcol("k_k", p), None, ALU.mult))
            w("act", "sig_w")
            done("cum", dve.tensor_tensor_scan(cum, smask, sg, 0.0, ALU.mult, ALU.add))
            w("dve", "cum")
            done("cum_m", dve.tensor_tensor(Pm, cum, sg, ALU.subtract))
            w("act", "sig_a")
            done("a_ka", dve.tensor_scalar(kn, aa, 1.0, vcol("k_a", p), ALU.subtract, ALU.mult))
            w("dve", "a_ka")
            done("k_new", dve.scalar_tensor_tensor(kn, kn, 1.0, k_, ALU.add, ALU.mult))
            w("act", "kk_root")
            done("kk_max", dve.tensor_scalar(tm, tm, 1e-12, None, ALU.max))
            w("dve", "kk_max")
            done("kk_rec", dve.reciprocal(tm, tm))
            w("dve", "kk_rec")
            done("kkn", dve.tensor_tensor(kkn, kkn, tm, ALU.mult))
            w("dve", "kkn")
            done("kk_a", dve.tensor_tensor(bhat, kkn, aa, ALU.mult))
            w("dve", "kk_a")
            w("act", "exp_pinv")
            done("bhat", dve.tensor_tensor(bhat, bhat, Pinv, ALU.mult))
            done("bonus", dve.scalar_tensor_tensor(bv, r_, vcol("r_k", p), kn, ALU.mult, ALU.mult))
            w("pe", "bon_sum")
            done("bonus_v", dve.tensor_tensor(bv, bank(3), v_, ALU.mult))
            w("act", "mbt")
            o = CONST["level"][0]
            done("tt_a", dve.tensor_tensor(flat8(Xm), flat8(MbT), eight(const[:, o:o + P]), ALU.mult))
            w("dve", "tt_a")
            done("tt", dve.tensor_tensor(flat8(TTm), eight(cst("ident")), flat8(Xm), ALU.subtract))
            w("pe", "p_mb")
            done("t_a", dve.tensor_tensor(flat8(Tm), banks8(2), eight(cst("first_low")), ALU.mult))
            w("dve", "t_a")
            done("t", dve.tensor_tensor(flat8(Tm), eight(cst("ident")), flat8(Tm), ALU.subtract))
            w("pe", "p_mkt")
            done("mkt", dve.tensor_tensor(flat8(MkT), banks8(4), eight(cst("strict64")), ALU.mult))
            w("pe", "p_rbt")
            done("rbt", dve.tensor_tensor(flat8(RBT), banks8(6), eight(cst("incl64")), ALU.mult))
            w("pe", "p_rkt")
            done("rkt", dve.tensor_tensor(flat8(RKT), banks8(0), eight(cst("incl64")), ALU.mult))
            for l in RW_LEVELS:
                for b in range(2):
                    w("pe", f"pd{l}{b}")
                    if l < 5:
                        t2 = Tm[:, b, :, :].rearrange("p t j -> p (t j)")
                        dve.tensor_tensor(t2, t2, bank(2 + b), ALU.subtract).then_inc(S("rw_t"), 1)
                    t2 = TTm[:, b, :, :].rearrange("p t j -> p (t j)")
                    if l < 5:
                        dve.wait_ge(S("rw_t"), 8 * u + 2 * (l - 1) + b + 1)
                    done(f"up{l}{b}", dve.tensor_tensor(t2, t2, bank(4 + b), ALU.subtract))
            if hf == 0:
                done("s_start", dve.memset(Sst[:, 0, :], 0.0))
            else:
                done("s_start", dve.tensor_copy(Sst[:, 0, :], Sst[:, 8, :]))
            w("pe", "p_gt")
            done("gt", dve.tensor_tensor(GT.rearrange("p t c k -> p c t k"), bank(4, 2).rearrange("p (c x) -> p c x", c=2)[:, :, 0:256]
                                         .rearrange("p c (t k) -> p c t k", t=TL),
                                         cst("ident64").unsqueeze(1).unsqueeze(1).broadcast_to([P, 2, TL, 64]), ALU.add))
            w("pe", "p_h")
            done("h", dve.tensor_tensor(Hb.rearrange("p t c k -> p c t k"), bank(6, 2).rearrange("p (c x) -> p c x", c=2)[:, :, 0:256]
                                        .rearrange("p c (t k) -> p c t k", t=TL),
                                        Pt.rearrange("p (t c s) -> p c t s", c=2, s=64)[:, :, :, 63:64].broadcast_to([P, 2, TL, 64]),
                                        ALU.mult))
            w("dve", "h")
            for c in range(8):
                w("pe", f"ps{c}")
                for h in range(2):
                    r = slice(64 * h, 64 * h + 64)
                    m = dve.scalar_tensor_tensor(Sst[r, c + 1, :], PS[r, h * HALF:h * HALF + 64], Pt[r, 64 * c + 63:64 * c + 64],
                                                 Hb[r, c // 2, c % 2, :], ALU.mult, ALU.add)
                    if h == 0:
                        m.then_inc(S("rw_s"), 1)
                dve.wait_ge(S("rw_s"), 8 * u + c + 1)
                done(f"s{c}", m)
            w("pe", "pu")
            done("u", dve.tensor_tensor(Ub, bank(2, 2).rearrange("p (h x) -> p h x", h=2)[:, :, 0:256].rearrange("p h (t v) -> p h t v", t=TL),
                                        nW[:, :, :, 64:128], ALU.add))
            w("pe", "y_sum")
            done("centre", dve.scalar_tensor_tensor(yv, bank(6), -1.0 / 64, yv, ALU.mult, ALU.add))
            w("act", "y_rstd")
            done("y_norm", dve.scalar_tensor_tensor(yv, yv, vcol("ln_w", p), tm, ALU.mult, ALU.mult))
            w("dve", "y_norm")
            done("y_sum", dve.scalar_tensor_tensor(yv, yv, vcol("ln_b", p), bv, ALU.add, ALU.add))
            w("dve", "y_sum")
            dst = yT[:, 4 + p, hf * HALF:(hf + 1) * HALF]
            done("gated", dve.tensor_tensor(dst, dst, yv, ALU.mult))

        def rw_pool(pool, u):
            p, hf, r_, k_, v_ = rw_rows(u)
            w, done = (lambda e, n, uu=u: pool.wait_ge(*rw(e, n, uu))), (lambda n, ins: rw_done("pool", n, ins))
            w("dve", "kkn")
            w("act", "exp_pm")
            done("chat", pool.tensor_tensor(chat, kkn, Pm, ALU.mult))
            done("khat", pool.tensor_tensor(khat, kn, Pinv, ALU.mult))
            done("rhat", pool.tensor_tensor(rhat, r_, Pt, ALU.mult))
            w("act", "mbt")
            for l in RW_LEVELS:
                for b in range(2):
                    if l > 1:
                        w("pe", f"px{l - 1}{b}")
                    o = CONST["level"][0] + l * P
                    done(f"ms{l}{b}", pool.tensor_tensor(Ms[:, b, :, :], MbT[:, b, :, :],
                                                         const[:, o:o + P].unsqueeze(1).broadcast_to([P, TL, P]), ALU.mult))

        Y3 = [[0, 1], [2, 3, 4], [6, 7], [5]]

        def y3_place(u, k):
            return split_from("y3") + sum(len(ks) for ks in Y3[:u]) + Y3[u].index(k) + 1

        def y3_act(act, u):
            for k in Y3[u]:
                if k in (4, 5):
                    act.wait_ge(*rw("dve", "gated", u))
                high(act, in_h(k, 0, T), yT[:, k, :]).then_inc(S("split_high"), 1)

        def y3_dve(dve, u):
            for k in Y3[u]:
                dve.wait_ge(S("split_high"), y3_place(u, k))
                low(dve, in_y(k, 0, T), yT[:, k, :], in_h(k, 0, T)).then_inc(S("split_low"), 1)

        Z = arena[:, 0:KC * T].rearrange("p (k t) -> p k t", k=KC)
        gpost = sb("gpost", [P, KC])
        small_delta = yT[:, 7, 0:256]
        BETWEEN = [[20 + 3 * l + x for x in range(3) if 3 * l + x < 20] for l in range(LEVELS)]

        park_d = nc.dram_tensor("parked_stream", (P, KC, T), F, kind="Internal").ap()
        block = ctx.enter_context(nc.Block())

        @block.sync
        def _(sync):
            sync.dma_start(const[:, :], const_d).then_inc(S("const_in"), 16)
            sync.dma_start(vec[:, :], vec_d).then_inc(S("vec_in"), 16)
            for k in range(KC):
                sync.dma_start(hT[:, k, :], xT_d[:, k, :]).then_inc(S("x_early" if k < KC // 2 else "x_in"), 16)
            sync.dma_start(pos_i[:, :], pos_d).then_inc(S("pos_in"), 16)
            def load_panel(g, x):
                sync.dma_start(w_raw[:, x, :], w_d[bass.ds(g, 1), :, :].rearrange("o p n -> p (o n)")).then_inc(w_in[x], 16)

            with loop(sync, UNITS) as u:
                for s in range(3):
                    sync.wait_ge(S("w_split"), 3 * u + (s + CREDIT))
                    load_panel(6 * u + 2 * s, 0)
                    sync.wait_ge(S("proj_evac"), PROJ * u + (3 * s + 1))
                    load_panel(6 * u + (2 * s + 1), 1)
            sync.wait_ge(S("w_split"), UNIT_MAIN + CREDIT)
            load_panel(2 * UNIT_MAIN, 0)
            sync.wait_ge(S("proj_evac"), PROJ * UNITS + 1)
            load_panel(2 * UNIT_MAIN + 1, 1)
            with loop(sync, LATER // 2 - 1) as i:
                for x in range(2):
                    sync.wait_ge(S("w_split"), 2 * i + (UNIT_MAIN + CREDIT + x + 1))
                    load_panel(2 * i + (2 * UNIT_MAIN + 2 + x), x)
            for k in range(KC):
                sync.wait_ge(S("final_ready"), k + 1)
                sync.dma_start(out_d[:, k, :], Z[:, k, :]).then_inc(S("stored"), 16)
            sync.wait_ge(S("stored"), 16 * KC)

        @block.vector
        def _(dve):
            dve.memset(u_r[:, :, 0:PAD].bitcast(F), 0.0)
            dve.memset(h_r[:, :, 0:PAD].bitcast(F), 0.0)
            dve.wait_ge(S("vec_in"), 16)
            o = VEC["lam"][0]
            dve.memset(lamt[:, :], 0.0).then_inc(S("lam_a"), 1)
            dve.wait_ge(S("lam_a"), 1)
            for x in range(2):
                dve.tensor_tensor(lamt[:, x:x + 1], vec[:, o + 2 * x:o + 2 * x + 1], vec[:, o + 2 * x + 1:o + 2 * x + 2],
                                  ALU.mult).then_inc(S("lam_prod"), 1)
            dve.tensor_scalar(gsub[:, :], vcol("g_subln"), 1.0 - LAM_INIT, None, ALU.mult)
            dve.wait_ge(S("pos_in"), 16)
            dve.wait_ge(S("const_in"), 16)
            dve.tensor_copy(posf, pos_i[:, :]).then_inc(S("ang_step"), 1)
            dve.wait_ge(S("ang_step"), 1)
            dve.tensor_scalar(ang, posf, cst("inv_freq"), None, ALU.mult).then_inc(S("ang_step"), 1)
            dve.wait_ge(S("ang_step"), 2)
            dve.tensor_scalar(turns, ang, 0.15915494309189535, 12582912.0, ALU.mult, ALU.add).then_inc(S("ang_step"), 1)
            dve.wait_ge(S("ang_step"), 3)
            dve.tensor_scalar(turns, turns, 12582912.0, None, ALU.subtract).then_inc(S("ang_step"), 1)
            dve.wait_ge(S("ang_step"), 4)
            dve.scalar_tensor_tensor(ang, turns, -6.28125, ang, ALU.mult, ALU.add).then_inc(S("ang_step"), 1)
            dve.wait_ge(S("ang_step"), 5)
            dve.scalar_tensor_tensor(ang, turns, -0.0019353071795864769, ang, ALU.mult, ALU.add).then_inc(S("ang_step"), 1)
            dve.wait_ge(S("ang_step"), 6)
            dve.tensor_scalar(ang, ang, 3.1415925, -3.1415925, ALU.min, ALU.max).then_inc(S("ang_step"), 1)
            dve.wait_ge(S("ang_step"), 7)
            dve.scalar_tensor_tensor(posf, ang, -1.0, ang, ALU.mult, ALU.max).then_inc(S("ang_ready"), 1)
            dve.wait_ge(S("lam_exp"), 1)
            dve.tensor_tensor(lamt[:, 4:5], lamt[:, 3:4], lamt[:, 2:3], ALU.subtract).then_inc(S("lam_a"), 1)
            dve.wait_ge(S("lam_a"), 2)
            dve.tensor_scalar(lamt[:, 5:6], lamt[:, 4:5], LAM_INIT, None, ALU.subtract).then_inc(S("lam_a"), 1)
            dve.wait_ge(S("lam_a"), 3)
            norm_split_dve(dve, "mix", in_(hT), in_(hT), lambda k: vcol("g_mix", k), n_rs, in_u, in_h, "mix")
            with loop(dve, 4) as i:
                da_dve(dve, i)
            with loop(dve, 4) as j:
                sb_dve(dve, j)
            dve.wait_ge(S("sb_y_ready"), 4)
            dve.sem_inc(S("wo_evac"), 4)
            split_dve(dve, "y1", in_(yT), in_u, in_y)
            dve.wait_ge(S("x_in"), 8 * KC + 16)
            gemm_evac(dve, "wo", 8, T, add_to_h(dve, "wo"))
            norm_split_dve(dve, "mem", in_(mraw), in_(mT), lambda k: vcol("g_mem", k), m_rs, mem_split_high, mem_split_low, "mem", MEM)
            norm_split_dve(dve, "x", in_(hT), in_(yT), lambda k: vcol("g_cross", k), x_rs, in_u, in_y, "x")
            with loop(dve, 4) as i:
                x_dve(dve, i)
            dve.wait_ge(S("x_o_evac"), 16)
            dve.sem_inc(S("xo_evac"), 4)
            split_dve(dve, "y2", in_(yT), in_u, in_y)
            gemm_evac(dve, "xo", 8, T, add_to_h(dve, "xo"))
            dve.wait_ge(S("xo_evac"), 20)
            dve.sem_inc(S("dn_evac"), 4)
            norm_split_dve(dve, "mlp", in_(hT), in_(ul), lambda k: vcol("g_mlp", k), f_rs, in_u, in_(ul_r), "mlp")
            with loop(dve, 4) as g:
                mlp_dve(dve, g)
            norm_dve(dve, "fin", lambda k: hT[:, k, :], lambda k: hT[:, k, :], lambda k: vcol("g_final", k), T, f_rs)
            dve.wait_ge(S("proj_evac"), PROJ * UNITS + 1)
            o = VEC["ada_b"][0]
            dve.tensor_tensor(ada[:, :], ada[:, :], vec[:, o:o + 24], ALU.add).then_inc(S("ada_ready"), 1)
            dve.wait_ge(S("ada_ready"), 1)
            o = VEC["norm_pre"][0]
            dve.scalar_tensor_tensor(gpre[:, :], ada[:, 8:16], 1.0, vec[:, o:o + 8], ALU.add, ALU.mult).then_inc(S("gpre_ready"), 1)
            dve.wait_ge(S("gpre_ready"), 1)
            norm_split_dve(dve, "pre", in_(hT), in_(uT[:, :, PAD:]), lambda k: gpre[:, k:k + 1], f_rs, in_h, in_u, "u2",
                           shift=lambda k: ada[:, k:k + 1])
            swa_dve(dve)
            gla_dve(dve, BETWEEN)
            dve.wait_ge(S("gl_y_ready"), 2)
            wa_dve(dve)
            for q in range(44, 48):
                if q == 46:
                    wa_split_dve(dve)
                apply_gate(dve, q)
            rw_pre_dve(dve)
            dve.wait_ge(S("rw_mask"), 2)
            dve.wait_ge(S("rkv_mixed"), 6)
            dve.wait_ge(S("lora_mm"), 2)
            for u in range(4):
                rw_dve(dve, u)
                y3_dve(dve, u)
            o = VEC["norm_post"][0]
            dve.tensor_tensor(gpost[:, :], ada[:, 16:24], vec[:, o:o + 8], ALU.mult).then_inc(S("gpost_ready"), 1)
            dve.wait_ge(S("gpost_ready"), 1)
            norm_dve(dve, "post", lambda k: Z[:, k, :], lambda k: Z[:, k, :], lambda k: gpost[:, k:k + 1], T, f_rs)

        @block.gpsimd
        def _(pool):
            pool.sem_inc(S("w_split"), CREDIT)
            pool.wait_ge(S("const_in"), 16)
            split_panel(pool, 0, 0, 0, 0)
            with loop(pool, 5) as u:
                for what in ("k", "v", "next q"):
                    split_unit_panel(pool, u, what)
            with loop(pool, 3) as j:
                sb_pool(pool, j, False)
            sb_pool(pool, 3, True)
            split_later_panel(pool, 0, 1)
            with loop(pool, (LATER - 8) // 2 - 1) as i:
                for x in range(2):
                    split_later_panel(pool, i + 1, x)
            split_later_panel(pool, (LATER - 8) // 2, 0)
            for u in range(4):
                rw_pool(pool, u)
            split_later_panel(pool, (LATER - 8) // 2, 1)
            with loop(pool, 3) as i:
                for x in range(2):
                    split_later_panel(pool, i + (LATER - 8) // 2 + 1, x)
            pool.wait_ge(S("parked"), 16 * (KC + 1))
            for k in range(KC):
                pool.wait_ge(*norm_out("post", k + 1))
                pool.tensor_tensor(Z[:, k, :], Z[:, k, :], U(k), ALU.add).then_inc(S("final_ready"), 1)

        @block.scalar
        def _(act):
            act.wait_ge(S("vec_in"), 16)
            act.activation(cact[:, :], vec[:, VEC["c"][0]:VEC["c"][0] + 8], ACT.Silu).then_inc(S("cact_ready"), 1)
            act.wait_ge(S("lam_sum"), 1)
            act.activation(lamt[:, 2:4], bank(0)[:, 0:2], ACT.Exp).then_inc(S("lam_exp"), 1)
            act.wait_ge(S("ang_ready"), 1)
            act.activation(sinT, ang, ACT.Sin)
            act.activation(cosT, posf, ACT.Sin, bias=cst("half_pi"), scale=-1.0)
            act.wait_ge(S("const_in"), 16)
            norm_act(act, "mix", lambda k: hT[:, k, :], T, n_sq, n_rs, lambda k: [(S("x_early" if k < KC // 2 else "x_in"), 8 * KC)])
            act.wait_ge(S("lam_exp"), 1)
            act.sem_inc(S("proj_evac"), 1)
            act.sem_inc(S("olog_ready"), 1)
            split_act(act, "mix", in_(hT), in_u, lambda n, k: norm_out("mix", n))
            for c in range(PROJ):
                proj_act(act, 0, c)
            with loop(act, 4) as i:
                da_act(act, i)
            with loop(act, 3) as j:
                sb_act(act, j, False)
            act.wait_ge(S("proj_mm"), PROJ * UNITS)
            act.dma_start(hT, xT_d).then_inc(S("x_in"), 16)
            sb_act(act, 3, True)
            act.wait_ge(S("sb_y_ready"), 4)
            act.dma_start(mraw, memT_d).then_inc(S("mem_in"), 16)
            split_act(act, "y1", in_(yT), in_u,
                      lambda n, k: (S("da_y_ready"), k + 1) if k < 4 else (S("sb_y_ready"), k - 3))
            norm_act(act, "mem", lambda k: mraw[:, k, :], MEM, m_sq, m_rs, lambda k: [(S("mem_in"), 16)])
            act.wait_ge(S("wo_evac"), 20)
            act.sem_inc(S("xk_evac"), 4)
            norm_squares(act, "x", lambda k: hT[:, k, :], T, x_sq, lambda k: [])
            split_act(act, "mem", in_(mT), mem_split_high, lambda n, k: norm_out("mem", n), MEM)
            norm_rstd(act, "x", T, x_rs)
            split_act(act, "x", in_(yT), in_u, lambda n, k: norm_out("x", n))

            def take_k(i, j, h, b):
                act.activation(dyn(KcT, NS * i + j, 1).rearrange("p o t -> p (o t)"), b, ACT.Copy).then_inc(S("xk_evac"), 1)

            def take_v(i, j, h, b):
                act.activation(dyn(VcT, NS * i + j, 1).rearrange("p o t -> p (o t)"), b, ACT.Copy).then_inc(S("xv_evac"), 1)

            def take_q(i, j, h, b):
                act.activation(dyn(qcT, NS * i + j, 1, h * HALF, (h + 1) * HALF).rearrange("p o t -> p (o t)"), b,
                               ACT.Copy, scale=1.0 / 16).then_inc(S("xq_evac"), 1)

            gemm_evac(act, "xk", 8, MEM, take_k)
            act.wait_ge(S("xk_evac"), 12)
            act.sem_inc(S("xv_evac"), 4)
            gemm_evac(act, "xv", 8, MEM, take_v)
            act.wait_ge(S("v_turned"), V_MEM)
            for b in range(4):
                act.activation(Vc[:, b // 2, b % 2 * HALF:(b % 2 + 1) * HALF], bank(4 + b), ACT.Copy).then_inc(S("v_copied"), 1)
            act.sem_inc(S("xq_evac"), 4)
            gemm_evac(act, "xq", 8, T, take_q)
            act.wait_ge(S("xq_evac"), 20)
            with loop(act, 4) as i:
                x_act(act, i)
            split_act(act, "y2", in_(yT), in_u, lambda n, k: (S("x_o_evac"), 4 * (k // 2) + 3 + k % 2))
            norm_act(act, "mlp", lambda k: hT[:, k, :], T, f_sq, f_rs, lambda k: [(S("xo_evac"), 4 + 2 * (k + 1))])
            split_act(act, "mlp", in_(ul), in_u, lambda n, k: norm_out("mlp", n))
            with loop(act, 4) as g:
                mlp_act(act, g)
            norm_act(act, "fin", lambda k: hT[:, k, :], T, ul, f_rs, lambda k: [(S("dn_evac"), 4 + 48 + 2 * (k + 1))])
            norm_act(act, "pre", lambda k: hT[:, k, :], T, ul, f_rs, lambda k: [norm_out("fin", k + 1)])
            for k in range(KC):
                act.dma_start(park_d[:, k, :], hT[:, k, :]).then_inc(S("parked"), 16)
            act.wait_ge(S("ada_ready"), 1)
            act.wait_ge(S("parked"), 16 * KC)
            split_act(act, "u2", in_(uT[:, :, PAD:]), in_h, lambda n, k: norm_out("pre", n), shift=lambda k: ada[:, k:k + 1])
            act.dma_start(sbias.rearrange("p h k -> p (h k)"), bias_d).then_inc(S("bias_in"), 16)
            for q in range(12):
                p2_act(act, q)
                if q == 9:
                    act.wait_ge(S("p2_evac"), 10)
                    act.dma_start(akx[0:64, :], ak[64:128, :]).then_inc(S("akx_in"), 16)
                    act.dma_start(akx[64:128, :], ak[0:64, :]).then_inc(S("akx_in"), 16)
            swa_act(act)
            act.wait_ge(S("sw_o_evac"), 16)
            gla_act(act, BETWEEN)
            wa_act(act)
            for q in range(44, 48):
                if q == 46:
                    wa_split_act(act)
                p2_act(act, q)
            rw_pre_act(act)
            for u in range(4):
                rw_act(act, u)
                y3_act(act, u)

            def take_z(i, j, h, b):
                act.activation(Z[:, bass.ds(NS * i + j, 1), h * HALF:(h + 1) * HALF].rearrange("p o t -> p (o t)"), b,
                               ACT.Copy).then_inc(S("out2_evac"), 1)

            act.wait_ge(*rw("dve", "gated", 3))
            act.dma_start(uT[:, :, PAD:], park_d).then_inc(S("parked"), 16)
            act.sem_inc(S("out2_evac"), 4)
            gemm_evac(act, "out2", 8, T, take_z)
            act.wait_ge(S("out2_evac"), 20)
            norm_act(act, "post", lambda k: Z[:, k, :], T, f_sq, f_rs, lambda k: [])

        @block.tensor
        def _(pe):
            pe.sem_inc(S("weight_free"), CREDIT)
            pe.wait_ge(S("const_in"), 16)
            pe.wait_ge(S("lam_prod"), 2)
            pe.matmul(bank(0)[:, 0:2], cst("ones"), lamt[:, 0:2], start=True, stop=True).then_inc(S("lam_sum"), 1)
            norm_pe(pe, "mix", T, n_sq)
            pe.wait_ge(S("cact_ready"), 1)
            for c in range(PROJ):
                proj_pe(pe, 0, c)
            with loop(pe, 4) as i:
                da_pe(pe, i)
            with loop(pe, 3) as j:
                sb_pe(pe, j, False)
            sb_pe(pe, 3, True)
            gemm_pe(pe, "wo", UNIT_MAIN, 8, pair(in_u, in_y), "y1")
            norm_pe(pe, "mem", MEM, m_sq)
            norm_pe(pe, "x", T, x_sq)
            gemm_pe(pe, "xk", UNIT_MAIN + 8, 8, mem_split, "mem", width=MEM)
            gemm_pe(pe, "xv", UNIT_MAIN + 16, 8, mem_split, "mem", width=MEM)
            pe.wait_ge(S("xv_evac"), 12)
            for t in range(2):
                for b in range(2):
                    for x in range(4):
                        m = pe.transpose(bank(4 + 2 * t + b)[:, x * P:(x + 1) * P], VcT[:, 4 * b + x, t * P:(t + 1) * P], cst("ident"))
            m.then_inc(S("v_turned"), 1)
            gemm_pe(pe, "xq", UNIT_MAIN + 24, 8, pair(in_u, in_y), "x")
            with loop(pe, 4) as i:
                x_pe(pe, i)
            gemm_pe(pe, "xo", UNIT_MAIN + 32, 8, pair(in_u, in_y), "y2")
            norm_pe(pe, "mlp", T, f_sq)
            with loop(pe, 4) as g:
                mlp_pe(pe, g)
            norm_pe(pe, "fin", T, ul)
            norm_pe(pe, "pre", T, ul)
            for q in range(12):
                p2_pe(pe, q)
            swa_pe(pe)
            gla_pe(pe, BETWEEN)
            for q in range(44, 48):
                p2_pe(pe, q)
            rw_pre_pe(pe)
            pe.wait_ge(S("lora_out"), 4)
            pe.wait_ge(S("rkv_mixed"), 6)
            pe.wait_ge(S("p2_evac"), 48)
            for u in range(4):
                rw_pe(pe, u)
            pe.wait_ge(*split_ready("y3"))
            gemm_pe(pe, "out2", G2 + 24, 8, pair(in_h, in_y), None)
            norm_pe(pe, "post", T, f_sq)


def columns(v):
    v = np.asarray(v).reshape(-1)
    return v.reshape(-1, P).T


def panels(w, starts):
    w = np.asarray(w).reshape(KC, P, -1)
    return [w[:, :, s:s + P].transpose(1, 0, 2).reshape(P, KC * P) for s in starts]


def lay_out(inputs):
    g = {k: np.asarray(v) for k, v in inputs.items()}
    vec = {}
    for name, key in [("g_mix", "g_mix"), ("g_cross", "g_cross"), ("g_mem", "g_mem"), ("g_mlp", "g_mlp"),
                      ("g_final", "g_final"), ("norm_pre", "norm_pre_2"), ("norm_post", "norm_post_2"),
                      ("g_subln", "g_subln"), ("c", "c_2"), ("ada_b", "ada_b_2"), ("mu_w", "rwkv_mu_w_2"),
                      ("mu_a", "rwkv_mu_a_2"), ("mu_rkv", "rwkv_mu_rkv_2"), ("w0", "rwkv_w0_2"), ("a0", "rwkv_a0_2"),
                      ("k_k", "rwkv_k_k_2"), ("k_a", "rwkv_k_a_2"), ("r_k", "rwkv_r_k_2"), ("ln_w", "rwkv_ln_w_2"),
                      ("ln_b", "rwkv_ln_b_2"), ("gk_b", "gla_gk_b_2")]:
        vec[name] = columns(g[key])
    n = g["gla_norm_w_2"].reshape(-1)
    vec["gla_norm"] = np.concatenate([n, n])[:, None]
    lam = np.zeros((P, 4), np.float32)
    for x, key in enumerate(["lambda_q1", "lambda_k1", "lambda_q2", "lambda_k2"]):
        lam[:64, x] = g[key].reshape(-1)
    vec["lam"] = lam
    order = [4 * x + 2 * c + par for x in range(2) for par in range(2) for c in range(2)]
    vec["sinks"] = np.broadcast_to(g["attn_sinks_2"].reshape(-1)[order][None, :], (P, 8))
    wa = np.concatenate([g["rwkv_w1_2"][0], g["rwkv_a1_2"][0]], axis=1)
    gk2 = np.concatenate([g["gla_gk2_2"][0], np.zeros((P - 16, P), np.float32)], axis=0)
    lora = np.concatenate([wa.reshape(KC, P, P).transpose(1, 0, 2).reshape(P, -1),
                           g["gla_gk1_2"][0].reshape(KC, P, 16).transpose(1, 0, 2).reshape(P, -1), gk2,
                           np.concatenate([g["rwkv_w2_2"][0], g["rwkv_a2_2"][0]], axis=0)], axis=1)
    vec_a = np.concatenate([vec[name] for name in VEC], axis=1)
    win = g["w_in"][0]
    adaw = g["ada_w_2"][0]
    w = []
    for u in range(UNITS):
        first, n = (0, u) if u < 4 else (1536, u - 4)
        for s in range(3):
            w += panels(win, [first + 512 * s + n * P]) + panels(adaw, [(3 * u + s) * P])
    every = range(0, D, P)
    w += panels(g["w_out"][0], every)
    w += panels(g["w_xkv"][0], range(0, 2 * D, P))
    w += panels(g["w_xq"][0], every)
    w += panels(g["w_xo"][0], every)
    for f in range(4):
        w += panels(g["w_up"][0], range(f * D, (f + 1) * D, P))
        w += panels(g["w_down"][0][f * D:(f + 1) * D], every)
    w2 = g["w_in_2"][0]
    w += panels(w2, [P * b for b in SECOND_ORDER])
    w += panels(g["w_out_2"][0], every)

    def feature_major(a):
        return a.T.reshape(KC, P, -1).transpose(1, 0, 2)

    return {
        "xT": np.ascontiguousarray(feature_major(g["x"][0])),
        "memT": np.ascontiguousarray(feature_major(g["mem"][0])),
        "pos": np.ascontiguousarray(np.broadcast_to(g["positions"].reshape(1, T), (P, T))),
        "vec": np.ascontiguousarray(vec_a),
        "const": constants(),
        "bias": window_bias(),
        "lora": np.ascontiguousarray(lora),
        "w": np.ascontiguousarray(np.stack(w)),
    }


SECOND_ORDER = [0, 1, 2, 3, 4, 5, 18, 19, 20, 21, 10, 11, 12, 13, 14, 15, 6, 7, 8, 9, 16, 17, 22, 23]


def kernel(**inputs):
    import concourse.bacc as bacc
    from concourse.bass_utils import run_bass_kernel_spmd

    arrays = lay_out(inputs)
    nc = bacc.Bacc("TRN2", target_bir_lowering=False, num_devices=1)
    args = [nc.dram_tensor("in_" + n, a.shape, mybir.dt.from_np(a.dtype), kind="ExternalInput").ap() for n, a in arrays.items()]
    args.append(nc.dram_tensor("out_0", (P, KC, T), mybir.dt.float32, kind="ExternalOutput").ap())
    program(nc, *args)
    r = run_bass_kernel_spmd(nc, [{"in_" + n: a for n, a in arrays.items()}], core_ids=[0])
    o = r.results[0]["out_0"]
    return o.transpose(1, 0, 2).reshape(D, T).T.reshape(1, T, D)
```
